# Optimizing a Trainium2 kernel written in Bass

```python
import math
import jax, jax.numpy as jnp
from jax import lax
import numpy as np

D_MODEL = 1024
BATCH = 1
SEQ = 1024
DEPTH = 2

N_META = 16
BLOCK = 128
PAD = BLOCK - N_META
WINDOW = 128
ROPE_THETA = 10000.0
HEAD_DIM = 64

A_HEADS = 4
A_KV_HEADS = 2
A_WIDTH = A_HEADS * HEAD_DIM
B_HEADS = 4
B_QK_DIM = HEAD_DIM
B_V_DIM = 2 * HEAD_DIM
B_WIDTH = B_HEADS * B_V_DIM
C_HEADS = 4
C_DK = HEAD_DIM
C_DV = HEAD_DIM
C_WIDTH = C_HEADS * C_DV
C_CHUNK = 16

D_MIX = A_WIDTH + B_WIDTH + C_WIDTH
IN_SPLITS = (A_WIDTH, A_KV_HEADS * HEAD_DIM, A_KV_HEADS * HEAD_DIM, A_WIDTH,
             2 * B_HEADS * B_QK_DIM, 2 * B_HEADS * B_QK_DIM, B_WIDTH, B_WIDTH,
             C_HEADS * C_DK, C_WIDTH, C_HEADS * C_DK, C_HEADS * C_DK, C_WIDTH)
N_IN = sum(IN_SPLITS)

ALPHA = (2 * DEPTH) ** 0.25
BETA = (8 * DEPTH) ** -0.25
LN_EPS = 1e-5
RMS_EPS = 1e-6
NEG = -1e30
F_MIN = 1e-30

kernel_name = "hymba_style_bidir_hybrid_block"

def layer_norm(x, g, b):
    xf = x.astype(jnp.float32)
    mu = jnp.mean(xf, axis=-1, keepdims=True)
    var = jnp.mean(jnp.square(xf - mu), axis=-1, keepdims=True)
    y = (xf - mu) * lax.rsqrt(var + LN_EPS) * g.astype(jnp.float32) + b.astype(jnp.float32)
    return y.astype(x.dtype)

def rms_norm(x, w):
    xf = x.astype(jnp.float32)
    return xf * lax.rsqrt(jnp.mean(jnp.square(xf), axis=-1, keepdims=True) + RMS_EPS) * w.astype(jnp.float32)

def rope_tables(lp):
    pos = (jnp.arange(lp) - PAD).astype(jnp.float32)
    inv = ROPE_THETA ** (-jnp.arange(0, HEAD_DIM, 2, dtype=jnp.float32) / HEAD_DIM)
    ang = pos[:, None] * inv[None, :]
    return jnp.cos(ang)[:, None, :], jnp.sin(ang)[:, None, :]

def rotary(x, cos, sin):
    xf = x.astype(jnp.float32)
    x1, x2 = jnp.split(xf, 2, axis=-1)
    return jnp.concatenate([x1 * cos - x2 * sin, x2 * cos + x1 * sin], axis=-1).astype(x.dtype)

def window_gqa(q, k, v, sink):
    bsz, lp = q.shape[:2]
    nb = lp // BLOCK
    grp = A_HEADS // A_KV_HEADS
    qb = q.reshape(bsz, nb, BLOCK, A_KV_HEADS, grp, HEAD_DIM)

    def band(t):
        tb = t.reshape(bsz, nb, BLOCK, A_KV_HEADS, HEAD_DIM)
        tp = jnp.pad(tb, ((0, 0), (1, 1), (0, 0), (0, 0), (0, 0)))
        return jnp.concatenate([tp[:, :-2], tp[:, 1:-1], tp[:, 2:]], axis=2)

    k_band, v_band = band(k), band(v)
    k_meta, v_meta = k[:, PAD:PAD + N_META], v[:, PAD:PAD + N_META]
    scale = HEAD_DIM ** -0.5
    s_band = jnp.einsum('bnqhgd,bnkhd->bnhgqk', qb, k_band).astype(jnp.float32) * scale
    s_meta = jnp.einsum('bnqhgd,bmhd->bnhgqm', qb, k_meta).astype(jnp.float32) * scale
    blk = jnp.arange(nb)[:, None]
    q_pos = blk * BLOCK + jnp.arange(BLOCK)[None, :]
    k_pos = (blk - 1) * BLOCK + jnp.arange(3 * BLOCK)[None, :]
    kp = k_pos[:, None, :]
    ok = (jnp.abs(q_pos[:, :, None] - kp) <= WINDOW) & (kp >= PAD + N_META) & (kp < lp)
    s_band = jnp.where(ok[None, :, None, None], s_band, NEG)
    sink_logit = jnp.broadcast_to(sink.astype(jnp.float32).reshape(1, 1, A_KV_HEADS, grp, 1, 1),
                                  s_meta.shape[:-1] + (1,))
    p = jax.nn.softmax(jnp.concatenate([sink_logit, s_meta, s_band], axis=-1), axis=-1).astype(v.dtype)
    out = (jnp.einsum('bnhgqm,bmhd->bnqhgd', p[..., 1:1 + N_META], v_meta)
           + jnp.einsum('bnhgqk,bnkhd->bnqhgd', p[..., 1 + N_META:], v_band))
    return out.reshape(bsz, lp, A_HEADS, HEAD_DIM)

def diff_attention(q, k, v, lam, key_ok):
    bsz, lp = q.shape[:2]
    nb = lp // BLOCK
    qb = q.reshape(bsz, nb, BLOCK, B_HEADS, 2, B_QK_DIM).swapaxes(0, 1)
    scale = B_QK_DIM ** -0.5

    def attend(q_blk):
        s = jnp.einsum('bqhcd,bkhcd->bhcqk', q_blk, k).astype(jnp.float32) * scale
        s = jnp.where(key_ok, s, NEG)
        p = jax.nn.softmax(s, axis=-1)
        a = p[:, :, 0] - lam * p[:, :, 1]
        return jnp.einsum('bhqk,bkhv->bqhv', a.astype(v.dtype), v)

    out = lax.map(attend, qb)
    return out.swapaxes(0, 1).reshape(bsz, lp, B_HEADS, B_V_DIM)

def hgrn2_chunked(q, k, v, logf):
    bsz, lp, nh, dk = q.shape
    dv = v.shape[-1]
    n = lp // C_CHUNK
    q, k, v, logf = (t.reshape(bsz, n, C_CHUNK, nh, t.shape[-1]) for t in (q, k, v, logf))
    b = jnp.cumsum(logf, axis=2)
    incl = jnp.tril(jnp.ones((C_CHUNK, C_CHUNK), dtype=bool))
    diff = b[:, :, :, None] - b[:, :, None, :]
    decay = jnp.exp(jnp.where(incl[None, None, :, :, None, None], diff, NEG))
    scores = jnp.einsum('bnthk,bnshk,bntshk->bnhts', q, k, decay)
    intra = jnp.einsum('bnhts,bnshv->bnthv', scores, v)
    b_last = b[:, :, -1]
    u = jnp.einsum('bnshk,bnshv->bnhkv', k * jnp.exp(b_last[:, :, None] - b), v)
    d_chunk = jnp.exp(b_last)

    def step(s, inp):
        dc, uc = inp
        return dc[..., None] * s + uc, s

    s0 = jnp.zeros((bsz, nh, dk, dv), jnp.float32)
    _, s_prev = lax.scan(step, s0, (d_chunk.swapaxes(0, 1), u.swapaxes(0, 1)))
    s_prev = s_prev.swapaxes(0, 1)
    inter = jnp.einsum('bnthk,bnhkv->bnthv', q * jnp.exp(b), s_prev)
    return (intra + inter).reshape(bsz, lp, nh, dv)

def mixer_layer(x, w_in, w_out, sink, lam_params, subln_w, lb, c_norm_w, lam_init, cos, sin, valid):
    bsz, seq_len, _ = x.shape
    lp = seq_len + PAD
    dt = x.dtype
    h = jnp.pad(x @ w_in, ((0, 0), (PAD, 0), (0, 0)))
    idx = [int(i) for i in np.cumsum(IN_SPLITS)[:-1]]
    (qa, ka, va, ga, qb, kb, vb, gb, qc, ic, zf, zb, gc) = jnp.split(h, idx, axis=-1)

    qa = rotary(qa.reshape(bsz, lp, A_HEADS, HEAD_DIM), cos, sin)
    ka = rotary(ka.reshape(bsz, lp, A_KV_HEADS, HEAD_DIM), cos, sin)
    va = va.reshape(bsz, lp, A_KV_HEADS, HEAD_DIM)
    ya = window_gqa(qa, ka, va, sink).reshape(bsz, lp, A_WIDTH) * jax.nn.silu(ga)

    qb = rotary(qb.reshape(bsz, lp, 2 * B_HEADS, B_QK_DIM), cos, sin).reshape(bsz, lp, B_HEADS, 2, B_QK_DIM)
    kb = rotary(kb.reshape(bsz, lp, 2 * B_HEADS, B_QK_DIM), cos, sin).reshape(bsz, lp, B_HEADS, 2, B_QK_DIM)
    vb = vb.reshape(bsz, lp, B_HEADS, B_V_DIM)
    lp32 = lam_params.astype(jnp.float32)
    lam = jnp.exp(jnp.sum(lp32[0] * lp32[1])) - jnp.exp(jnp.sum(lp32[2] * lp32[3])) + lam_init
    ob = diff_attention(qb, kb, vb, lam, valid)
    ob = rms_norm(ob, subln_w.reshape(B_HEADS, B_V_DIM)) * (1.0 - lam_init)
    yb = ob.reshape(bsz, lp, B_WIDTH).astype(dt) * jax.nn.silu(gb)

    qc = jax.nn.silu(qc).reshape(bsz, lp, C_HEADS, C_DK).astype(jnp.float32)
    ic = ic.reshape(bsz, lp, C_HEADS, C_DV).astype(jnp.float32)
    lb_h = lb.reshape(C_HEADS, C_DK)
    vmask = valid[None, :, None, None]

    def gates(z):
        z = z.reshape(bsz, lp, C_HEADS, C_DK).astype(jnp.float32)
        f = lb_h + (1.0 - lb_h) * jax.nn.sigmoid(z)
        logf = jnp.log(jnp.maximum(f, F_MIN))
        kk = (1.0 - lb_h) * jax.nn.sigmoid(-z)
        return jnp.where(vmask, kk, 0.0), jnp.where(vmask, logf, 0.0)

    k_f, logf_f = gates(zf)
    k_b, logf_b = gates(zb)
    y_f = hgrn2_chunked(qc, k_f, ic, logf_f)
    flip = lambda t: jnp.flip(t, axis=1)
    y_b = flip(hgrn2_chunked(flip(qc), flip(k_b), flip(ic), flip(logf_b)))
    oc = rms_norm(y_f + y_b, c_norm_w.reshape(C_HEADS, C_DV))
    yc = oc.reshape(bsz, lp, C_WIDTH).astype(dt) * jax.nn.silu(gc)

    y = jnp.concatenate([ya, yb, yc], axis=-1)[:, PAD:]
    return y @ w_out

def setup_inputs(seed: int = 0) -> dict:
    key = jax.random.key(seed)
    ks = jax.random.split(key, 14)
    nrm = jax.random.normal
    return {
        "x": nrm(ks[0], (BATCH, SEQ, D_MODEL), jnp.float32),
        "meta": nrm(ks[1], (N_META, D_MODEL), jnp.float32),
        "emb_ln_g": 1.0 + 0.02 * nrm(ks[2], (D_MODEL,), jnp.float32),
        "emb_ln_b": 0.02 * nrm(ks[3], (D_MODEL,), jnp.float32),
        "w_in": nrm(ks[4], (DEPTH, D_MODEL, N_IN), jnp.float32) * D_MODEL ** -0.5,
        "w_out": nrm(ks[5], (DEPTH, D_MIX, D_MODEL), jnp.float32) * (D_MIX ** -0.5) * BETA,
        "a_sink": 0.5 * nrm(ks[6], (DEPTH, A_HEADS), jnp.float32),
        "b_lam": 0.1 * nrm(ks[7], (DEPTH, 4, B_QK_DIM), jnp.float32),
        "b_subln_w": 1.0 + 0.02 * nrm(ks[8], (DEPTH, B_WIDTH), jnp.float32),
        "c_lb_logits": 0.5 * nrm(ks[9], (DEPTH, C_HEADS * C_DK), jnp.float32),
        "c_norm_w": 1.0 + 0.02 * nrm(ks[10], (DEPTH, C_WIDTH), jnp.float32),
        "ln_g": 1.0 + 0.02 * nrm(ks[11], (DEPTH, D_MODEL), jnp.float32),
        "ln_b": 0.02 * nrm(ks[12], (DEPTH, D_MODEL), jnp.float32),
    }

def reference(x, meta, emb_ln_g, emb_ln_b, w_in, w_out, a_sink, b_lam, b_subln_w, c_lb_logits, c_norm_w, ln_g, ln_b):
    bsz = x.shape[0]
    h = jnp.concatenate([jnp.broadcast_to(meta[None].astype(x.dtype), (bsz, N_META, D_MODEL)), x], axis=1)
    h = layer_norm(h, emb_ln_g, emb_ln_b)
    lp = h.shape[1] + PAD
    cos, sin = rope_tables(lp)
    valid = jnp.arange(lp) >= PAD
    p_lb = jax.nn.softmax(c_lb_logits.astype(jnp.float32), axis=0)
    lb_all = jnp.cumsum(p_lb, axis=0) - p_lb[0:1]
    for l in range(DEPTH):
        lam_init = 0.8 - 0.6 * math.exp(-0.3 * l)
        y = mixer_layer(h, w_in[l], w_out[l], a_sink[l], b_lam[l], b_subln_w[l], lb_all[l], c_norm_w[l],
                        lam_init, cos, sin, valid)
        h = layer_norm(ALPHA * h + y, ln_g[l], ln_b[l])
    return h[:, N_META:]


_drawn_inputs = setup_inputs


def setup_inputs(seed=0):
    import zlib

    import numpy as np

    out = dict(_drawn_inputs(seed))
    spreads = {}
    factors = {'meta': 3.306,
     'a_sink': 64.0,
     'b_subln_w': 23.769,
     'c_lb_logits': 6.551,
     'c_norm_w': 25.026}
    for name, (base, spread) in spreads.items():
        noise = np.random.default_rng([zlib.crc32(name.encode()), seed]).standard_normal(out[name].shape)
        drawn = base * np.exp(spread * noise) if base else spread * noise
        out[name] = __import__('jax').numpy.asarray(drawn.astype(out[name].dtype))
    for name, factor in factors.items():
        out[name] = (out[name] * factor).astype(out[name].dtype)
    return out
```

```python
from contextlib import ExitStack

import numpy as np

import concourse.bass as bass
from concourse import mybir

ALU = mybir.AluOpType
ACT = mybir.ActivationFunctionType
F32 = mybir.dt.float32
F32R = mybir.dt.float32r
I32 = mybir.dt.int32
AX = mybir.AxisListType

P = 128
DM = 1024
DEPTH = 2
META = 16
HD = 64
REAL = 8
TILES = REAL + 1
MT = REAL
TOK = REAL * P + META
KT = DM // P
CW = 256
SCALE = HD ** -0.5
ALPHA = (2 * DEPTH) ** 0.25
LN_EPS, RMS_EPS, F_MIN, E_MAX, NEG = 1e-5, 1e-6, 1e-30, 1e37, -1e30
LAM_INIT = [0.8 - 0.6 * float(np.exp(-0.3 * l)) for l in range(DEPTH)]

QA, KA, VA, GA, QB, KB, VB, GB, QC, IC, ZF, ZB, GC = (
    0, 256, 384, 512, 768, 1280, 1792, 2304, 2816, 3072, 3328, 3584, 3840)

LEVELS = 8
HALF = [0] + [2 ** (i - 1) for i in range(1, LEVELS)]
SPAN = [(0, 4 * P), (4 * P, TOK)]


def span(half, h):
    a, b = SPAN[half]
    return (a, b) if h <= META // 2 else (a, min(b, REAL * P))


SEG_N = [TOK if h <= META else REAL * P for h in (1, 2, 4, 8, 16, 32, 64, 128)]
SEG_LEN = [n // h for n, h in zip(SEG_N, (1, 2, 4, 8, 16, 32, 64, 128))]
SEG_AT = [sum(SEG_LEN[:i]) for i in range(8)]
SEG_ALL = sum(SEG_LEN)

GROUPS = ["C0", "C1", "A", "B0", "B1", "B2", "B3"]
Y_COL = {"A": 0, "B0": 256, "B1": 384, "B2": 512, "B3": 640, "C0": 768, "C1": 896}
Y_WIDTH = {g: 256 if g == "A" else 128 for g in GROUPS}
Y_SLOTS = 4
H_LAG = 4


def rows(t):
    return META if t == MT else P


def q_tiles(l):
    return TILES if l < DEPTH - 1 else REAL


def cols(t):
    return slice(t * P, t * P + rows(t))


def numbered(keys):
    return {k: i + 1 for i, k in enumerate(keys)}


def chunks_of(group):
    if group[0] == "C":
        o = P * int(group[1])
        return [("qf", "T", [(QC + o, P), (ZF + o, P)]), ("b", "T", [(ZB + o, P)]),
                ("vg", "N", [(IC + o, P), (GC + o, P)])]
    if group == "A":
        return [("q", "N", [(QA, CW)]), ("kv", "N", [(KA, CW)]), ("g", "N", [(GA, CW)])]
    if group[0] == "B":
        o = P * int(group[1])
        return [("qk", "N", [(QB + o, P), (KB + o, P)]), ("vg", "N", [(VB + o, P), (GB + o, P)])]
    return [(c, "N", [(c * CW, CW)]) for c in range(DM // CW)]


CHUNKS = [(l, g, *c) for l in range(DEPTH) for g in [*GROUPS, "O"] for c in chunks_of(g)]
CHUNK = {(l, g, name): i for i, (l, g, name, _, _) in enumerate(CHUNKS)}
CHUNK_DMAS = np.cumsum([len(c[4]) for c in CHUNKS]).tolist()
T_PIECES = [(0, 348), (348, 346), (694, 346)]
S_PIECES = [(0, 348), (348, 348), (696, 344)]
S_W = 348
PHASES = ["I"] + [(l, g) for l in range(DEPTH) for g in [*GROUPS, "O"]]
PHASE = {k: i for i, k in enumerate(PHASES)}


def window(t):
    if t == MT:
        return 0, 1
    return max(t - 1, 0), min(t + 1, REAL - 1) - max(t - 1, 0) + 1


def units(l, g, name):
    if g[0] == "C" and name != "vg":
        return [(f, j) for f in range(2 if name == "qf" else 1) for j in range(3)]
    if g == "O" or (g == "A" and name in ("q", "g")):
        return list(range(q_tiles(l)))
    return list(range(TILES))


def level_fills(half, lev):
    a = 4 * half
    out = [(a, 2), (a + 2, 2)]
    if half and HALF[lev] <= META // 2:
        out.append((MT, 1))
    return out


def bank_plan():
    used, plan = [0] * 8, {}

    def add(key, bank):
        plan[key] = (bank, used[bank])
        used[bank] += 1

    def transposed(what, l, n):
        for t in range(n):
            for j in range(2):
                add((what, l, t, j), (2 if what == "h" else 0) + j)

    transposed("h", 0, TILES)
    for l in range(DEPTH):
        u = 0
        for g in GROUPS:
            for name, kind, _ in chunks_of(g):
                for x in units(l, g, name):
                    add(("unit", l, g, name, x), u % 2)
                    u += 1
            if g[0] == "C":
                n = 0
                for lev in range(LEVELS):
                    for half in range(2):
                        for first, _ in level_fills(half, lev):
                            add(("level", l, g, lev, first), 2 + n % 6)
                            n += 1
                for i, t in enumerate([MT, *range(REAL)]):
                    add(("knat", l, g, t), 2 + i % 2)
                    add(("u", l, g, t), 4 + i % 2)
                for t in range(q_tiles(l)):
                    add(("o", l, g, t), 6 + t % 2)
            if g == "A":
                for t in units(l, g, "q"):
                    add(("qT", l, g, t), 2 + 2 * (t % 2))
                for t in units(l, g, "kv"):
                    add(("kT", l, g, t), 3 + 2 * (t % 2))
                for t in range(q_tiles(l)):
                    for h in range(4):
                        add(("s", l, g, t, h), 2 + h)
                        add(("pT", l, g, t, h), 6 + h % 2)
                    add(("o", l, g, t), t % 2)
            if g[0] == "B":
                for t in range(TILES):
                    add(("qkT", l, g, t), 2 + 3 * (t % 2))
                for t in range(q_tiles(l)):
                    for c in range(2):
                        add(("s", l, g, t, c), 2 + 3 * c)
                    for j in range(3):
                        add(("aT", l, g, t, j), 1)
                    add(("o", l, g, t), 0)
        transposed("y", l, q_tiles(l))
        for c in range(DM // CW):
            for t in units(l, "O", c):
                add(("unit", l, "O", c, t), t % 2)
        if l < DEPTH - 1:
            transposed("h", l + 1, TILES)
    return plan


BANK = bank_plan()

HT = [("h", 0, TILES)] + [x for l in range(DEPTH) for x in
                          [("y", l, q_tiles(l))] + ([("h", l + 1, TILES)] if l < DEPTH - 1 else [])]
T_SPLIT = numbered([(w, l, t, j) for w, l, n in HT for t in range(n) for j in range(2)])
NORM = numbered([("I", t) for t in range(TILES)] + [(l, t) for l in range(DEPTH) for t in range(q_tiles(l))])
HEADS_IN = [(l, g, x, t) for l in range(DEPTH) for g in GROUPS if g[0] != "C"
            for x in (("q", "kv") if g == "A" else ("qk",)) for t in units(l, g, x)]
ROPE = numbered(HEADS_IN)
QK_HI = numbered(HEADS_IN)
Y_OUT = numbered([(l, g, t) for l in range(DEPTH) for g in GROUPS for t in range(q_tiles(l))])
LEVEL = numbered([(l, g, lev, half) for l in range(DEPTH) for g in GROUPS if g[0] == "C"
                  for lev in range(LEVELS) for half in range(2)])
SEG = numbered([(l, g, lev, half) for l in range(DEPTH) for g in GROUPS if g[0] == "C"
                for lev in range(LEVELS + 1) for half in range(2)])
B_HEAD = numbered([(l, g) for l in range(DEPTH) for g in GROUPS if g[0] == "B"])
C_PAIR = numbered([(l, g) for l in range(DEPTH) for g in GROUPS if g[0] == "C"])
RSTD = numbered([("I", t) for t in range(TILES)] + [x for l in range(DEPTH) for x in
                [(l, g, t) for g in GROUPS if g != "A" for t in range(q_tiles(l))]
                + [(l, t) for t in range(q_tiles(l))]])
A_HEAD = numbered([(l, t, h) for l in range(DEPTH) for t in range(q_tiles(l)) for h in range(4)])
B_COMP = numbered([(l, g, t, c) for l in range(DEPTH) for g in GROUPS if g[0] == "B"
                   for t in range(q_tiles(l)) for c in range(2)])
B_STEP = numbered([(l, g, t) for l in range(DEPTH) for g in GROUPS if g[0] == "B" for t in range(q_tiles(l))])
A_PV = numbered([(l, t, h) for l in range(DEPTH) for t in range(q_tiles(l)) for h in range(3)])
GATE = numbered([(l, g, t) for l in range(DEPTH) for g in GROUPS if g[0] != "C"
                 for t in units(l, g, "g" if g == "A" else "vg")])


def shape_constants():
    pos = np.zeros((P, TILES), np.float32)
    for t in range(REAL):
        pos[:, t] = META + t * P + np.arange(P)
    pos[:META, MT] = np.arange(META)
    inv = np.float32(10000.0) ** (-np.arange(0, HD, 2, dtype=np.float32) / np.float32(HD))
    ang = pos[:, :, None] * inv[None, None, :].astype(np.float32)
    cos, sin = np.cos(ang).astype(np.float32), np.sin(ang).astype(np.float32)
    s, t = np.arange(P)[:, None], np.arange(P)[None, :]
    pair = np.zeros((P, LEVELS, P), np.float32)
    pair[:, 0] = s == t
    for i in range(1, LEVELS):
        h = HALF[i]
        pair[:, i] = (s // (2 * h) == t // (2 * h)) & (s // h != t // h)
    i, j = np.arange(P)[:, None], np.arange(P)[None, :]
    prev = np.where(j >= i, 0, NEG).astype(np.float32)
    nxt = np.where(j <= i, 0, NEG).astype(np.float32)
    zero = np.zeros((P, P), np.float32)
    zm = np.zeros((P, META), np.float32)
    meta_q = np.where(j <= P - META + i, 0, NEG).astype(np.float32)
    band = np.concatenate([prev, zero, nxt, zm, prev, zero, zm, meta_q, zm], axis=1)
    return {"eye": np.eye(P, dtype=np.float32), "rope_cos": np.concatenate([cos, cos], axis=2),
            "rope_sin": np.concatenate([-sin, sin], axis=2), "pair_mask": pair, "band_mask": band}


BAND_W = 400 + 272 + 144
CONSTS = shape_constants()


def band_columns(t):
    if t == MT:
        return slice(672, 816)
    if t == REAL - 1:
        return slice(400, 672)
    return slice(P, 400) if t == 0 else slice(0, 400)


def build(nc, x, meta, emb_ln_g, emb_ln_b, w_in, w_out, a_sink, b_lam, b_subln_w, c_lb_logits,
          c_norm_w, ln_g, ln_b, eye, rope_cos, rope_sin, pair_mask, band_mask, out):
    top = ExitStack()

    def sb(stack, name, shape, dt=F32):
        return stack.enter_context(nc.sbuf_tensor(name, shape, dt))

    def sem(name):
        return top.enter_context(nc.semaphore(name))

    h_dram = nc.dram_tensor("h_dram", (TILES, P, DM), F32, kind="Internal").ap()
    y_dram = nc.dram_tensor("y_dram", (TILES, P, DM), F32, kind="Internal").ap()

    hT_hi = sb(top, "hT_hi", [P, KT, TILES * P], F32R)
    hT_lo = sb(top, "hT_lo", [P, KT, TILES * P], F32R)
    w_raw = sb(top, "w_raw", [P, KT, CW])
    w_hi = sb(top, "w_hi", [P, 2, KT, CW], F32R)
    w_lo = sb(top, "w_lo", [P, 2, KT, CW], F32R)
    ident = sb(top, "ident", [P, P])
    cos_sb = sb(top, "cos_sb", [P, TILES, HD])
    sin_sb = sb(top, "sin_sb", [P, TILES, HD])
    pair_sb = sb(top, "pair_sb", [P, LEVELS, P])
    band_sb = sb(top, "band_sb", [P, BAND_W])
    norm_w = sb(top, "norm_w", [P, 768])
    y_stage = sb(top, "y_stage", [P, Y_SLOTS, 256])
    sink_sb = sb(top, "sink_sb", [P, DEPTH, 4])
    lam_sb = sb(top, "lam_sb", [P, DEPTH, 4, HD])
    lam_tmp = sb(top, "lam_tmp", [P, HD])
    lam_dot = sb(top, "lam_dot", [P, DEPTH, 2])
    lam_exp = sb(top, "lam_exp", [P, DEPTH, 2])
    neg_lam = sb(top, "neg_lam", [P, DEPTH])
    lbl = sb(top, "lbl", [P, DEPTH, 2])
    lb = sb(top, "lb", [P, DEPTH, 2])
    one_lb = sb(top, "one_lb", [P, DEPTH, 2])
    lb_max = sb(top, "lb_max", [P, 2])
    lb_sum = sb(top, "lb_sum", [P, 2])
    stats = sb(top, "stats", [P, TILES, 2, 6])
    mean_var = sb(top, "mean_var", [P, TILES, 2])
    rstd = sb(top, "rstd", [P, TILES, 2])
    sumsq = sb(top, "sumsq", [P, TILES, 2])
    fscale = sb(top, "fscale", [P, 2, 1])
    row_max = sb(top, "row_max", [P, 2, 4])
    neg_max = sb(top, "neg_max", [P, 2, 4])
    row_sum = sb(top, "row_sum", [P, 2, 4])
    sink_exp = sb(top, "sink_exp", [P, 2, 4])
    inv_sum = sb(top, "inv_sum", [P, 2, 4])
    coef = sb(top, "coef", [P, 2, 2])
    eps_ln = sb(top, "eps_ln", [P, 1])
    eps_rms = sb(top, "eps_rms", [P, 1])

    so = ExitStack()
    hbuf = sb(so, "hbuf", [P, TILES, DM])
    y_load = sb(so, "y_load", [P, 2, DM])
    ln_w = sb(so, "ln_w", [P, 2, DM])
    so.close()
    sc = ExitStack()
    KF_, QB_, QF_, KB_ = range(4)
    qk = sb(sc, "qk", [P, 4, TOK])
    q_c = sb(sc, "q_c", [P, TOK])
    seg = sb(sc, "seg", [P, 2, SEG_ALL])
    k_pair = sb(sc, "k_pair", [P, 2, TOK])
    pc = sb(sc, "pc", [P, REAL, 2, P])
    pc_meta = sb(sc, "pc_meta", [META, 2, META])
    v_c = sb(sc, "v_c", [P, TILES, P])
    g_c = sb(sc, "g_c", [P, TILES, P])
    state = sb(sc, "state", [P, 2, TILES, P])
    k_nat = sb(sc, "k_nat", [P, 2, 2, P])
    sc.close()
    sa = ExitStack()
    n_a = sb(sa, "n_a", [P, 2, 256])
    twice_a = sb(sa, "twice_a", [P, 2, 4, 2, HD])
    v_a = sb(sa, "v_a", [P, TILES, P])
    g_a = sb(sa, "g_a", [P, TILES, 256])
    ge_a = sb(sa, "ge_a", [P, 256])
    qkT_a = sb(sa, "qkT_a", [P, 6, TOK], F32R)
    klT_a = sb(sa, "klT_a", [P, 2, TOK], F32R)
    s_a = sb(sa, "s_a", [P, 4, 400])
    pT_a = sb(sa, "pT_a", [P, 2, 4, P])
    ra = sb(sa, "ra", [P, 2, 256])
    sa.close()
    sB = ExitStack()
    n_b = sb(sB, "n_b", [P, 2, 256])
    twice_b = sb(sB, "twice_b", [P, 2, 4, 2, HD])
    v_b = sb(sB, "v_b", [P, TILES, P])
    g_b = sb(sB, "g_b", [P, TILES, P])
    qkT_b = sb(sB, "qkT_b", [P, 4, TOK], F32R)
    klT_b = sb(sB, "klT_b", [P, 2, TOK], F32R)
    p_b = sb(sB, "p_b", [P, 2, 2, TILES * P])
    aT_b = sb(sB, "aT_b", [P, TILES, P])
    rb = sb(sB, "rb", [P, 2, 256])
    ge_b = sb(sB, "ge_b", [P, P])
    b_junk = sb(sB, "b_junk", [P, P])
    sB.close()

    psum = top.enter_context(nc.psum_tensor("psum", [P, 8, 512], F32))

    filled = [sem(f"bank{b}_filled") for b in range(8)]
    released = [sem(f"bank{b}_released") for b in range(8)]
    consts_in = sem("consts_in")
    norm_w_in = sem("norm_w_in")
    w_loaded = sem("w_loaded")
    w_hi_done = sem("w_hi_done")
    w_split = sem("w_split")
    h_in = sem("h_in")
    ln_in = sem("ln_in")
    y_in = [sem(f"y_in{i}") for i in range(2)]
    y_saved = [sem(f"y_saved{i}") for i in range(Y_SLOTS)]
    h_saved = sem("h_saved")
    out_saved = sem("out_saved")
    var_ready = sem("var_ready")
    rstd_ready = sem("rstd_ready")
    h_ready = sem("h_ready")
    hi_split = sem("hi_split")
    gate_ready = sem("gate_ready")
    seg_ready = sem("seg_ready")
    level_selected = sem("level_selected")
    scores_c_ready = sem("scores_c_ready")
    state_ready = sem("state_ready")
    roped = sem("roped")
    qk_hi = sem("qk_hi")
    a_masked = sem("a_masked")
    a_exp = sem("a_exp")
    a_pv = sem("a_pv")
    b_max = sem("b_max")
    b_comb = sem("b_comb")
    b_pad = sem("b_pad")
    setup_v = sem("setup_v")
    setup_s = sem("setup_s")
    vec = sem("vec")
    sca = sem("sca")

    block = top.enter_context(nc.Block())

    def view(t, p0, np_, off, dims):
        full = t[:]
        width = full.ap[0][0]
        return bass.AP(tensor=full.tensor, offset=p0 * width + off, ap=[[width, np_], *dims])

    def bank(key):
        return BANK[key][0]

    def wait_free(eng, key):
        b, n = BANK[key]
        if n:
            eng.wait_ge(released[b], n)

    def wait_filled(eng, key):
        b, n = BANK[key]
        eng.wait_ge(filled[b], n + 1)

    def wait_read(eng, key):
        b, n = BANK[key]
        eng.wait_ge(released[b], n + 1)

    def phase_start(eng, key):
        before = PHASES[PHASE[key] - 1]
        if before == "I":
            wait_read(eng, ("h", 0, TILES - 1, 1))
        elif before[1] == "O":
            wait_read(eng, ("h", before[0] + 1, TILES - 1, 1))
        else:
            wait_read(eng, ("o", *before, q_tiles(before[0]) - 1))

    def level_ap(lev, side, p0, np_, a, n):
        h = HALF[lev]
        left, right = (KF_, KB_) if side == "k" else (QB_, QF_)
        return view(qk, p0, np_, left * TOK + a, [[2 * h, n // (2 * h)], [(right - left) * TOK + h, 2], [1, h]])

    def k_sum():
        return state[:, 0].rearrange("p t c -> p (t c)")[:, 0:TOK]

    @block.sync
    def _(sp):
        for dst, src in ((ident[:], eye), (cos_sb[:], rope_cos), (sin_sb[:], rope_sin),
                         (pair_sb[:], pair_mask), (band_sb[:], band_mask)):
            sp.dma_start(dst, src).then_inc(consts_in, 16)
        sp.dma_start(sink_sb[:], a_sink.partition_broadcast(P)).then_inc(consts_in, 16)
        sp.dma_start(lam_sb[:], b_lam.partition_broadcast(P)).then_inc(consts_in, 16)
        for l in range(DEPTH):
            for p in range(2):
                sp.dma_start(lbl[:, l, p:p + 1],
                             c_lb_logits[l, p * P:(p + 1) * P].rearrange("(p o) -> p o", o=1)).then_inc(consts_in, 16)

        def load_ln(g_ap, b_ap):
            sp.dma_start(ln_w[:, 0], g_ap.partition_broadcast(P)).then_inc(ln_in, 16)
            sp.dma_start(ln_w[:, 1], b_ap.partition_broadcast(P)).then_inc(ln_in, 16)

        for t in range(REAL):
            sp.dma_start(hbuf[:, t], x[0, t * P:(t + 1) * P, :]).then_inc(h_in, 16)
        sp.dma_start(hbuf[0:META, MT], meta).then_inc(h_in, 16)
        load_ln(emb_ln_g, emb_ln_b)

        def load_chunk(i):
            l, g, name, kind, parts = CHUNKS[i]
            if i:
                sp.wait_ge(w_split, i)
            w = (w_out if g == "O" else w_in)[l].rearrange("(k p) n -> p k n", p=P)
            at = 0
            for c0, n in parts:
                sp.dma_start(w_raw[:, :, at:at + n], w[:, :, c0:c0 + n]).then_inc(w_loaded, 16)
                at += n

        def save_h(l, n):
            for t in range(n):
                sp.wait_ge(h_ready, NORM["I" if l < 0 else l, t])
                if l == DEPTH - 1:
                    sp.dma_start(out[0, t * P:(t + 1) * P, :], hbuf[:, t]).then_inc(out_saved, 16)
                else:
                    sp.dma_start(h_dram[t, 0:rows(t)], hbuf[0:rows(t), t]).then_inc(h_saved, 16)

        load_chunk(0)
        load_chunk(1)
        save_h(-1, TILES)
        n_chunk = 2
        for l in range(DEPTH):
            if l:
                phase_start(sp, (l - 1, "O"))
            sp.dma_start(norm_w[:, 0:512], b_subln_w[l].partition_broadcast(P)).then_inc(norm_w_in, 16)
            sp.dma_start(norm_w[:, 512:768], c_norm_w[l].partition_broadcast(P)).then_inc(norm_w_in, 16)
            for g in GROUPS:
                while n_chunk < len(CHUNKS) and n_chunk <= CHUNK[l, g, chunks_of(g)[-1][0]] + 2:
                    load_chunk(n_chunk)
                    n_chunk += 1
                for t in range(q_tiles(l)):
                    n = Y_OUT[l, g, t]
                    wait_read(sp, ("o", l, g, t))
                    c = Y_COL[g]
                    sp.dma_start(y_dram[t, 0:rows(t), c:c + Y_WIDTH[g]],
                                 y_stage[0:rows(t), n % Y_SLOTS, 0:Y_WIDTH[g]]).then_inc(y_saved[n % Y_SLOTS], 16)
            phase_start(sp, (l, "O"))
            for t in range(q_tiles(l)):
                sp.dma_start(hbuf[0:rows(t), t], h_dram[t, 0:rows(t)]).then_inc(h_in, 16)
            load_ln(ln_g[l], ln_b[l])
            done = Y_OUT[l, GROUPS[-1], q_tiles(l) - 1]
            for s in range(Y_SLOTS):
                sp.wait_ge(y_saved[s], 16 * sum(1 for n in range(1, done + 1) if n % Y_SLOTS == s))
            for t in range(q_tiles(l)):
                if t >= 2:
                    wait_filled(sp, ("y", l, t - 2, 1))
                sp.dma_start(y_load[0:rows(t), t % 2], y_dram[t, 0:rows(t)]).then_inc(y_in[t % 2], 16)
                if n_chunk <= CHUNK[l, "O", 2]:
                    load_chunk(n_chunk)
                    n_chunk += 1
            while n_chunk < len(CHUNKS) and n_chunk <= CHUNK[l, "O", 3] + 2:
                load_chunk(n_chunk)
                n_chunk += 1
            save_h(l, q_tiles(l))
        sp.wait_ge(out_saved, 16 * REAL)

    @block.gpsimd
    def _(pool):
        for i, (l, g, name, kind, parts) in enumerate(CHUNKS):
            n = sum(p[1] for p in parts)
            pool.wait_ge(w_loaded, 16 * CHUNK_DMAS[i])
            if i >= 2:
                before = CHUNKS[i - 2][:3]
                wait_filled(pool, ("unit", *before, units(*before)[-1]))
            pool.tensor_copy(w_hi[:, i % 2, :, 0:n], w_raw[:, :, 0:n]).then_inc(w_hi_done, 1)
            pool.wait_ge(w_hi_done, i + 1)
            pool.tensor_tensor(w_lo[:, i % 2, :, 0:n], w_raw[:, :, 0:n],
                               w_hi[:, i % 2, :, 0:n].bitcast(F32), ALU.subtract).then_inc(w_split, 1)

    @block.tensor
    def _(pe):
        def split_product(out_ap, lhs, rhs):
            n = 0
            for k in range(KT):
                for a, b in ((0, 0), (1, 0), (0, 1)):
                    last = nc.tensor.matmul(out_ap, lhs[a](k), rhs[b](k), start=n == 0, stop=n == 3 * KT - 1)
                    n += 1
            return last

        def project(l, g, name, kind):
            heads = g != "O" and name in HEAD_T
            last_chunk = g == "O" and name == DM // CW - 1 and l < DEPTH - 1
            if heads:
                phase_start(pe, (l, g))
            i = CHUNK[l, g, name]
            pe.wait_ge(w_split, i + 1)
            for x in units(l, g, name):
                key = ("unit", l, g, name, x)
                b = bank(key)
                if g == "O" and name == 0:
                    for j in range(2):
                        wait_read(pe, ("y", l, x, j))
                wait_free(pe, key)
                if kind == "T":
                    f, (a, n) = x[0], T_PIECES[x[1]]
                    last = split_product(
                        psum[:, b, 0:n],
                        [lambda k, w=w: w[:, i % 2, k, f * P:(f + 1) * P] for w in (w_hi, w_lo)],
                        [lambda k, h=h: h[:, k, a:a + n] for h in (hT_hi, hT_lo)])
                else:
                    last = split_product(
                        psum[:, b, 0:CW],
                        [lambda k, h=h: h[:, k, x * P:(x + 1) * P] for h in (hT_hi, hT_lo)],
                        [lambda k, w=w: w[:, i % 2, k, 0:CW] for w in (w_hi, w_lo)])
                last.then_inc(filled[b], 1)
                if heads and x:
                    transposes_of(l, g, name, x - 1)
                if last_chunk and x >= H_LAG - 1:
                    transpose_h(l, x - H_LAG + 1)
            if heads:
                transposes_of(l, g, name, units(l, g, name)[-1])
            if last_chunk:
                for t in range(TILES - H_LAG + 1, TILES):
                    transpose_h(l, t)

        def transpose_h(l, t):
            pe.wait_ge(h_ready, NORM[l, t])
            transpose_rows("h", l + 1, t, hbuf[:, t])

        def transpose_rows(what, l, t, src):
            for j in range(2):
                key = (what, l, t, j)
                b = bank(key)
                wait_free(pe, key)
                for k in range(4):
                    c = (4 * j + k) * P
                    last = nc.tensor.transpose(psum[:, b, k * P:k * P + rows(t)], src[0:rows(t), c:c + P],
                                               ident[0:rows(t), 0:rows(t)])
                last.then_inc(filled[b], 1)

        def mix_c(l, g):
            phase_start(pe, (l, g))
            for lev in range(LEVELS):
                h = HALF[lev]
                for half in range(2):
                    pe.wait_ge(level_selected, LEVEL[l, g, lev, half])
                    pe.wait_ge(seg_ready, SEG[l, g, lev, half])
                    for first, n in level_fills(half, lev):
                        key = ("level", l, g, lev, first)
                        b = bank(key)
                        wait_free(pe, key)
                        for j in range(n):
                            a, m = (first + j) * P, rows(first)
                            q_ap = q_c[:, a:a + m] if lev == 0 else level_ap(lev, "q", 0, P, a, m)
                            for hh in range(2):
                                at = (2 * j + hh) * m
                                o_ap = psum[0:m, b, at:at + m]
                                if lev:
                                    o_ap = o_ap.rearrange("p (n s h) -> p n s h", s=2, h=h)
                                last = nc.tensor.matmul(o_ap, k_pair[:, hh, a:a + m], q_ap, start=True, stop=True)
                        last.then_inc(filled[b], 1)
            for half in range(2):
                pe.wait_ge(seg_ready, SEG[l, g, LEVELS, half])

            def k_transposes(t):
                key = ("knat", l, g, t)
                wait_free(pe, key)
                for d, slot in enumerate((KF_, KB_)):
                    last = nc.tensor.transpose(psum[0:rows(t), bank(key), d * P:(d + 1) * P],
                                               qk[:, slot, cols(t)], ident[:])
                last.then_inc(filled[bank(key)], 1)

            order = [MT, *range(REAL)]
            k_transposes(order[0])
            for i, t in enumerate(order):
                if i + 1 < TILES:
                    k_transposes(order[i + 1])
                key = ("u", l, g, t)
                wait_free(pe, key)
                wait_read(pe, ("knat", l, g, t))
                wait_read(pe, ("unit", l, g, "vg", t))
                for d in range(2):
                    last = nc.tensor.matmul(psum[:, bank(key), d * P:(d + 1) * P], k_nat[0:rows(t), i % 2, d, :],
                                            v_c[0:rows(t), t, :], start=True, stop=True)
                last.then_inc(filled[bank(key)], 1)
            pe.wait_ge(state_ready, C_PAIR[l, g])
            pe.wait_ge(scores_c_ready, C_PAIR[l, g])
            for t in range(q_tiles(l)):
                key = ("o", l, g, t)
                b, m = bank(key), rows(t)
                wait_free(pe, key)
                first = True
                for d, slot in enumerate((QF_, QB_)):
                    if t == (MT, REAL - 1)[d]:
                        continue
                    nc.tensor.matmul(psum[0:m, b, 0:P], qk[:, slot, cols(t)], state[:, d, t, :],
                                     start=first, stop=False)
                    first = False
                for hh in range(2):
                    s_ap = pc_meta[:, hh, :] if t == MT else pc[:, t, hh, :]
                    last = nc.tensor.matmul(psum[0:m, b, hh * HD:(hh + 1) * HD], s_ap,
                                            v_c[0:m, t, hh * HD:(hh + 1) * HD], start=False, stop=hh == 1)
                last.then_inc(filled[b], 1)

        def stacked(out_ap, q_ap, kh_ap, kl_ap):
            nc.tensor.matmul(out_ap, q_ap, kh_ap, start=True, stop=False)
            return nc.tensor.matmul(out_ap, q_ap, kl_ap, start=False, stop=True)

        def transposes_of(l, g, x, t):
            key, n, src = HEAD_T[x](l, g, t)
            pe.wait_ge(roped, ROPE[l, g, x, t])
            wait_free(pe, key)
            for j in range(n):
                last = nc.tensor.transpose(psum[:, bank(key), j * P:(j + 1) * P],
                                           src[:, t % 2, j].rearrange("p d c -> p (d c)"), ident[:])
            last.then_inc(filled[bank(key)], 1)

        HEAD_T = {"q": lambda l, g, t: (("qT", l, g, t), 4, twice_a),
                  "kv": lambda l, g, t: (("kT", l, g, t), 2, twice_a),
                  "qk": lambda l, g, t: (("qkT", l, g, t), 4, twice_b)}

        def mix_a(l):
            g = "A"
            for name, x in (("qT", "q"), ("kT", "kv")):
                for t in units(l, g, x)[-2:]:
                    wait_read(pe, (name, l, g, t))
            wait_read(pe, ("unit", l, g, "kv", TILES - 1))

            def scores(t):
                f, n = window(t)
                m = rows(t)
                for h in range(4):
                    key = ("s", l, g, t, h)
                    b = bank(key)
                    wait_free(pe, key)
                    q_ap = qkT_a[:, h, cols(t)]
                    stacked(psum[0:m, b, 0:n * P], q_ap, qkT_a[:, 4 + h // 2, f * P:(f + n) * P],
                            klT_a[:, h // 2, f * P:(f + n) * P])
                    last = stacked(psum[0:m, b, n * P:n * P + META], q_ap, qkT_a[:, 4 + h // 2, cols(MT)],
                                   klT_a[:, h // 2, cols(MT)])
                    last.then_inc(filled[b], 1)

            def attend(t):
                f, n = window(t)
                m = rows(t)
                o_key = ("o", l, g, t)

                def p_transposes(h):
                    key = ("pT", l, g, t, h)
                    b = bank(key)
                    pe.wait_ge(a_exp, A_HEAD[l, t, h])
                    wait_free(pe, key)
                    for j in range(n):
                        nc.tensor.transpose(psum[:, b, j * P:j * P + m], s_a[0:m, h, j * P:(j + 1) * P],
                                            ident[0:m, 0:m])
                    last = nc.tensor.transpose(psum[0:META, b, n * P:n * P + m], s_a[0:m, h, n * P:n * P + META],
                                               ident[0:m, 0:m])
                    last.then_inc(filled[b], 1)

                p_transposes(0)
                for h in range(4):
                    if h < 3:
                        p_transposes(h + 1)
                    wait_read(pe, ("pT", l, g, t, h))
                    if h == 0:
                        wait_free(pe, o_key)
                    for j in range(n + 1):
                        kr = P if j < n else META
                        last = nc.tensor.matmul(psum[0:m, bank(o_key), h * P:(h + 1) * P],
                                                pT_a[0:kr, h % 2, j, 0:m], v_a[0:kr, f + j if j < n else MT, :],
                                                start=j == 0, stop=j == n)
                    last.then_inc(a_pv if h < 3 else filled[bank(o_key)], 1)

            for t in range(q_tiles(l)):
                scores(t)
                attend(t)

        def mix_b(l, g):
            def scores(t):
                m = rows(t)
                for c in range(2):
                    key = ("s", l, g, t, c)
                    b = bank(key)
                    wait_free(pe, key)
                    for i, (a, n) in enumerate(S_PIECES):
                        last = stacked(psum[0:m, b + i, 0:n], qkT_b[:, c, cols(t)], qkT_b[:, 2 + c, a:a + n],
                                       klT_b[:, c, a:a + n])
                    last.then_inc(filled[b], 1)

            def attend(t):
                m = rows(t)
                pe.wait_ge(b_comb, B_STEP[l, g, t])
                for j in range(3):
                    key = ("aT", l, g, t, j)
                    wait_free(pe, key)
                    for i in range(3):
                        k = 3 * j + i
                        last = nc.tensor.transpose(psum[:, 1, i * P:i * P + m], p_b[0:m, t % 2, 0, k * P:(k + 1) * P],
                                                   ident[0:m, 0:m])
                    last.then_inc(filled[1], 1)
                key = ("o", l, g, t)
                wait_free(pe, key)
                for k in range(TILES):
                    if k % 3 == 0:
                        wait_read(pe, ("aT", l, g, t, k // 3))
                    last = nc.tensor.matmul(psum[0:m, 0, 0:P], aT_b[:, k, 0:m], v_b[:, k, :],
                                            start=k == 0, stop=k == TILES - 1)
                last.then_inc(filled[0], 1)

            for t in (TILES - 2, TILES - 1):
                wait_read(pe, ("qkT", l, g, t))
            wait_read(pe, ("unit", l, g, "vg", TILES - 1))
            pe.wait_ge(b_pad, B_HEAD[l, g])
            for t in range(q_tiles(l) + 1):
                if t < q_tiles(l):
                    scores(t)
                if t:
                    attend(t - 1)

        pe.wait_ge(consts_in, 16 * N_CONSTS)
        for t in range(TILES):
            pe.wait_ge(h_ready, NORM["I", t])
            transpose_rows("h", 0, t, hbuf[:, t])
        for l in range(DEPTH):
            for j in range(2):
                wait_read(pe, ("h", l, TILES - 1, j))
            for g in GROUPS:
                for name, kind, _ in chunks_of(g):
                    project(l, g, name, kind)
                if g[0] == "C":
                    mix_c(l, g)
                elif g == "A":
                    mix_a(l)
                else:
                    mix_b(l, g)
            for t in range(q_tiles(l)):
                pe.wait_ge(y_in[t % 2], 16 * (sum((q_tiles(m) + 1 - t % 2) // 2 for m in range(l)) + t // 2 + 1))
                transpose_rows("y", l, t, y_load[:, t % 2])
            for name, kind, _ in chunks_of("O"):
                project(l, "O", name, kind)

    @block.scalar
    def _(act):
        n_sca = [0]

        def then(ins):
            n_sca[0] += 1
            ins.then_inc(sca, 1)
            act.wait_ge(sca, n_sca[0])

        def hi_of_rows(what, l, t):
            for j in range(2):
                key = (what, l, t, j)
                wait_filled(act, key)
                nc.scalar.copy(hT_hi[:, 4 * j:4 * j + 4, cols(t)],
                               psum[:, bank(key), :].rearrange("p (k c) -> p k c", k=4)[:, :, 0:rows(t)]).then_inc(hi_split, 1)

        def rstd_of(l, t):
            m = rows(t)
            act.wait_ge(var_ready, NORM[l, t])
            then(nc.scalar.activation(rstd[0:m, t, 0:1], mean_var[0:m, t, 1:2], ACT.Ln, bias=eps_ln[0:m]))
            nc.scalar.activation(rstd[0:m, t, 0:1], rstd[0:m, t, 0:1], ACT.Exp, scale=-0.5).then_inc(rstd_ready, 1)

        nc.scalar.preload_act_table_set("natural_log_exp_and_others")
        act.wait_ge(setup_v, 1)
        then(nc.scalar.activation(lam_exp[:], lam_dot[:], ACT.Exp))
        nc.scalar.activation(lbl[:], lbl[:], ACT.Exp).then_inc(setup_s, 1)
        for t in range(TILES):
            rstd_of("I", t)
            if t:
                hi_of_rows("h", 0, t - 1)
        hi_of_rows("h", 0, TILES - 1)

        def evac_c(l, g):
            for name, kind, _ in chunks_of(g):
                for x in units(l, g, name):
                    key = ("unit", l, g, name, x)
                    wait_filled(act, key)
                    b = bank(key)
                    if kind == "T":
                        f, (a, n) = x[0], T_PIECES[x[1]]
                        src = psum[:, b, 0:n]
                        if name == "qf" and f == 0:
                            nc.scalar.copy(q_c[:, a:a + n], src)
                            ins = nc.scalar.activation(qk[:, QB_, a:a + n], src, ACT.Exp, scale=-1.0)
                        else:
                            d = 0 if name == "qf" else 1
                            ins = nc.scalar.activation(qk[:, (KF_, KB_)[d], a:a + n], src, ACT.Exp, scale=-1.0)
                    else:
                        nc.scalar.copy(v_c[:, x, :], psum[:, b, 0:P])
                        nc.scalar.copy(g_c[:, x, :], psum[:, b, P:2 * P])
                        ins = nc.scalar.activation(gate_exp(g)[:, x * P:(x + 1) * P], psum[:, b, P:2 * P],
                                                   ACT.Exp, scale=-1.0)
                    ins.then_inc(released[b], 1)

        def gate_exp(g):
            return k_pair[:].rearrange("p h t -> p (h t)")

        def mix_c(l, g):
            for lev in range(LEVELS):
                for half in range(2):
                    act.wait_ge(seg_ready, SEG[l, g, lev, half])
                    if lev:
                        wait_filled(act, ("level", l, g, lev - 1, level_fills(half, lev - 1)[-1][0]))
                    a, e = span(half, HALF[lev])
                    for hh in range(2):
                        p0 = hh * HD
                        src = k_sum()[p0:p0 + HD, a:e] if lev == 0 else \
                            level_ap(lev, "k", p0, HD, a, e - a)
                        dst = k_pair[p0:p0 + HD, hh, a:e]
                        if lev:
                            dst = dst.rearrange("p (n s h) -> p n s h", s=2, h=HALF[lev])
                        ins = nc.scalar.copy(dst, src)
                    ins.then_inc(level_selected, 1)
            for i, t in enumerate([MT, *range(REAL)]):
                key = ("knat", l, g, t)
                wait_filled(act, key)
                if i >= 2:
                    wait_filled(act, ("u", l, g, [MT, *range(REAL)][i - 2]))
                m = rows(t)
                nc.scalar.copy(k_nat[0:m, i % 2], psum[0:m, bank(key), 0:2 * P].rearrange("p (d c) -> p d c", d=2))\
                    .then_inc(released[bank(key)], 1)
            for t in range(q_tiles(l)):
                key = ("o", l, g, t)
                wait_filled(act, key)
                m = rows(t)
                for hh in range(2):
                    then(nc.scalar.activation(k_nat[0:m, 0, 0, hh * HD:(hh + 1) * HD],
                                              psum[0:m, bank(key), hh * HD:(hh + 1) * HD], ACT.Square,
                                              accum_out=sumsq[0:m, t, hh:hh + 1]))
                then(nc.scalar.activation(rstd[0:m, t, :], sumsq[0:m, t, :], ACT.Ln, bias=eps_rms[0:m], scale=1.0 / HD))
                nc.scalar.activation(rstd[0:m, t, :], rstd[0:m, t, :], ACT.Exp, scale=-0.5).then_inc(rstd_ready, 1)

        def evac_n(l, g, name, x, copies, exps):
            key = ("unit", l, g, name, x)
            wait_filled(act, key)
            b = bank(key)
            for dst, a, n in copies:
                ins = nc.scalar.copy(dst, psum[:, b, a:a + n])
            if exps:
                dst, a, n = exps
                ins = nc.scalar.activation(dst, psum[:, b, a:a + n], ACT.Exp, scale=-1.0)
            ins.then_inc(released[b], 1)

        def qk_hi_of(key, dst, n, m):
            wait_filled(act, key)
            nc.scalar.copy(dst, psum[:, bank(key), 0:n * P].rearrange("p (s c) -> p s c", s=n)[:, :, 0:m])\
                .then_inc(qk_hi, 1)

        def evac_heads(l, g, x, key_of, nat, dst, n, more):
            us = units(l, g, x)
            for t in [*us, None]:
                if t is not None:
                    if ROPE[l, g, x, t] > 2:
                        act.wait_ge(roped, ROPE[l, g, x, t] - 2)
                    evac_n(l, g, x, t, [(nat[:, t % 2, 0:n * HD], 0, n * HD)] + more(t), None)
                if t != 0:
                    u = us[-1] if t is None else t - 1
                    qk_hi_of((key_of, l, g, u), dst[:, :, cols(u)], n, rows(u))

        def group_a(l):
            g = "A"
            evac_heads(l, g, "q", "qT", n_a, qkT_a[:, 0:4], 4, lambda t: [])
            evac_heads(l, g, "kv", "kT", n_a, qkT_a[:, 4:6], 2, lambda t: [(v_a[:, t, :], P, P)])
            for t in units(l, g, "g"):
                if GATE[l, g, t] > 1:
                    act.wait_ge(gate_ready, GATE[l, g, t] - 1)
                evac_n(l, g, "g", t, [(g_a[:, t, :], 0, 256)], (ge_a[:], 0, 256))
            for t in range(q_tiles(l)):
                m = rows(t)
                w = window(t)[1] * P + META
                for h in range(4):
                    act.wait_ge(a_masked, A_HEAD[l, t, h])
                    nc.scalar.activation(sink_exp[0:m, t % 2, h:h + 1], sink_sb[0:m, l, h:h + 1], ACT.Exp,
                                         bias=neg_max[0:m, t % 2, h:h + 1])
                    nc.scalar.activation(s_a[0:m, h, 0:w], s_a[0:m, h, 0:w], ACT.Exp, scale=SCALE,
                                         bias=neg_max[0:m, t % 2, h:h + 1],
                                         accum_out=row_sum[0:m, t % 2, h:h + 1]).then_inc(a_exp, 1)
                for h in range(4):
                    key = ("pT", l, g, t, h)
                    n = window(t)[1]
                    wait_filled(act, key)
                    if h >= 2:
                        act.wait_ge(a_pv, A_PV[l, t, h - 2])
                    elif t and h == 0:
                        act.wait_ge(a_pv, A_PV[l, t - 1, 2])
                    elif t:
                        wait_filled(act, ("o", l, g, t - 1))
                    src = psum[:, bank(key), :].rearrange("p (k c) -> p k c", k=4)
                    nc.scalar.copy(pT_a[:, h % 2, 0:n, 0:m], src[:, 0:n, 0:m])
                    nc.scalar.copy(pT_a[0:META, h % 2, n, 0:m], src[0:META, n, 0:m])\
                        .then_inc(released[bank(key)], 1)

        def group_b(l, g):
            evac_heads(l, g, "qk", "qkT", n_b, qkT_b, 4, lambda t: [])
            for t in units(l, g, "vg"):
                act.wait_ge(gate_ready, GATE[l, g, t] - 1)
                evac_n(l, g, "vg", t, [(v_b[:, t, :], 0, P), (g_b[:, t, :], P, P)], (ge_b[:], P, P))

            def tail(t):
                m = rows(t)
                for j in range(3):
                    key = ("aT", l, g, t, j)
                    wait_filled(act, key)
                    if t and j == 0:
                        wait_filled(act, ("o", l, g, t - 1))
                    nc.scalar.copy(aT_b[:, 3 * j:3 * j + 3, 0:m],
                                   psum[:, 1, 0:3 * P].rearrange("p (k c) -> p k c", k=3)[:, :, 0:m]).then_inc(released[1], 1)
                wait_filled(act, ("o", l, g, t))
                then(nc.scalar.activation(b_junk[0:m, :], psum[0:m, 0, 0:P], ACT.Square,
                                          accum_out=sumsq[0:m, t, 0:1]))
                then(nc.scalar.activation(rstd[0:m, t, 0:1], sumsq[0:m, t, 0:1], ACT.Ln, bias=eps_rms[0:m],
                                          scale=fscale[0:m, t % 2, :]))
                nc.scalar.activation(rstd[0:m, t, 0:1], rstd[0:m, t, 0:1], ACT.Exp, scale=-0.5).then_inc(rstd_ready, 1)

            for t in range(q_tiles(l) + 1):
                if t < q_tiles(l):
                    m = rows(t)
                    for c in range(2):
                        n = B_COMP[l, g, t, c]
                        act.wait_ge(b_max, n)
                        b = bank(("s", l, g, t, c))
                        nc.scalar.activation(p_b[0:m, t % 2, c, 0:2 * S_W].rearrange("p (i n) -> p i n", i=2),
                                             psum[0:m, b:b + 2, 0:S_W], ACT.Exp, scale=SCALE,
                                             bias=neg_max[0:m, t % 2, c:c + 1],
                                             accum_out=row_sum[0:m, t % 2, 2 * c:2 * c + 1])
                        nc.scalar.activation(p_b[0:m, t % 2, c, 2 * S_W:TOK], psum[0:m, b + 2, 0:TOK - 2 * S_W],
                                             ACT.Exp, scale=SCALE, bias=neg_max[0:m, t % 2, c:c + 1],
                                             accum_out=row_sum[0:m, t % 2, 2 * c + 1:2 * c + 2])\
                            .then_inc(released[b], 1)
                if t:
                    tail(t - 1)

        for l in range(DEPTH):
            for g in GROUPS:
                phase_start(act, (l, g))
                if g == "C0":
                    act.wait_ge(h_saved, 16 * TILES * (l + 1))
                if g[0] == "C":
                    evac_c(l, g)
                    mix_c(l, g)
                elif g == "A":
                    group_a(l)
                else:
                    group_b(l, g)
            for t in range(q_tiles(l)):
                hi_of_rows("y", l, t)
            for t in range(q_tiles(l)):
                rstd_of(l, t)
                if t >= H_LAG and l < DEPTH - 1:
                    hi_of_rows("h", l + 1, t - H_LAG)
            if l < DEPTH - 1:
                for t in range(TILES - H_LAG, TILES):
                    hi_of_rows("h", l + 1, t)

    @block.vector
    def _(dve):
        n_vec = [0]

        def then(ins):
            n_vec[0] += 1
            ins.then_inc(vec, 1)
            dve.wait_ge(vec, n_vec[0])

        def mark():
            return n_vec[0]

        tt, ts, stt = nc.vector.tensor_tensor, nc.vector.tensor_scalar, nc.vector.scalar_tensor_tensor

        def release(key):
            dve.sem_inc(released[bank(key)], 1)

        def lo_of_rows(what, l, t):
            for j in range(2):
                key = (what, l, t, j)
                dve.wait_ge(hi_split, T_SPLIT[key])
                tt(hT_lo[:, 4 * j:4 * j + 4, cols(t)],
                   psum[:, bank(key), :].rearrange("p (k c) -> p k c", k=4)[:, :, 0:rows(t)],
                   hT_hi[:, 4 * j:4 * j + 4, cols(t)].bitcast(F32), ALU.subtract).then_inc(released[bank(key)], 1)

        def ln_stats(l, t):
            m = rows(t)
            for i in range(2):
                then(nc.vector.bn_stats(stats[0:m, t, i, :], hbuf[0:m, t, i * 512:(i + 1) * 512]))
            nc.vector.bn_aggr(mean_var[0:m, t, :], stats[0:m, t, :, :].rearrange("p a b -> p (a b)")).then_inc(var_ready, 1)

        def ln_apply(l, t):
            m = rows(t)
            dve.wait_ge(rstd_ready, RSTD[l, t])
            row = hbuf[0:m, t, :]
            then(ts(row, row, mean_var[0:m, t, 0:1], rstd[0:m, t, 0:1], ALU.subtract, ALU.mult))
            then(tt(row, row, ln_w[0:m, 0, :], ALU.mult))
            tt(row, row, ln_w[0:m, 1, :], ALU.add).then_inc(h_ready, 1)

        for h in (hT_hi, hT_lo):
            nc.vector.memset(h[:, :, TOK:].bitcast(F32), 0.0)
        nc.vector.memset(eps_ln[:], LN_EPS)
        nc.vector.memset(eps_rms[:], RMS_EPS)
        dve.wait_ge(consts_in, 16 * N_CONSTS)
        for l in range(DEPTH):
            for i in range(2):
                then(nc.vector.tensor_tensor_reduce(lam_tmp[:], lam_sb[:, l, 2 * i, :], lam_sb[:, l, 2 * i + 1, :],
                                                    1.0, 0.0, ALU.mult, ALU.add, lam_dot[:, l, i:i + 1]))
        then(tt(lb_max[:], lbl[:, 0], lbl[:, 1], ALU.max))
        for l in range(DEPTH):
            then(tt(lbl[:, l], lbl[:, l], lb_max[:], ALU.subtract))
        dve.sem_inc(setup_v, 1)
        dve.wait_ge(setup_s, 1)
        for l in range(DEPTH):
            then(stt(neg_lam[:, l:l + 1], lam_exp[:, l, 1:2], -LAM_INIT[l], lam_exp[:, l, 0:1], ALU.add, ALU.subtract))
        then(tt(lb_sum[:], lbl[:, 0], lbl[:, 1], ALU.add))
        then(nc.vector.reciprocal(lb_sum[:], lb_sum[:]))
        for l in range(DEPTH):
            then(tt(lbl[:, l], lbl[:, l], lb_sum[:], ALU.mult))
        then(tt(lb[:, 1], lbl[:, 0], lbl[:, 1], ALU.add))
        then(tt(lb[:, 1], lb[:, 1], lbl[:, 0], ALU.subtract))
        then(tt(lb[:, 0], lbl[:, 0], lbl[:, 0], ALU.subtract))
        then(ts(one_lb[:], lb[:], -1.0, 1.0, ALU.mult, ALU.add))

        dve.wait_ge(h_in, 16 * TILES)
        dve.wait_ge(ln_in, 32)
        ln_stats("I", 0)
        for t in range(TILES):
            if t + 1 < TILES:
                ln_stats("I", t + 1)
            ln_apply("I", t)
            if t:
                lo_of_rows("h", 0, t - 1)
        lo_of_rows("h", 0, TILES - 1)

        def y_slot(l, g, t):
            n = Y_OUT[l, g, t]
            s = n % Y_SLOTS
            before = (n - 1) // Y_SLOTS if s else n // Y_SLOTS - 1
            if before > 0:
                dve.wait_ge(y_saved[s], 16 * before)
            return s

        def group_c(l, g):
            p = int(g[1])
            for name in ("qf", "b"):
                for x in units(l, g, name):
                    wait_read(dve, ("unit", l, g, name, x))
            oml, lbp = one_lb[:, l, p:p + 1], lb[:, l, p:p + 1]
            f = seg[:, :, 0:TOK]
            k = qk[:, 0:4:3, :]
            then(ts(k, k, E_MAX, None, ALU.min))
            then(ts(f, k, 1.0, None, ALU.add))
            then(nc.vector.reciprocal(f, f))
            for d, slot in enumerate((KF_, KB_)):
                ins = stt(qk[:, slot, :], qk[:, slot, :], oml, seg[:, d, 0:TOK], ALU.mult, ALU.mult)
            then(ins)
            then(ts(f, f, oml, lbp, ALU.mult, ALU.add))
            then(ts(f, f, F_MIN, None, ALU.max))
            qe = qk[:, QB_, :]
            then(ts(qe, qe, 1.0, None, ALU.add))
            then(nc.vector.reciprocal(qe, qe))
            then(tt(q_c[:], q_c[:], qe, ALU.mult))
            for t in (TILES - 2, TILES - 1):
                wait_read(dve, ("unit", l, g, "vg", t))
            ge = k_pair[:].rearrange("p h t -> p (h t)")[:, 0:TILES * P].rearrange("p (t c) -> p t c", c=P)
            then(ts(ge, ge, 1.0, None, ALU.add))
            then(nc.vector.reciprocal(ge, ge))
            then(tt(g_c[:], g_c[:], ge, ALU.mult))
            if g == "C0":
                dve.wait_ge(norm_w_in, 32 * (l + 1))
            w = view(norm_w, 0, P, 512 + p * P, [[0, TILES], [1, P]])
            then(tt(g_c[:], g_c[:], w, ALU.mult))
            then(nc.vector.memset(k_pair[HD:P, 0, :], 0.0))
            then(nc.vector.memset(k_pair[0:HD, 1, :], 0.0))
            then(tt(k_sum(), qk[:, KF_, :], qk[:, KB_, :], ALU.add))
            dve.sem_inc(seg_ready, 2)
            then(tt(qk[:, QF_, :], q_c[:], seg[:, 0, 0:TOK], ALU.mult))
            then(tt(qk[:, QB_, :], q_c[:], seg[:, 1, 0:TOK], ALU.mult))
            dve.sem_inc(seg_ready, 2)
            for lev in range(LEVELS):
                for half in range(2):
                    fills = level_fills(half, lev)
                    if lev:
                        wait_filled(dve, ("level", l, g, lev, fills[-1][0]))
                        extend_segments(lev, half)
                        dve.sem_inc(seg_ready, 1)
                    for first, n in fills:
                        key = ("level", l, g, lev, first)
                        wait_filled(dve, key)
                        m = rows(first)
                        if first == MT:
                            then(nc.vector.copy_predicated(
                                pc_meta[:], view(pair_sb, 0, META, lev * P, [[0, 2], [1, META]]).bitcast(I32),
                                psum[0:m, bank(key), 0:2 * m].rearrange("p (h t) -> p h t", h=2)))
                        else:
                            then(nc.vector.copy_predicated(
                                pc[:, first:first + n].rearrange("p n h t -> p (n h) t"),
                                view(pair_sb, 0, P, lev * P, [[0, 2 * n], [1, P]]).bitcast(I32),
                                psum[:, bank(key), 0:2 * n * P].rearrange("p (h t) -> p h t", t=P)))
                        release(key)
                if lev == 0:
                    then(nc.vector.memset(state[:].rearrange("p d t c -> p (d t c)"), 0.0))
            dve.sem_inc(scores_c_ready, 1)
            uu = k_pair[:].rearrange("p h t -> p (h t)")[:, 0:TILES * P].rearrange("p (t d c) -> p t d c", d=2, c=HD)
            for t in [MT, *range(REAL)]:
                key = ("u", l, g, t)
                wait_filled(dve, key)
                src = psum[:, bank(key), 0:2 * P].rearrange("p (d c) -> p d c", d=2)
                for p0 in (0, HD):
                    then(nc.vector.tensor_copy(uu[p0:p0 + HD, t], src[p0:p0 + HD, :, p0:p0 + HD]))
                release(key)
            fwd = [MT, *range(REAL)]
            bwd = [*range(REAL - 1, -1, -1), MT]
            for i in range(TILES - 1):
                for d, order in ((0, fwd), (1, bwd)):
                    a, b_ = order[i], order[i + 1]
                    for p0 in (0, HD):
                        ps = slice(p0, p0 + HD)
                        if i == 0:
                            ins = nc.vector.tensor_copy(state[ps, d, b_, ps], uu[ps, a, d, :])
                        else:
                            tot = seg[ps, d, SEG_AT[7] + a:SEG_AT[7] + a + 1]
                            ins = stt(state[ps, d, b_, ps], state[ps, d, a, ps], tot, uu[ps, a, d, :],
                                      ALU.mult, ALU.add)
                        if d and p0:
                            then(ins)
            dve.sem_inc(state_ready, 1)
            for t in range(q_tiles(l)):
                key = ("o", l, g, t)
                m = rows(t)
                dve.wait_ge(rstd_ready, RSTD[l, g, t])
                s = y_slot(l, g, t)
                for hh in range(2):
                    hs = slice(hh * HD, (hh + 1) * HD)
                    ins = stt(y_stage[0:m, s, hs], psum[0:m, bank(key), hs], rstd[0:m, t, hh:hh + 1],
                              g_c[0:m, t, hs], ALU.mult, ALU.mult)
                ins.then_inc(released[bank(key)], 1)

        def extend_segments(lev, half):
            h = HALF[lev]
            a, e = span(half, h)
            n = (e - a) // (2 * h)
            at = SEG_AT[lev - 1] + a // h
            tot = [view(seg, 0, P, at + side, [[SEG_ALL, 2], [2, n], [0, h]]) for side in (0, 1)]
            left = view(qk, 0, P, KF_ * TOK + a, [[(QB_ - KF_) * TOK, 2], [2 * h, n], [1, h]])
            right = view(qk, 0, P, QF_ * TOK + a + h, [[(KB_ - QF_) * TOK, 2], [2 * h, n], [1, h]])
            tt(left, left, tot[1], ALU.mult)
            tt(right, right, tot[0], ALU.mult)
            then(tt(view(seg, 0, P, SEG_AT[lev] + a // (2 * h), [[SEG_ALL, 2], [1, n]]),
                    view(seg, 0, P, at, [[SEG_ALL, 2], [2, n]]),
                    view(seg, 0, P, at + 1, [[SEG_ALL, 2], [2, n]]), ALU.mult))

        def rope(l, g, x, t, nat, dup, n, tmp):
            wait_read(dve, ("unit", l, g, x, t))
            if ROPE[l, g, x, t] > 1:
                dve.wait_ge(roped, ROPE[l, g, x, t] - 1)
            base = (t % 2) * 256
            cs = view(cos_sb, 0, P, t * HD, [[0, n], [1, HD]])
            tt(view(tmp, 0, P, 0, [[HD, n], [1, HD]]), view(nat, 0, P, base, [[HD, n], [1, HD]]), cs, ALU.mult)
            for dst, src in ((0, HD // 2), (HD // 2, 0)):
                ins = tt(view(tmp, 0, P, 256 + dst, [[HD, n], [1, HD // 2]]),
                         view(nat, 0, P, base + src, [[HD, n], [1, HD // 2]]),
                         view(sin_sb, 0, P, t * HD + dst, [[0, n], [1, HD // 2]]), ALU.mult)
            then(ins)
            if t >= 2:
                wait_filled(dve, ({"q": "qT", "kv": "kT", "qk": "qkT"}[x], l, g, t - 2))
            elif x == "kv":
                wait_filled(dve, ("qT", l, g, units(l, g, "q")[-1]))
            tt(dup[:, t % 2, 0:n], view(tmp, 0, P, 0, [[HD, n], [0, 2], [1, HD]]),
               view(tmp, 0, P, 256, [[HD, n], [0, 2], [1, HD]]), ALU.add).then_inc(roped, 1)

        def heads(l, g, x, key_of, nat, dup, n, tmp, *parts):
            for t in [*units(l, g, x), None]:
                if t is not None:
                    rope(l, g, x, t, nat, dup, n, tmp)
                if t != 0:
                    u = units(l, g, x)[-1] if t is None else t - 1
                    qk_lo_of(l, g, x, u, (key_of, l, g, u), *parts)

        def qk_lo_of(l, g, x, t, key, qkT, klT, nq, k0, nk):
            dve.wait_ge(qk_hi, QK_HI[l, g, x, t])
            m = rows(t)
            src = psum[:, bank(key), :].rearrange("p (s c) -> p s c", s=4)
            if nq:
                dst = qkT[HD:P, 0:nq, cols(t)]
                ins = tt(dst, src[HD:P, 0:nq, 0:m], dst.bitcast(F32), ALU.subtract)
            if nk:
                ins = tt(klT[:, 0:nk, cols(t)], src[:, nq:nq + nk, 0:m], qkT[:, k0:k0 + nk, cols(t)].bitcast(F32),
                         ALU.subtract)
            ins.then_inc(released[bank(key)], 1)

        def gate(l, g, t, gn, ge, w):
            then(ts(ge, ge, 1.0, None, ALU.add))
            then(nc.vector.reciprocal(ge, ge))
            ins = tt(gn, gn, ge, ALU.mult)
            if w is not None:
                then(ins)
                ins = tt(gn, gn, w, ALU.mult)
            ins.then_inc(gate_ready, 1)

        def group_a(l):
            g = "A"
            heads(l, g, "q", "qT", n_a, twice_a, 4, ra, qkT_a, None, 4, 0, 0)
            heads(l, g, "kv", "kT", n_a, twice_a, 2, ra, qkT_a, klT_a, 0, 4, 2)
            for t in units(l, g, "g"):
                wait_read(dve, ("unit", l, g, "g", t))
                gate(l, g, t, g_a[:, t, :], ge_a[:], None)
            for t in range(q_tiles(l)):
                m = rows(t)
                w = window(t)[1] * P + META
                i = t % 2
                for h in range(4):
                    key = ("s", l, g, t, h)
                    wait_filled(dve, key)
                    if t:
                        wait_filled(dve, ("pT", l, g, t - 1, h))
                    then(nc.vector.tensor_tensor_reduce(s_a[0:m, h, 0:w], psum[0:m, bank(key), 0:w],
                                                        band_sb[0:m, band_columns(t)], 1.0, NEG, ALU.add, ALU.max,
                                                        row_max[0:m, i, h:h + 1]))
                    release(key)
                    then(ts(neg_max[0:m, i, h:h + 1], row_max[0:m, i, h:h + 1], SCALE, sink_sb[0:m, l, h:h + 1],
                            ALU.mult, ALU.max))
                    ts(neg_max[0:m, i, h:h + 1], neg_max[0:m, i, h:h + 1], -1.0, None, ALU.mult).then_inc(a_masked, 1)
                dve.wait_ge(a_exp, A_HEAD[l, t, 3])
                then(tt(inv_sum[0:m, i, :], row_sum[0:m, i, :], sink_exp[0:m, i, :], ALU.add))
                then(nc.vector.reciprocal(inv_sum[0:m, i, :], inv_sum[0:m, i, :]))
                key = ("o", l, g, t)
                wait_filled(dve, key)
                s = y_slot(l, g, t)
                for h in range(4):
                    v0 = h * P + (h // 2) * HD
                    ins = stt(y_stage[0:m, s, h * HD:(h + 1) * HD], psum[0:m, bank(key), v0:v0 + HD],
                              inv_sum[0:m, i, h:h + 1], g_a[0:m, t, h * HD:(h + 1) * HD], ALU.mult, ALU.mult)
                ins.then_inc(released[bank(key)], 1)

        def group_b(l, g):
            hb = int(g[1])
            for c in range(2):
                for j in range(2):
                    nc.vector.memset(p_b[:, j, c, TOK:], 0.0)
            heads(l, g, "qk", "qkT", n_b, twice_b, 4, rb, qkT_b, klT_b, 2, 2, 2)
            for t in units(l, g, "vg"):
                wait_read(dve, ("unit", l, g, "vg", t))
                gate(l, g, t, g_b[:, t, :], ge_b[:], norm_w[:, hb * P:(hb + 1) * P])
            for c in range(2):
                then(nc.vector.memset(psum[:, 4 + 3 * c, TOK - 2 * S_W:S_W], NEG))
            dve.sem_inc(b_pad, 1)

            def finish(t):
                m, i = rows(t), t % 2
                dve.wait_ge(rstd_ready, RSTD[l, g, t])
                then(stt(coef[0:m, i, 1:2], rstd[0:m, t, 0:1], 1.0 - LAM_INIT[l], inv_sum[0:m, i, 0:1],
                         ALU.mult, ALU.mult))
                key = ("o", l, g, t)
                s = y_slot(l, g, t)
                stt(y_stage[0:m, s, 0:P], psum[0:m, 0, 0:P], coef[0:m, i, 1:2], g_b[0:m, t, :],
                    ALU.mult, ALU.mult).then_inc(released[bank(key)], 1)

            for t in range(q_tiles(l) + 1):
                if t < q_tiles(l):
                    m, i = rows(t), t % 2
                    for c in range(2):
                        key = ("s", l, g, t, c)
                        b = bank(key)
                        wait_filled(dve, key)
                        if t >= 2 and c == 0:
                            wait_filled(dve, ("aT", l, g, t - 2, 2))
                        then(nc.vector.tensor_reduce(row_max[0:m, i, c:c + 1], psum[0:m, b:b + 3, 0:S_W],
                                                     AX.XY, ALU.max))
                        ts(neg_max[0:m, i, c:c + 1], row_max[0:m, i, c:c + 1], -SCALE, None,
                           ALU.mult).then_inc(b_max, 1)
                if t:
                    finish(t - 1)
                if t < q_tiles(l):
                    for c in range(2):
                        wait_read(dve, ("s", l, g, t, c))
                    then(tt(row_sum[0:m, i, 0:4:2], row_sum[0:m, i, 0:4:2], row_sum[0:m, i, 1:4:2], ALU.add))
                    then(nc.vector.reciprocal(inv_sum[0:m, i, 0:2], row_sum[0:m, i, 0:4:2]))
                    then(stt(coef[0:m, i, 0:1], inv_sum[0:m, i, 1:2], neg_lam[0:m, l:l + 1], row_sum[0:m, i, 0:1],
                             ALU.mult, ALU.mult))
                    then(stt(fscale[0:m, i, :], inv_sum[0:m, i, 0:1], 1.0 / P, inv_sum[0:m, i, 0:1],
                             ALU.mult, ALU.mult))
                    stt(p_b[0:m, i, 0, 0:TOK], p_b[0:m, i, 1, 0:TOK], coef[0:m, i, 0:1], p_b[0:m, i, 0, 0:TOK],
                        ALU.mult, ALU.add).then_inc(b_comb, 1)

        for l in range(DEPTH):
            for g in GROUPS:
                phase_start(dve, (l, g))
                if g[0] == "C":
                    group_c(l, g)
                elif g == "A":
                    group_a(l)
                else:
                    group_b(l, g)
            phase_start(dve, (l, "O"))
            for t in range(q_tiles(l)):
                lo_of_rows("y", l, t)
            dve.wait_ge(h_in, 16 * (TILES + sum(q_tiles(m) for m in range(l + 1))))
            dve.wait_ge(ln_in, 32 * (l + 2))

            for c in range(DM // CW):
                for t in units(l, "O", c):
                    key = ("unit", l, "O", c, t)
                    wait_filled(dve, key)
                    part = hbuf[0:rows(t), t, c * CW:(c + 1) * CW]
                    then(stt(part, part, ALPHA, psum[0:rows(t), bank(key), 0:CW], ALU.mult, ALU.add))
                    release(key)
                    if c == DM // CW - 1:
                        ln_stats(l, t)
                        if t:
                            ln_apply(l, t - 1)
                        if t >= H_LAG and l < DEPTH - 1:
                            lo_of_rows("h", l + 1, t - H_LAG)
            ln_apply(l, q_tiles(l) - 1)
            if l < DEPTH - 1:
                for t in range(TILES - H_LAG, TILES):
                    lo_of_rows("h", l + 1, t)


N_CONSTS = 5 + 2 + DEPTH * 2
_INS = ["x", "meta", "emb_ln_g", "emb_ln_b", "w_in", "w_out", "a_sink", "b_lam", "b_subln_w", "c_lb_logits",
        "c_norm_w", "ln_g", "ln_b"]


def kernel(**inputs):
    import concourse.bacc as bacc
    from concourse.bass_utils import run_bass_kernel_spmd

    nc = bacc.Bacc("TRN2", target_bir_lowering=False, num_devices=1, dynamic_dma_scratch_size=1024)
    arrays, args = {}, []
    for name, a in [(n, inputs[n]) for n in _INS] + list(CONSTS.items()):
        a = np.ascontiguousarray(a)
        arrays[f"in_{name}"] = a
        args.append(nc.dram_tensor(f"in_{name}", a.shape, mybir.dt.from_np(a.dtype), kind="ExternalInput").ap())
    args.append(nc.dram_tensor("out", (1, REAL * P, DM), F32, kind="ExternalOutput").ap())
    build(nc, *args)
    r = run_bass_kernel_spmd(nc, [arrays], core_ids=[0])
    return r.results[0]["out"]
```

```python
from contextlib import ExitStack

import numpy as np

import concourse.bass as bass
from concourse import mybir

ALU = mybir.AluOpType
ACT = mybir.ActivationFunctionType
F32 = mybir.dt.float32
F32R = mybir.dt.float32r
I32 = mybir.dt.int32
AX = mybir.AxisListType

P = 128
DM = 1024
DEPTH = 2
META = 16
HD = 64
REAL = 8
TILES = REAL + 1
MT = REAL
TOK = REAL * P + META
KT = DM // P
CW = 256
SCALE = HD ** -0.5
ALPHA = (2 * DEPTH) ** 0.25
LN_EPS, RMS_EPS, F_MIN, E_MAX, NEG = 1e-5, 1e-6, 1e-30, 1e37, -1e30
LAM_INIT = [0.8 - 0.6 * float(np.exp(-0.3 * l)) for l in range(DEPTH)]

QA, KA, VA, GA, QB, KB, VB, GB, QC, IC, ZF, ZB, GC = (
    0, 256, 384, 512, 768, 1280, 1792, 2304, 2816, 3072, 3328, 3584, 3840)

LEVELS = 8
HALF = [0] + [2 ** (i - 1) for i in range(1, LEVELS)]
SPAN = [(0, 4 * P), (4 * P, TOK)]


def span(half, h):
    a, b = SPAN[half]
    return (a, b) if h <= META // 2 else (a, min(b, REAL * P))


SEG_N = [TOK if h <= META else REAL * P for h in (1, 2, 4, 8, 16, 32, 64, 128)]
SEG_LEN = [n // h for n, h in zip(SEG_N, (1, 2, 4, 8, 16, 32, 64, 128))]
SEG_AT = [sum(SEG_LEN[:i]) for i in range(8)]
SEG_ALL = sum(SEG_LEN)

GROUPS = ["C0", "C1", "A", "B0", "B1", "B2", "B3"]
Y_COL = {"A": 0, "B0": 256, "B1": 384, "B2": 512, "B3": 640, "C0": 768, "C1": 896}
Y_WIDTH = {g: 256 if g == "A" else 128 for g in GROUPS}
Y_SLOTS = 4
Y_LAG = 3
I_LAG = 2
H_LAG = 4


def rows(t):
    return META if t == MT else P


def q_tiles(l):
    return TILES if l < DEPTH - 1 else REAL


def cols(t):
    return slice(t * P, t * P + rows(t))


def numbered(keys):
    return {k: i + 1 for i, k in enumerate(keys)}


def chunks_of(group):
    if group[0] == "C":
        o = P * int(group[1])
        return [("qf", "T", [(QC + o, P), (ZF + o, P)]), ("b", "T", [(ZB + o, P)]),
                ("vg", "N", [(IC + o, P), (GC + o, P)])]
    if group == "A":
        return [("q", "N", [(QA, CW)]), ("kv", "N", [(KA, CW)]), ("g", "N", [(GA, CW)])]
    if group[0] == "B":
        o = P * int(group[1])
        return [("qk", "N", [(QB + o, P), (KB + o, P)]), ("vg", "N", [(VB + o, P), (GB + o, P)])]
    return [(c, "N", [(c * CW, CW)]) for c in range(DM // CW)]


CHUNKS = [(l, g, *c) for l in range(DEPTH) for g in [*GROUPS, "O"] for c in chunks_of(g)]
CHUNK = {(l, g, name): i for i, (l, g, name, _, _) in enumerate(CHUNKS)}
CHUNK_DMAS = np.cumsum([len(c[4]) for c in CHUNKS]).tolist()
T_PIECES = [(0, 348), (348, 346), (694, 346)]
S_PIECES = [(0, 348), (348, 348), (696, 344)]
S_W = 348
PHASES = ["I"] + [(l, g) for l in range(DEPTH) for g in [*GROUPS, "O"]]
PHASE = {k: i for i, k in enumerate(PHASES)}


def window(t):
    if t == MT:
        return 0, 1
    return max(t - 1, 0), min(t + 1, REAL - 1) - max(t - 1, 0) + 1


def units(l, g, name):
    if g[0] == "C" and name != "vg":
        return [(f, j) for f in range(2 if name == "qf" else 1) for j in range(3)]
    if g == "O" or (g == "A" and name in ("q", "g")):
        return list(range(q_tiles(l)))
    return list(range(TILES))


def level_fills(half, lev):
    a = 4 * half
    out = [(a, 2), (a + 2, 2)]
    if half and HALF[lev] <= META // 2:
        out.append((MT, 1))
    return out


def level_steps():
    steps = [(lev, half) for lev in range(LEVELS) for half in range(2)]
    return [(lev, half, i if i < TILES else None) for i, (lev, half) in enumerate(steps)]


def bank_plan():
    used, plan = [0] * 8, {}

    def add(key, bank):
        plan[key] = (bank, used[bank])
        used[bank] += 1

    def transposed(what, l, tiles, beside_scores=False):
        for t in tiles:
            for j in range(2):
                add((what, l, t, j), j if beside_scores else 2 + 2 * (t % 2) + j)

    transposed("h", 0, range(TILES))
    for l in range(DEPTH):
        u = 0
        for g in GROUPS:
            for name, kind, _ in chunks_of(g):
                for x in units(l, g, name):
                    add(("unit", l, g, name, x), u % 2)
                    u += 1
            if g[0] == "C":
                n = 0
                for lev in range(LEVELS):
                    for half in range(2):
                        for first, _ in level_fills(half, lev):
                            add(("level", l, g, lev, first), 2 + n % 6)
                            n += 1
                for i, t in enumerate([MT, *range(REAL)]):
                    add(("knat", l, g, t), 2 + i % 2)
                    add(("u", l, g, t), 4 + i % 2)
                for t in range(q_tiles(l)):
                    add(("o", l, g, t), (6, 7, 2, 3)[t % 4])
            if g == "A":
                for t in units(l, g, "q"):
                    add(("qT", l, g, t), 2 + 2 * (t % 2))
                for t in units(l, g, "kv"):
                    add(("kT", l, g, t), 3 + 2 * (t % 2))
                for t in range(q_tiles(l)):
                    for h in range(4):
                        add(("s", l, g, t, h), 2 + h)
                        add(("pT", l, g, t, h), 6 + h % 2)
                    add(("o", l, g, t), t % 2)
            if g[0] == "B":
                for t in range(TILES):
                    add(("qkT", l, g, t), 2 + 3 * (t % 2))
                for t in range(q_tiles(l)):
                    for c in range(2):
                        add(("s", l, g, t, c), 2 + 3 * c)
                    for j in range(3):
                        add(("aT", l, g, t, j), (1, 0, 1)[j])
                    add(("o", l, g, t), 0)
                    if g == GROUPS[-1] and t >= Y_LAG:
                        transposed("y", l, [t - Y_LAG], True)
        transposed("y", l, range(q_tiles(l) - Y_LAG, q_tiles(l)))
        for c in range(DM // CW):
            for t in units(l, "O", c):
                add(("unit", l, "O", c, t), t % 2)
        if l < DEPTH - 1:
            transposed("h", l + 1, range(TILES))
    return plan


BANK = bank_plan()

HT = [("h", 0, TILES)] + [x for l in range(DEPTH) for x in
                          [("y", l, q_tiles(l))] + ([("h", l + 1, TILES)] if l < DEPTH - 1 else [])]
T_SPLIT = numbered([(w, l, t, j) for w, l, n in HT for t in range(n) for j in range(2)])
NORM = numbered([("I", t) for t in range(TILES)] + [(l, t) for l in range(DEPTH) for t in range(q_tiles(l))])
HEADS_IN = [(l, g, x, t) for l in range(DEPTH) for g in GROUPS if g[0] != "C"
            for x in (("q", "kv") if g == "A" else ("qk",)) for t in units(l, g, x)]
ROPE = numbered(HEADS_IN)
QK_HI = numbered(HEADS_IN)
Y_OUT = numbered([(l, g, t) for l in range(DEPTH) for g in GROUPS for t in range(q_tiles(l))])
LEVEL = numbered([(l, g, lev, half) for l in range(DEPTH) for g in GROUPS if g[0] == "C"
                  for lev in range(LEVELS) for half in range(2)])
SEG = numbered([(l, g, lev, half) for l in range(DEPTH) for g in GROUPS if g[0] == "C"
                for lev in range(LEVELS + 1) for half in range(2)])
B_HEAD = numbered([(l, g) for l in range(DEPTH) for g in GROUPS if g[0] == "B"])
C_PAIR = numbered([(l, g) for l in range(DEPTH) for g in GROUPS if g[0] == "C"])
RSTD = numbered([("I", t) for t in range(TILES)] + [x for l in range(DEPTH) for x in
                [(l, g, t) for g in GROUPS if g != "A" for t in range(q_tiles(l))]
                + [(l, t) for t in range(q_tiles(l))]])
A_HEAD = numbered([(l, t, h) for l in range(DEPTH) for t in range(q_tiles(l)) for h in range(4)])
B_COMP = numbered([(l, g, t, c) for l in range(DEPTH) for g in GROUPS if g[0] == "B"
                   for t in range(q_tiles(l)) for c in range(2)])
B_STEP = numbered([(l, g, t) for l in range(DEPTH) for g in GROUPS if g[0] == "B" for t in range(q_tiles(l))])
A_PV = numbered([(l, t, h) for l in range(DEPTH) for t in range(q_tiles(l)) for h in range(3)])
GATE = numbered([(l, g, t) for l in range(DEPTH) for g in GROUPS
                 for t in units(l, g, "g" if g == "A" else "vg")])


def shape_constants():
    pos = np.zeros((P, TILES), np.float32)
    for t in range(REAL):
        pos[:, t] = META + t * P + np.arange(P)
    pos[:META, MT] = np.arange(META)
    inv = np.float32(10000.0) ** (-np.arange(0, HD, 2, dtype=np.float32) / np.float32(HD))
    ang = pos[:, :, None] * inv[None, None, :].astype(np.float32)
    cos, sin = np.cos(ang).astype(np.float32), np.sin(ang).astype(np.float32)
    s, t = np.arange(P)[:, None], np.arange(P)[None, :]
    pair = np.zeros((P, LEVELS, P), np.float32)
    pair[:, 0] = s == t
    for i in range(1, LEVELS):
        h = HALF[i]
        pair[:, i] = (s // (2 * h) == t // (2 * h)) & (s // h != t // h)
    i, j = np.arange(P)[:, None], np.arange(P)[None, :]
    prev = np.where(j >= i, 0, NEG).astype(np.float32)
    nxt = np.where(j <= i, 0, NEG).astype(np.float32)
    zero = np.zeros((P, P), np.float32)
    zm = np.zeros((P, META), np.float32)
    meta_q = np.where(j <= P - META + i, 0, NEG).astype(np.float32)
    band = np.concatenate([prev, zero, nxt, zm, prev, zero, zm, meta_q, zm], axis=1)
    return {"eye": np.eye(P, dtype=np.float32), "rope_cos": np.concatenate([cos, cos], axis=2),
            "rope_sin": np.concatenate([-sin, sin], axis=2), "pair_mask": pair, "band_mask": band}


BAND_W = 400 + 272 + 144
CONSTS = shape_constants()


def band_columns(t):
    if t == MT:
        return slice(672, 816)
    if t == REAL - 1:
        return slice(400, 672)
    return slice(P, 400) if t == 0 else slice(0, 400)


def build(nc, x, meta, emb_ln_g, emb_ln_b, w_in, w_out, a_sink, b_lam, b_subln_w, c_lb_logits,
          c_norm_w, ln_g, ln_b, eye, rope_cos, rope_sin, pair_mask, band_mask, out):
    top = ExitStack()

    def sb(stack, name, shape, dt=F32):
        return stack.enter_context(nc.sbuf_tensor(name, shape, dt))

    def sem(name):
        return top.enter_context(nc.semaphore(name))

    h_dram = nc.dram_tensor("h_dram", (TILES, P, DM), F32, kind="Internal").ap()
    y_dram = nc.dram_tensor("y_dram", (TILES, P, DM), F32, kind="Internal").ap()

    hT_hi = sb(top, "hT_hi", [P, KT, TILES * P], F32R)
    hT_lo = sb(top, "hT_lo", [P, KT, TILES * P], F32R)
    w_raw = sb(top, "w_raw", [P, KT, CW])
    w_hi = sb(top, "w_hi", [P, 2, KT, CW], F32R)
    w_lo = sb(top, "w_lo", [P, 2, KT, CW], F32R)
    ident = sb(top, "ident", [P, P])
    cos_sb = sb(top, "cos_sb", [P, TILES, HD])
    sin_sb = sb(top, "sin_sb", [P, TILES, HD])
    pair_sb = sb(top, "pair_sb", [P, LEVELS, P])
    band_sb = sb(top, "band_sb", [P, BAND_W])
    norm_w = sb(top, "norm_w", [P, 768])
    y_load = sb(top, "y_load", [P, 2, DM])
    y_stage = sb(top, "y_stage", [P, Y_SLOTS, 256])
    sink_sb = sb(top, "sink_sb", [P, DEPTH, 4])
    lam_sb = sb(top, "lam_sb", [P, DEPTH, 4, HD])
    lam_tmp = sb(top, "lam_tmp", [P, HD])
    lam_dot = sb(top, "lam_dot", [P, DEPTH, 2])
    lam_exp = sb(top, "lam_exp", [P, DEPTH, 2])
    neg_lam = sb(top, "neg_lam", [P, DEPTH])
    lbl = sb(top, "lbl", [P, DEPTH, 2])
    lb = sb(top, "lb", [P, DEPTH, 2])
    one_lb = sb(top, "one_lb", [P, DEPTH, 2])
    lb_max = sb(top, "lb_max", [P, 2])
    lb_sum = sb(top, "lb_sum", [P, 2])
    stats = sb(top, "stats", [P, TILES, 2, 6])
    mean_var = sb(top, "mean_var", [P, TILES, 2])
    rstd = sb(top, "rstd", [P, TILES, 2])
    sumsq = sb(top, "sumsq", [P, TILES, 2])
    fscale = sb(top, "fscale", [P, 2, 1])
    row_max = sb(top, "row_max", [P, 2, 4])
    neg_max = sb(top, "neg_max", [P, 2, 4])
    row_sum = sb(top, "row_sum", [P, 2, 4])
    sink_exp = sb(top, "sink_exp", [P, 2, 4])
    inv_sum = sb(top, "inv_sum", [P, 2, 4])
    coef = sb(top, "coef", [P, 2, 2])
    eps_ln = sb(top, "eps_ln", [P, 1])
    eps_rms = sb(top, "eps_rms", [P, 1])

    so = ExitStack()
    hbuf = sb(so, "hbuf", [P, TILES, DM])
    ln_w = sb(so, "ln_w", [P, 2, DM])
    so.close()
    sc = ExitStack()
    KF_, QB_, QF_, KB_ = range(4)
    qk = sb(sc, "qk", [P, 4, TOK])
    q_c = sb(sc, "q_c", [P, TOK])
    seg = sb(sc, "seg", [P, 2, SEG_ALL])
    k_pair = sb(sc, "k_pair", [P, 2, TOK])
    pc = sb(sc, "pc", [P, REAL, 2, P])
    pc_meta = sb(sc, "pc_meta", [META, 2, META])
    v_c = sb(sc, "v_c", [P, TILES, P])
    g_c = sb(sc, "g_c", [P, TILES, P])
    state = sb(sc, "state", [P, 2, TILES, P])
    k_nat = sb(sc, "k_nat", [P, 2, 2, P])
    ge_c = sb(sc, "ge_c", [P, 2, P])
    sc.close()
    sa = ExitStack()
    n_a = sb(sa, "n_a", [P, 2, 256])
    twice_a = sb(sa, "twice_a", [P, 2, 4, 2, HD])
    v_a = sb(sa, "v_a", [P, TILES, P])
    g_a = sb(sa, "g_a", [P, TILES, 256])
    ge_a = sb(sa, "ge_a", [P, 256])
    qkT_a = sb(sa, "qkT_a", [P, 6, TOK], F32R)
    klT_a = sb(sa, "klT_a", [P, 2, TOK], F32R)
    s_a = sb(sa, "s_a", [P, 2, 4, 400])
    pT_a = sb(sa, "pT_a", [P, 2, 4, P])
    ra = sb(sa, "ra", [P, 2, 256])
    sa.close()
    sB = ExitStack()
    n_b = sb(sB, "n_b", [P, 2, 256])
    twice_b = sb(sB, "twice_b", [P, 2, 4, 2, HD])
    v_b = sb(sB, "v_b", [P, TILES, P])
    g_b = sb(sB, "g_b", [P, TILES, P])
    qkT_b = sb(sB, "qkT_b", [P, 4, TOK], F32R)
    klT_b = sb(sB, "klT_b", [P, 2, TOK], F32R)
    p_b = sb(sB, "p_b", [P, 2, 2, TILES * P])
    aT_b = sb(sB, "aT_b", [P, TILES, P])
    rb = sb(sB, "rb", [P, 2, 256])
    ge_b = sb(sB, "ge_b", [P, P])
    o_b = sb(sB, "o_b", [P, 2, P])
    b_junk = sb(sB, "b_junk", [P, P])
    sB.close()

    psum = top.enter_context(nc.psum_tensor("psum", [P, 8, 512], F32))

    filled = [sem(f"bank{b}_filled") for b in range(8)]
    released = [sem(f"bank{b}_released") for b in range(8)]
    consts_in = sem("consts_in")
    norm_w_in = sem("norm_w_in")
    w_loaded = sem("w_loaded")
    w_hi_done = sem("w_hi_done")
    w_split = sem("w_split")
    ident_in = sem("ident_in")
    rows_in = [sem(f"rows_in{t}") for t in range(TILES)]
    ln_in = sem("ln_in")
    y_in = [sem(f"y_in{i}") for i in range(2)]
    y_saved = [sem(f"y_saved{i}") for i in range(Y_SLOTS)]
    h_saved = sem("h_saved")
    out_saved = sem("out_saved")
    var_ready = sem("var_ready")
    rstd_ready = sem("rstd_ready")
    scaled = sem("scaled")
    h_ready = sem("h_ready")
    hi_split = sem("hi_split")
    gate_ready = sem("gate_ready")
    seg_ready = sem("seg_ready")
    level_selected = sem("level_selected")
    scores_c_ready = sem("scores_c_ready")
    state_ready = sem("state_ready")
    roped = sem("roped")
    qk_hi = sem("qk_hi")
    a_masked = sem("a_masked")
    a_exp = sem("a_exp")
    a_sinks = sem("a_sinks")
    a_pv = sem("a_pv")
    b_max = sem("b_max")
    b_comb = sem("b_comb")
    b_pad = sem("b_pad")
    b_y = sem("b_y")
    setup_v = sem("setup_v")
    setup_s = sem("setup_s")
    vec = sem("vec")
    sca = sem("sca")

    block = top.enter_context(nc.Block())

    def view(t, p0, np_, off, dims):
        full = t[:]
        width = full.ap[0][0]
        return bass.AP(tensor=full.tensor, offset=p0 * width + off, ap=[[width, np_], *dims])

    def bank(key):
        return BANK[key][0]

    def wait_free(eng, key):
        b, n = BANK[key]
        if n:
            eng.wait_ge(released[b], n)

    def wait_filled(eng, key):
        b, n = BANK[key]
        eng.wait_ge(filled[b], n + 1)

    def wait_read(eng, key):
        b, n = BANK[key]
        eng.wait_ge(released[b], n + 1)

    def phase_start(eng, key):
        before = PHASES[PHASE[key] - 1]
        if before == "I":
            wait_read(eng, ("h", 0, TILES - 1, 1))
        elif before[1] == "O":
            wait_read(eng, ("h", before[0] + 1, TILES - 1, 1))
        else:
            wait_y(eng, *before, q_tiles(before[0]) - 1)

    def wait_y(eng, l, g, t):
        if g[0] == "B":
            eng.wait_ge(b_y, B_STEP[l, g, t])
        else:
            wait_read(eng, ("o", l, g, t))

    def level_ap(lev, side, p0, np_, a, n):
        h = HALF[lev]
        left, right = (KF_, KB_) if side == "k" else (QB_, QF_)
        return view(qk, p0, np_, left * TOK + a, [[2 * h, n // (2 * h)], [(right - left) * TOK + h, 2], [1, h]])

    def k_sum():
        return state[:, 0].rearrange("p t c -> p (t c)")[:, 0:TOK]

    @block.sync
    def _(sp):
        def load_ln(g_ap, b_ap):
            sp.dma_start(ln_w[:, 0], g_ap.partition_broadcast(P)).then_inc(ln_in, 16)
            sp.dma_start(ln_w[:, 1], b_ap.partition_broadcast(P)).then_inc(ln_in, 16)

        for t in range(REAL):
            sp.dma_start(hbuf[:, t], x[0, t * P:(t + 1) * P, :]).then_inc(rows_in[t], 16)
            if t == 0:
                sp.dma_start(ident[:], eye).then_inc(ident_in, 16)
                load_ln(emb_ln_g, emb_ln_b)
        sp.dma_start(hbuf[0:META, MT], meta).then_inc(rows_in[MT], 16)

        def load_chunk(i):
            l, g, name, kind, parts = CHUNKS[i]
            if i:
                sp.wait_ge(w_split, i)
            w = (w_out if g == "O" else w_in)[l].rearrange("(k p) n -> p k n", p=P)
            at = 0
            for c0, n in parts:
                sp.dma_start(w_raw[:, :, at:at + n], w[:, :, c0:c0 + n]).then_inc(w_loaded, 16)
                at += n

        def save_h(l, n):
            for t in range(n):
                sp.wait_ge(h_ready, NORM["I" if l < 0 else l, t])
                if l == DEPTH - 1:
                    sp.dma_start(out[0, t * P:(t + 1) * P, :], hbuf[:, t]).then_inc(out_saved, 16)
                else:
                    sp.dma_start(h_dram[t, 0:rows(t)], hbuf[0:rows(t), t]).then_inc(h_saved, 16)

        load_chunk(0)
        for dst, src in ((cos_sb[:], rope_cos), (sin_sb[:], rope_sin),
                         (pair_sb[:], pair_mask), (band_sb[:], band_mask)):
            sp.dma_start(dst, src).then_inc(consts_in, 16)
        sp.dma_start(sink_sb[:], a_sink.partition_broadcast(P)).then_inc(consts_in, 16)
        sp.dma_start(lam_sb[:], b_lam.partition_broadcast(P)).then_inc(consts_in, 16)
        for l in range(DEPTH):
            for p in range(2):
                sp.dma_start(lbl[:, l, p:p + 1],
                             c_lb_logits[l, p * P:(p + 1) * P].rearrange("(p o) -> p o", o=1)).then_inc(consts_in, 16)

        load_chunk(1)
        save_h(-1, TILES)
        n_chunk = 2
        for l in range(DEPTH):
            if l:
                phase_start(sp, (l - 1, "O"))
            sp.dma_start(norm_w[:, 0:512], b_subln_w[l].partition_broadcast(P)).then_inc(norm_w_in, 16)
            sp.dma_start(norm_w[:, 512:768], c_norm_w[l].partition_broadcast(P)).then_inc(norm_w_in, 16)
            for g in GROUPS:
                while n_chunk < len(CHUNKS) and n_chunk <= CHUNK[l, g, chunks_of(g)[-1][0]] + 2:
                    load_chunk(n_chunk)
                    n_chunk += 1
                for t in range(q_tiles(l)):
                    n = Y_OUT[l, g, t]
                    wait_y(sp, l, g, t)
                    c = Y_COL[g]
                    sp.dma_start(y_dram[t, 0:rows(t), c:c + Y_WIDTH[g]],
                                 y_stage[0:rows(t), n % Y_SLOTS, 0:Y_WIDTH[g]]).then_inc(y_saved[n % Y_SLOTS], 16)
                    if g == GROUPS[-1]:
                        for s in range(Y_SLOTS):
                            sp.wait_ge(y_saved[s], 16 * sum(1 for k in range(1, n + 1) if k % Y_SLOTS == s))
                        if t >= 2:
                            wait_filled(sp, ("y", l, t - 2, 1))
                        sp.dma_start(y_load[0:rows(t), t % 2], y_dram[t, 0:rows(t)]).then_inc(y_in[t % 2], 16)
            load_chunk(n_chunk)
            n_chunk += 1
            phase_start(sp, (l, "O"))
            for t in range(q_tiles(l)):
                sp.dma_start(hbuf[0:rows(t), t], h_dram[t, 0:rows(t)]).then_inc(rows_in[t], 16)
            load_ln(ln_g[l], ln_b[l])
            while n_chunk < len(CHUNKS) and n_chunk <= CHUNK[l, "O", 3] + 2:
                load_chunk(n_chunk)
                n_chunk += 1
            save_h(l, q_tiles(l))
        sp.wait_ge(out_saved, 16 * REAL)

    @block.gpsimd
    def _(pool):
        def split_chunk(i):
            l, g, name, kind, parts = CHUNKS[i]
            n = sum(p[1] for p in parts)
            pool.wait_ge(w_loaded, 16 * CHUNK_DMAS[i])
            if i >= 2:
                before = CHUNKS[i - 2][:3]
                wait_filled(pool, ("unit", *before, units(*before)[-1]))
            pool.tensor_copy(w_hi[:, i % 2, :, 0:n], w_raw[:, :, 0:n]).then_inc(w_hi_done, 1)
            pool.wait_ge(w_hi_done, i + 1)
            pool.tensor_tensor(w_lo[:, i % 2, :, 0:n], w_raw[:, :, 0:n],
                               w_hi[:, i % 2, :, 0:n].bitcast(F32), ALU.subtract).then_inc(w_split, 1)

        def add_ln_bias(l, tiles):
            for t in tiles:
                pool.wait_ge(scaled, NORM[l, t])
                row = hbuf[0:rows(t), t, :]
                pool.tensor_tensor(row, row, ln_w[0:rows(t), 1, :], ALU.add).then_inc(h_ready, 1)

        add_ln_bias("I", range(4))
        split_chunk(0)
        add_ln_bias("I", range(4, TILES))
        for i, (l, g, name, _, _) in enumerate(CHUNKS):
            if i + 1 < len(CHUNKS):
                split_chunk(i + 1)
            if g == "O" and name == DM // CW - 1:
                add_ln_bias(l, range(q_tiles(l)))

    @block.tensor
    def _(pe):
        def split_product(out_ap, lhs, rhs):
            n = 0
            for k in range(KT):
                for a, b in ((0, 0), (1, 0), (0, 1)):
                    last = nc.tensor.matmul(out_ap, lhs[a](k), rhs[b](k), start=n == 0, stop=n == 3 * KT - 1)
                    n += 1
            return last

        def project(l, g, name, kind, only=None):
            heads = g != "O" and name in HEAD_T
            last_chunk = g == "O" and name == DM // CW - 1 and l < DEPTH - 1
            if heads and g == "A":
                phase_start(pe, (l, g))
            i = CHUNK[l, g, name]
            pe.wait_ge(w_split, i + 1)
            for x in units(l, g, name) if only is None else [only]:
                key = ("unit", l, g, name, x)
                b = bank(key)
                if g == "O" and name == 0:
                    for j in range(2):
                        wait_read(pe, ("y", l, x, j))
                wait_free(pe, key)
                if kind == "T":
                    f, (a, n) = x[0], T_PIECES[x[1]]
                    last = split_product(
                        psum[:, b, 0:n],
                        [lambda k, w=w: w[:, i % 2, k, f * P:(f + 1) * P] for w in (w_hi, w_lo)],
                        [lambda k, h=h: h[:, k, a:a + n] for h in (hT_hi, hT_lo)])
                else:
                    last = split_product(
                        psum[:, b, 0:CW],
                        [lambda k, h=h: h[:, k, x * P:(x + 1) * P] for h in (hT_hi, hT_lo)],
                        [lambda k, w=w: w[:, i % 2, k, 0:CW] for w in (w_hi, w_lo)])
                last.then_inc(filled[b], 1)
                if heads and x:
                    transposes_of(l, g, name, x - 1)
                if last_chunk and x >= H_LAG - 1:
                    transpose_h(l, x - H_LAG + 1)
            if heads:
                transposes_of(l, g, name, units(l, g, name)[-1])
            if last_chunk:
                for t in range(TILES - H_LAG + 1, TILES):
                    transpose_h(l, t)

        def transpose_h(l, t):
            pe.wait_ge(h_ready, NORM[l, t])
            transpose_rows("h", l + 1, t, hbuf[:, t])

        def transpose_y(l, t):
            pe.wait_ge(y_in[t % 2], 16 * (sum((q_tiles(m) + 1 - t % 2) // 2 for m in range(l)) + t // 2 + 1))
            transpose_rows("y", l, t, y_load[:, t % 2])

        def transpose_rows(what, l, t, src):
            for j in range(2):
                key = (what, l, t, j)
                b = bank(key)
                wait_free(pe, key)
                for k in range(4):
                    c = (4 * j + k) * P
                    last = nc.tensor.transpose(psum[:, b, k * P:k * P + rows(t)], src[0:rows(t), c:c + P],
                                               ident[0:rows(t), 0:rows(t)])
                last.then_inc(filled[b], 1)

        def mix_c(l, g):
            phase_start(pe, (l, g))
            for lev, half, vg_tile in level_steps():
                h = HALF[lev]
                pe.wait_ge(level_selected, LEVEL[l, g, lev, half])
                pe.wait_ge(seg_ready, SEG[l, g, lev, half])
                for first, n in level_fills(half, lev):
                    key = ("level", l, g, lev, first)
                    b = bank(key)
                    wait_free(pe, key)
                    for j in range(n):
                        a, m = (first + j) * P, rows(first)
                        q_ap = q_c[:, a:a + m] if lev == 0 else level_ap(lev, "q", 0, P, a, m)
                        for hh in range(2):
                            at = (2 * j + hh) * m
                            o_ap = psum[0:m, b, at:at + m]
                            if lev:
                                o_ap = o_ap.rearrange("p (n s h) -> p n s h", s=2, h=h)
                            last = nc.tensor.matmul(o_ap, k_pair[:, hh, a:a + m], q_ap, start=True, stop=True)
                    last.then_inc(filled[b], 1)
                if vg_tile is not None:
                    project(l, g, "vg", "N", vg_tile)
            for half in range(2):
                pe.wait_ge(seg_ready, SEG[l, g, LEVELS, half])

            def k_transposes(t):
                key = ("knat", l, g, t)
                wait_free(pe, key)
                for d, slot in enumerate((KF_, KB_)):
                    last = nc.tensor.transpose(psum[0:rows(t), bank(key), d * P:(d + 1) * P],
                                               qk[:, slot, cols(t)], ident[:])
                last.then_inc(filled[bank(key)], 1)

            order = [MT, *range(REAL)]
            k_transposes(order[0])
            for i, t in enumerate(order):
                if i + 1 < TILES:
                    k_transposes(order[i + 1])
                key = ("u", l, g, t)
                wait_free(pe, key)
                wait_read(pe, ("knat", l, g, t))
                wait_read(pe, ("unit", l, g, "vg", t))
                for d in range(2):
                    last = nc.tensor.matmul(psum[:, bank(key), d * P:(d + 1) * P], k_nat[0:rows(t), i % 2, d, :],
                                            v_c[0:rows(t), t, :], start=True, stop=True)
                last.then_inc(filled[bank(key)], 1)
            pe.wait_ge(state_ready, C_PAIR[l, g])
            pe.wait_ge(scores_c_ready, C_PAIR[l, g])
            for t in range(q_tiles(l)):
                key = ("o", l, g, t)
                b, m = bank(key), rows(t)
                wait_free(pe, key)
                first = True
                for d, slot in enumerate((QF_, QB_)):
                    if t == (MT, REAL - 1)[d]:
                        continue
                    nc.tensor.matmul(psum[0:m, b, 0:P], qk[:, slot, cols(t)], state[:, d, t, :],
                                     start=first, stop=False)
                    first = False
                for hh in range(2):
                    s_ap = pc_meta[:, hh, :] if t == MT else pc[:, t, hh, :]
                    last = nc.tensor.matmul(psum[0:m, b, hh * HD:(hh + 1) * HD], s_ap,
                                            v_c[0:m, t, hh * HD:(hh + 1) * HD], start=False, stop=hh == 1)
                last.then_inc(filled[b], 1)

        def stacked(out_ap, q_ap, kh_ap, kl_ap):
            nc.tensor.matmul(out_ap, q_ap, kh_ap, start=True, stop=False)
            return nc.tensor.matmul(out_ap, q_ap, kl_ap, start=False, stop=True)

        def transposes_of(l, g, x, t):
            key, n, src = HEAD_T[x](l, g, t)
            pe.wait_ge(roped, ROPE[l, g, x, t])
            wait_free(pe, key)
            for j in range(n):
                last = nc.tensor.transpose(psum[:, bank(key), j * P:(j + 1) * P],
                                           src[:, t % 2, j].rearrange("p d c -> p (d c)"), ident[:])
            last.then_inc(filled[bank(key)], 1)

        HEAD_T = {"q": lambda l, g, t: (("qT", l, g, t), 4, twice_a),
                  "kv": lambda l, g, t: (("kT", l, g, t), 2, twice_a),
                  "qk": lambda l, g, t: (("qkT", l, g, t), 4, twice_b)}

        def mix_a(l):
            g = "A"
            for name, x in (("qT", "q"), ("kT", "kv")):
                for t in units(l, g, x)[-2:]:
                    wait_read(pe, (name, l, g, t))
            wait_read(pe, ("unit", l, g, "kv", TILES - 1))

            def scores(t, h):
                if t >= q_tiles(l):
                    return
                f, n = window(t)
                m = rows(t)
                key = ("s", l, g, t, h)
                b = bank(key)
                wait_free(pe, key)
                q_ap = qkT_a[:, h, cols(t)]
                stacked(psum[0:m, b, 0:n * P], q_ap, qkT_a[:, 4 + h // 2, f * P:(f + n) * P],
                        klT_a[:, h // 2, f * P:(f + n) * P])
                last = stacked(psum[0:m, b, n * P:n * P + META], q_ap, qkT_a[:, 4 + h // 2, cols(MT)],
                               klT_a[:, h // 2, cols(MT)])
                last.then_inc(filled[b], 1)

            def attend(t):
                f, n = window(t)
                m = rows(t)
                o_key = ("o", l, g, t)

                def p_transposes(h):
                    key = ("pT", l, g, t, h)
                    b = bank(key)
                    pe.wait_ge(a_exp, A_HEAD[l, t, h])
                    wait_free(pe, key)
                    for j in range(n):
                        nc.tensor.transpose(psum[:, b, j * P:j * P + m], s_a[0:m, t % 2, h, j * P:(j + 1) * P],
                                            ident[0:m, 0:m])
                    last = nc.tensor.transpose(psum[0:META, b, n * P:n * P + m],
                                               s_a[0:m, t % 2, h, n * P:n * P + META], ident[0:m, 0:m])
                    last.then_inc(filled[b], 1)

                p_transposes(0)
                for h in range(4):
                    if h < 3:
                        p_transposes(h + 1)
                    scores(t + 1, h)
                    wait_read(pe, ("pT", l, g, t, h))
                    if h == 0:
                        wait_free(pe, o_key)
                    for j in range(n + 1):
                        kr = P if j < n else META
                        last = nc.tensor.matmul(psum[0:m, bank(o_key), h * P:(h + 1) * P],
                                                pT_a[0:kr, h % 2, j, 0:m], v_a[0:kr, f + j if j < n else MT, :],
                                                start=j == 0, stop=j == n)
                    last.then_inc(a_pv if h < 3 else filled[bank(o_key)], 1)

            for h in range(4):
                scores(0, h)
            for t in range(q_tiles(l)):
                attend(t)

        def mix_b(l, g):
            def scores(t, c):
                if t >= q_tiles(l):
                    return
                m = rows(t)
                key = ("s", l, g, t, c)
                b = bank(key)
                wait_free(pe, key)
                for i, (a, n) in enumerate(S_PIECES):
                    last = stacked(psum[0:m, b + i, 0:n], qkT_b[:, c, cols(t)], qkT_b[:, 2 + c, a:a + n],
                                   klT_b[:, c, a:a + n])
                last.then_inc(filled[b], 1)

            def transposes(t, j):
                m = rows(t)
                key = ("aT", l, g, t, j)
                b = bank(key)
                wait_free(pe, key)
                for i in range(3):
                    k = 3 * j + i
                    last = nc.tensor.transpose(psum[:, b, i * P:i * P + m], p_b[0:m, t % 2, 0, k * P:(k + 1) * P],
                                               ident[0:m, 0:m])
                last.then_inc(filled[b], 1)

            def values(t):
                m = rows(t)
                key = ("o", l, g, t)
                wait_free(pe, key)
                for k in range(TILES):
                    if k % 3 == 0:
                        wait_read(pe, ("aT", l, g, t, k // 3))
                    last = nc.tensor.matmul(psum[0:m, 0, 0:P], aT_b[:, k, 0:m], v_b[:, k, :],
                                            start=k == 0, stop=k == TILES - 1)
                last.then_inc(filled[0], 1)

            for t in (TILES - 2, TILES - 1):
                wait_read(pe, ("qkT", l, g, t))
            wait_read(pe, ("unit", l, g, "vg", TILES - 1))
            pe.wait_ge(b_pad, B_HEAD[l, g])
            scores(0, 0)
            scores(0, 1)
            scores(1, 0)
            for t in range(q_tiles(l)):
                scores(t + 1, 1)
                pe.wait_ge(b_comb, B_STEP[l, g, t])
                transposes(t, 0)
                transposes(t, 1)
                scores(t + 2, 0)
                transposes(t, 2)
                values(t)
                if g == GROUPS[-1] and t >= Y_LAG:
                    transpose_y(l, t - Y_LAG)

        pe.wait_ge(ident_in, 16)
        for t in range(TILES):
            pe.wait_ge(h_ready, NORM["I", t])
            transpose_rows("h", 0, t, hbuf[:, t])
        for l in range(DEPTH):
            for j in range(2):
                wait_read(pe, ("h", l, TILES - 1, j))
            for g in GROUPS:
                for name, kind, _ in chunks_of(g):
                    if g[0] != "C" or name != "vg":
                        project(l, g, name, kind)
                if g[0] == "C":
                    mix_c(l, g)
                elif g == "A":
                    mix_a(l)
                else:
                    mix_b(l, g)
            for t in range(q_tiles(l) - Y_LAG, q_tiles(l)):
                transpose_y(l, t)
            for name, kind, _ in chunks_of("O"):
                project(l, "O", name, kind)

    @block.scalar
    def _(act):
        n_sca = [0]

        def then(ins):
            n_sca[0] += 1
            ins.then_inc(sca, 1)
            act.wait_ge(sca, n_sca[0])

        def hi_of_rows(what, l, t):
            for j in range(2):
                key = (what, l, t, j)
                wait_filled(act, key)
                nc.scalar.copy(hT_hi[:, 4 * j:4 * j + 4, cols(t)],
                               psum[:, bank(key), :].rearrange("p (k c) -> p k c", k=4)[:, :, 0:rows(t)]).then_inc(hi_split, 1)

        def rstd_of(l, t):
            m = rows(t)
            act.wait_ge(var_ready, NORM[l, t])
            then(nc.scalar.activation(rstd[0:m, t, 0:1], mean_var[0:m, t, 1:2], ACT.Ln, bias=eps_ln[0:m]))
            then(nc.scalar.activation(rstd[0:m, t, 0:1], rstd[0:m, t, 0:1], ACT.Exp, scale=-0.5))
            then(nc.scalar.activation(rstd[0:m, t, 1:2], mean_var[0:m, t, 0:1], ACT.Copy, scale=rstd[0:m, t, 0:1]))
            then(nc.scalar.activation(rstd[0:m, t, 1:2], rstd[0:m, t, 1:2], ACT.Copy, scale=-1.0))
            nc.scalar.activation(hbuf[0:m, t, :], hbuf[0:m, t, :], ACT.Identity, scale=rstd[0:m, t, 0:1],
                                 bias=rstd[0:m, t, 1:2]).then_inc(rstd_ready, 1)

        nc.scalar.preload_act_table_set("natural_log_exp_and_others")
        for t in range(TILES + I_LAG):
            if t < TILES:
                rstd_of("I", t)
            if t >= I_LAG:
                hi_of_rows("h", 0, t - I_LAG)
        act.wait_ge(setup_v, 1)
        then(nc.scalar.activation(lam_exp[:], lam_dot[:], ACT.Exp))
        nc.scalar.activation(lbl[:], lbl[:], ACT.Exp).then_inc(setup_s, 1)

        def evac_c(l, g):
            for name in ("qf", "b"):
                for f, j in units(l, g, name):
                    key = ("unit", l, g, name, (f, j))
                    wait_filled(act, key)
                    b = bank(key)
                    a, n = T_PIECES[j]
                    src = psum[:, b, 0:n]
                    if name == "qf" and f == 0:
                        nc.scalar.copy(q_c[:, a:a + n], src)
                        slot = QB_
                    else:
                        slot = KF_ if name == "qf" else KB_
                    nc.scalar.activation(qk[:, slot, a:a + n], src, ACT.Exp, scale=-1.0).then_inc(released[b], 1)

        def mix_c(l, g):
            for i, (lev, half, vg_tile) in enumerate(level_steps()):
                act.wait_ge(seg_ready, SEG[l, g, lev, half])
                if lev:
                    wait_filled(act, ("level", l, g, lev - 1, level_fills(half, lev - 1)[-1][0]))
                a, e = span(half, HALF[lev])
                for hh in range(2):
                    p0 = hh * HD
                    src = k_sum()[p0:p0 + HD, a:e] if lev == 0 else level_ap(lev, "k", p0, HD, a, e - a)
                    dst = k_pair[p0:p0 + HD, hh, a:e]
                    if lev:
                        dst = dst.rearrange("p (n s h) -> p n s h", s=2, h=HALF[lev])
                    ins = nc.scalar.copy(dst, src)
                ins.then_inc(level_selected, 1)
                x = level_steps()[i - 1][2] if i else None
                if x is not None:
                    key = ("unit", l, g, "vg", x)
                    wait_filled(act, key)
                    if x >= 2:
                        act.wait_ge(gate_ready, GATE[l, g, x - 2])
                    nc.scalar.copy(v_c[:, x, :], psum[:, bank(key), 0:P])
                    nc.scalar.copy(g_c[:, x, :], psum[:, bank(key), P:2 * P])
                    nc.scalar.activation(ge_c[:, x % 2, :], psum[:, bank(key), P:2 * P], ACT.Exp, scale=-1.0)\
                        .then_inc(released[bank(key)], 1)
            for i, t in enumerate([MT, *range(REAL)]):
                key = ("knat", l, g, t)
                wait_filled(act, key)
                if i >= 2:
                    wait_filled(act, ("u", l, g, [MT, *range(REAL)][i - 2]))
                m = rows(t)
                nc.scalar.copy(k_nat[0:m, i % 2], psum[0:m, bank(key), 0:2 * P].rearrange("p (d c) -> p d c", d=2))\
                    .then_inc(released[bank(key)], 1)
            for t in range(q_tiles(l)):
                key = ("o", l, g, t)
                wait_filled(act, key)
                m = rows(t)
                for hh in range(2):
                    then(nc.scalar.activation(k_nat[0:m, 0, 0, hh * HD:(hh + 1) * HD],
                                              psum[0:m, bank(key), hh * HD:(hh + 1) * HD], ACT.Square,
                                              accum_out=sumsq[0:m, t, hh:hh + 1]))
                then(nc.scalar.activation(rstd[0:m, t, :], sumsq[0:m, t, :], ACT.Ln, bias=eps_rms[0:m], scale=1.0 / HD))
                nc.scalar.activation(rstd[0:m, t, :], rstd[0:m, t, :], ACT.Exp, scale=-0.5).then_inc(rstd_ready, 1)

        def evac_n(l, g, name, x, copies, exps):
            key = ("unit", l, g, name, x)
            wait_filled(act, key)
            b = bank(key)
            for dst, a, n in copies:
                ins = nc.scalar.copy(dst, psum[:, b, a:a + n])
            if exps:
                dst, a, n = exps
                ins = nc.scalar.activation(dst, psum[:, b, a:a + n], ACT.Exp, scale=-1.0)
            ins.then_inc(released[b], 1)

        def qk_hi_of(key, dst, n, m):
            wait_filled(act, key)
            nc.scalar.copy(dst, psum[:, bank(key), 0:n * P].rearrange("p (s c) -> p s c", s=n)[:, :, 0:m])\
                .then_inc(qk_hi, 1)

        def evac_heads(l, g, x, key_of, nat, dst, n, more):
            us = units(l, g, x)
            for t in [*us, None]:
                if t is not None:
                    if ROPE[l, g, x, t] > 2:
                        act.wait_ge(roped, ROPE[l, g, x, t] - 2)
                    evac_n(l, g, x, t, [(nat[:, t % 2, 0:n * HD], 0, n * HD)] + more(t), None)
                if t != 0:
                    u = us[-1] if t is None else t - 1
                    qk_hi_of((key_of, l, g, u), dst[:, :, cols(u)], n, rows(u))

        def group_a(l):
            g = "A"
            evac_heads(l, g, "q", "qT", n_a, qkT_a[:, 0:4], 4, lambda t: [])
            evac_heads(l, g, "kv", "kT", n_a, qkT_a[:, 4:6], 2, lambda t: [(v_a[:, t, :], P, P)])
            for t in units(l, g, "g"):
                if GATE[l, g, t] > 1:
                    act.wait_ge(gate_ready, GATE[l, g, t] - 1)
                evac_n(l, g, "g", t, [(g_a[:, t, :], 0, 256)], (ge_a[:], 0, 256))

            def exps(t, h):
                if t >= q_tiles(l):
                    return
                m, i = rows(t), t % 2
                w = window(t)[1] * P + META
                act.wait_ge(a_masked, A_HEAD[l, t, h])
                nc.scalar.activation(s_a[0:m, i, h, 0:w], s_a[0:m, i, h, 0:w], ACT.Exp, scale=SCALE,
                                     bias=neg_max[0:m, i, h:h + 1], accum_out=row_sum[0:m, i, h:h + 1])\
                    .then_inc(a_exp, 1)
                nc.scalar.activation(sink_exp[0:m, i, h:h + 1], sink_sb[0:m, l, h:h + 1], ACT.Exp,
                                     bias=neg_max[0:m, i, h:h + 1]).then_inc(a_sinks, 1)

            def evac_probs(t, h):
                key = ("pT", l, g, t, h)
                m, n = rows(t), window(t)[1]
                wait_filled(act, key)
                if h >= 2:
                    act.wait_ge(a_pv, A_PV[l, t, h - 2])
                elif t and h == 0:
                    act.wait_ge(a_pv, A_PV[l, t - 1, 2])
                elif t:
                    wait_filled(act, ("o", l, g, t - 1))
                src = psum[:, bank(key), :].rearrange("p (k c) -> p k c", k=4)
                nc.scalar.copy(pT_a[:, h % 2, 0:n, 0:m], src[:, 0:n, 0:m])
                nc.scalar.copy(pT_a[0:META, h % 2, n, 0:m], src[0:META, n, 0:m]).then_inc(released[bank(key)], 1)

            for h in range(4):
                exps(0, h)
            for t in range(q_tiles(l)):
                for h in range(4):
                    evac_probs(t, h)
                    exps(t + 1, h)

        def group_b(l, g):
            evac_heads(l, g, "qk", "qkT", n_b, qkT_b, 4, lambda t: [])
            for t in units(l, g, "vg"):
                act.wait_ge(gate_ready, GATE[l, g, t] - 1)
                evac_n(l, g, "vg", t, [(v_b[:, t, :], 0, P), (g_b[:, t, :], P, P)], (ge_b[:], P, P))

            def exps(t, c):
                if t >= q_tiles(l):
                    return
                m = rows(t)
                act.wait_ge(b_max, B_COMP[l, g, t, c])
                b = bank(("s", l, g, t, c))
                nc.scalar.activation(p_b[0:m, t % 2, c, 0:2 * S_W].rearrange("p (i n) -> p i n", i=2),
                                     psum[0:m, b:b + 2, 0:S_W], ACT.Exp, scale=SCALE,
                                     bias=neg_max[0:m, t % 2, c:c + 1],
                                     accum_out=row_sum[0:m, t % 2, 2 * c:2 * c + 1])
                nc.scalar.activation(p_b[0:m, t % 2, c, 2 * S_W:TOK], psum[0:m, b + 2, 0:TOK - 2 * S_W],
                                     ACT.Exp, scale=SCALE, bias=neg_max[0:m, t % 2, c:c + 1],
                                     accum_out=row_sum[0:m, t % 2, 2 * c + 1:2 * c + 2])\
                    .then_inc(released[b], 1)

            def evac_probs(t, j):
                key = ("aT", l, g, t, j)
                b, m = bank(key), rows(t)
                wait_filled(act, key)
                if t and j == 0:
                    wait_filled(act, ("o", l, g, t - 1))
                nc.scalar.copy(aT_b[:, 3 * j:3 * j + 3, 0:m],
                               psum[:, b, 0:3 * P].rearrange("p (k c) -> p k c", k=3)[:, :, 0:m])\
                    .then_inc(released[b], 1)

            def norm(t):
                key = ("o", l, g, t)
                m = rows(t)
                wait_filled(act, key)
                if B_STEP[l, g, t] > 2:
                    act.wait_ge(b_y, B_STEP[l, g, t] - 2)
                nc.scalar.copy(o_b[0:m, t % 2, :], psum[0:m, 0, 0:P]).then_inc(released[0], 1)
                wait_read(act, key)
                then(nc.scalar.activation(b_junk[0:m, :], o_b[0:m, t % 2, :], ACT.Square,
                                          accum_out=sumsq[0:m, t, 0:1]))
                then(nc.scalar.activation(rstd[0:m, t, 0:1], sumsq[0:m, t, 0:1], ACT.Ln, bias=eps_rms[0:m],
                                          scale=fscale[0:m, t % 2, :]))
                nc.scalar.activation(rstd[0:m, t, 0:1], rstd[0:m, t, 0:1], ACT.Exp, scale=-0.5).then_inc(rstd_ready, 1)

            exps(0, 0)
            exps(0, 1)
            for t in range(q_tiles(l)):
                if g == GROUPS[-1] and t > Y_LAG:
                    hi_of_rows("y", l, t - 1 - Y_LAG)
                exps(t + 1, 0)
                for j in range(3):
                    evac_probs(t, j)
                exps(t + 1, 1)
                norm(t)

        for l in range(DEPTH):
            for g in GROUPS:
                phase_start(act, (l, g))
                if g == "C0":
                    act.wait_ge(h_saved, 16 * TILES * (l + 1))
                if g[0] == "C":
                    evac_c(l, g)
                    mix_c(l, g)
                elif g == "A":
                    group_a(l)
                else:
                    group_b(l, g)
            for t in range(q_tiles(l) - 1 - Y_LAG, q_tiles(l)):
                hi_of_rows("y", l, t)
            for t in range(q_tiles(l)):
                rstd_of(l, t)
                if t >= H_LAG and l < DEPTH - 1:
                    hi_of_rows("h", l + 1, t - H_LAG)
            if l < DEPTH - 1:
                for t in range(TILES - H_LAG, TILES):
                    hi_of_rows("h", l + 1, t)

    @block.vector
    def _(dve):
        n_vec = [0]

        def then(ins):
            n_vec[0] += 1
            ins.then_inc(vec, 1)
            dve.wait_ge(vec, n_vec[0])

        def mark():
            return n_vec[0]

        tt, ts, stt = nc.vector.tensor_tensor, nc.vector.tensor_scalar, nc.vector.scalar_tensor_tensor

        def release(key):
            dve.sem_inc(released[bank(key)], 1)

        def lo_of_rows(what, l, t):
            for j in range(2):
                key = (what, l, t, j)
                dve.wait_ge(hi_split, T_SPLIT[key])
                tt(hT_lo[:, 4 * j:4 * j + 4, cols(t)],
                   psum[:, bank(key), :].rearrange("p (k c) -> p k c", k=4)[:, :, 0:rows(t)],
                   hT_hi[:, 4 * j:4 * j + 4, cols(t)].bitcast(F32), ALU.subtract).then_inc(released[bank(key)], 1)

        def ln_stats(l, t):
            m = rows(t)
            for i in range(2):
                then(nc.vector.bn_stats(stats[0:m, t, i, :], hbuf[0:m, t, i * 512:(i + 1) * 512]))
            nc.vector.bn_aggr(mean_var[0:m, t, :], stats[0:m, t, :, :].rearrange("p a b -> p (a b)")).then_inc(var_ready, 1)

        def ln_apply(l, t):
            m = rows(t)
            dve.wait_ge(rstd_ready, RSTD[l, t])
            row = hbuf[0:m, t, :]
            tt(row, row, ln_w[0:m, 0, :], ALU.mult).then_inc(scaled, 1)

        for h in (hT_hi, hT_lo):
            nc.vector.memset(h[:, :, TOK:].bitcast(F32), 0.0)
        nc.vector.memset(eps_ln[:], LN_EPS)
        nc.vector.memset(eps_rms[:], RMS_EPS)
        dve.wait_ge(rows_in[0], 16)
        ln_stats("I", 0)
        dve.wait_ge(ln_in, 32)
        for t in range(TILES + I_LAG):
            if t + 1 < TILES:
                dve.wait_ge(rows_in[t + 1], 16)
                ln_stats("I", t + 1)
            if t < TILES:
                ln_apply("I", t)
            if t >= I_LAG:
                lo_of_rows("h", 0, t - I_LAG)
        dve.wait_ge(consts_in, 16 * N_CONSTS)
        for l in range(DEPTH):
            for i in range(2):
                then(nc.vector.tensor_tensor_reduce(lam_tmp[:], lam_sb[:, l, 2 * i, :], lam_sb[:, l, 2 * i + 1, :],
                                                    1.0, 0.0, ALU.mult, ALU.add, lam_dot[:, l, i:i + 1]))
        then(tt(lb_max[:], lbl[:, 0], lbl[:, 1], ALU.max))
        for l in range(DEPTH):
            then(tt(lbl[:, l], lbl[:, l], lb_max[:], ALU.subtract))
        dve.sem_inc(setup_v, 1)
        dve.wait_ge(setup_s, 1)
        for l in range(DEPTH):
            then(stt(neg_lam[:, l:l + 1], lam_exp[:, l, 1:2], -LAM_INIT[l], lam_exp[:, l, 0:1], ALU.add, ALU.subtract))
        then(tt(lb_sum[:], lbl[:, 0], lbl[:, 1], ALU.add))
        then(nc.vector.reciprocal(lb_sum[:], lb_sum[:]))
        for l in range(DEPTH):
            then(tt(lbl[:, l], lbl[:, l], lb_sum[:], ALU.mult))
        then(tt(lb[:, 1], lbl[:, 0], lbl[:, 1], ALU.add))
        then(tt(lb[:, 1], lb[:, 1], lbl[:, 0], ALU.subtract))
        then(tt(lb[:, 0], lbl[:, 0], lbl[:, 0], ALU.subtract))
        then(ts(one_lb[:], lb[:], -1.0, 1.0, ALU.mult, ALU.add))

        def y_slot(l, g, t):
            n = Y_OUT[l, g, t]
            s = n % Y_SLOTS
            before = (n - 1) // Y_SLOTS if s else n // Y_SLOTS - 1
            if before > 0:
                dve.wait_ge(y_saved[s], 16 * before)
            return s

        def group_c(l, g):
            p = int(g[1])
            oml, lbp = one_lb[:, l, p:p + 1], lb[:, l, p:p + 1]
            then(nc.vector.memset(k_pair[HD:P, 0, :], 0.0))
            then(nc.vector.memset(k_pair[0:HD, 1, :], 0.0))
            for name in ("qf", "b"):
                for fb, j in units(l, g, name):
                    wait_read(dve, ("unit", l, g, name, (fb, j)))
                    a, n = T_PIECES[j]
                    if name == "qf" and fb == 0:
                        qe = qk[:, QB_, a:a + n]
                        then(ts(qe, qe, 1.0, None, ALU.add))
                        then(nc.vector.reciprocal(qe, qe))
                        then(tt(q_c[:, a:a + n], q_c[:, a:a + n], qe, ALU.mult))
                        continue
                    d, slot = (0, KF_) if name == "qf" else (1, KB_)
                    k, f = qk[:, slot, a:a + n], seg[:, d, a:a + n]
                    then(ts(k, k, E_MAX, None, ALU.min))
                    then(ts(f, k, 1.0, None, ALU.add))
                    then(nc.vector.reciprocal(f, f))
                    then(stt(k, k, oml, f, ALU.mult, ALU.mult))
                    then(ts(f, f, oml, lbp, ALU.mult, ALU.add))
                    then(ts(f, f, F_MIN, None, ALU.max))
            if g == "C0":
                dve.wait_ge(norm_w_in, 32 * (l + 1))
            w = norm_w[:, 512 + p * P:512 + (p + 1) * P]
            then(tt(k_sum(), qk[:, KF_, :], qk[:, KB_, :], ALU.add))
            dve.sem_inc(seg_ready, 2)
            then(tt(qk[:, QF_, :], q_c[:], seg[:, 0, 0:TOK], ALU.mult))
            then(tt(qk[:, QB_, :], q_c[:], seg[:, 1, 0:TOK], ALU.mult))
            dve.sem_inc(seg_ready, 2)
            for i, (lev, half, _) in enumerate(level_steps()):
                fills = level_fills(half, lev)
                if lev:
                    wait_filled(dve, ("level", l, g, lev, fills[-1][0]))
                    extend_segments(lev, half)
                    dve.sem_inc(seg_ready, 1)
                for first, n in fills:
                    key = ("level", l, g, lev, first)
                    wait_filled(dve, key)
                    m = rows(first)
                    if first == MT:
                        then(nc.vector.copy_predicated(
                            pc_meta[:], view(pair_sb, 0, META, lev * P, [[0, 2], [1, META]]).bitcast(I32),
                            psum[0:m, bank(key), 0:2 * m].rearrange("p (h t) -> p h t", h=2)))
                    else:
                        then(nc.vector.copy_predicated(
                            pc[:, first:first + n].rearrange("p n h t -> p (n h) t"),
                            view(pair_sb, 0, P, lev * P, [[0, 2 * n], [1, P]]).bitcast(I32),
                            psum[:, bank(key), 0:2 * n * P].rearrange("p (h t) -> p h t", t=P)))
                    release(key)
                if lev == 0 and half:
                    then(nc.vector.memset(state[:].rearrange("p d t c -> p (d t c)"), 0.0))
                x = level_steps()[i - 2][2] if i >= 2 else None
                if x is not None:
                    wait_read(dve, ("unit", l, g, "vg", x))
                    gate(l, g, x, g_c[:, x, :], ge_c[:, x % 2, :], w)
            for t in (TILES - 2, TILES - 1):
                dve.wait_ge(gate_ready, GATE[l, g, t])
            dve.sem_inc(scores_c_ready, 1)
            uu = k_pair[:].rearrange("p h t -> p (h t)")[:, 0:TILES * P].rearrange("p (t d c) -> p t d c", d=2, c=HD)
            for t in [MT, *range(REAL)]:
                key = ("u", l, g, t)
                wait_filled(dve, key)
                src = psum[:, bank(key), 0:2 * P].rearrange("p (d c) -> p d c", d=2)
                for p0 in (0, HD):
                    then(nc.vector.tensor_copy(uu[p0:p0 + HD, t], src[p0:p0 + HD, :, p0:p0 + HD]))
                release(key)
            fwd = [MT, *range(REAL)]
            bwd = [*range(REAL - 1, -1, -1), MT]
            for i in range(TILES - 1):
                for d, order in ((0, fwd), (1, bwd)):
                    a, b_ = order[i], order[i + 1]
                    for p0 in (0, HD):
                        ps = slice(p0, p0 + HD)
                        if i == 0:
                            ins = nc.vector.tensor_copy(state[ps, d, b_, ps], uu[ps, a, d, :])
                        else:
                            tot = seg[ps, d, SEG_AT[7] + a:SEG_AT[7] + a + 1]
                            ins = stt(state[ps, d, b_, ps], state[ps, d, a, ps], tot, uu[ps, a, d, :],
                                      ALU.mult, ALU.add)
                        if d and p0:
                            then(ins)
            dve.sem_inc(state_ready, 1)
            for t in range(q_tiles(l)):
                key = ("o", l, g, t)
                m = rows(t)
                dve.wait_ge(rstd_ready, RSTD[l, g, t])
                s = y_slot(l, g, t)
                for hh in range(2):
                    hs = slice(hh * HD, (hh + 1) * HD)
                    ins = stt(y_stage[0:m, s, hs], psum[0:m, bank(key), hs], rstd[0:m, t, hh:hh + 1],
                              g_c[0:m, t, hs], ALU.mult, ALU.mult)
                ins.then_inc(released[bank(key)], 1)

        def extend_segments(lev, half):
            h = HALF[lev]
            a, e = span(half, h)
            n = (e - a) // (2 * h)
            at = SEG_AT[lev - 1] + a // h
            tot = [view(seg, 0, P, at + side, [[SEG_ALL, 2], [2, n], [0, h]]) for side in (0, 1)]
            left = view(qk, 0, P, KF_ * TOK + a, [[(QB_ - KF_) * TOK, 2], [2 * h, n], [1, h]])
            right = view(qk, 0, P, QF_ * TOK + a + h, [[(KB_ - QF_) * TOK, 2], [2 * h, n], [1, h]])
            tt(left, left, tot[1], ALU.mult)
            tt(right, right, tot[0], ALU.mult)
            then(tt(view(seg, 0, P, SEG_AT[lev] + a // (2 * h), [[SEG_ALL, 2], [1, n]]),
                    view(seg, 0, P, at, [[SEG_ALL, 2], [2, n]]),
                    view(seg, 0, P, at + 1, [[SEG_ALL, 2], [2, n]]), ALU.mult))

        def rope(l, g, x, t, nat, dup, n, tmp):
            wait_read(dve, ("unit", l, g, x, t))
            if ROPE[l, g, x, t] > 1:
                dve.wait_ge(roped, ROPE[l, g, x, t] - 1)
            base = (t % 2) * 256
            cs = view(cos_sb, 0, P, t * HD, [[0, n], [1, HD]])
            tt(view(tmp, 0, P, 0, [[HD, n], [1, HD]]), view(nat, 0, P, base, [[HD, n], [1, HD]]), cs, ALU.mult)
            for dst, src in ((0, HD // 2), (HD // 2, 0)):
                ins = tt(view(tmp, 0, P, 256 + dst, [[HD, n], [1, HD // 2]]),
                         view(nat, 0, P, base + src, [[HD, n], [1, HD // 2]]),
                         view(sin_sb, 0, P, t * HD + dst, [[0, n], [1, HD // 2]]), ALU.mult)
            then(ins)
            if t >= 2:
                wait_filled(dve, ({"q": "qT", "kv": "kT", "qk": "qkT"}[x], l, g, t - 2))
            elif x == "kv":
                wait_filled(dve, ("qT", l, g, units(l, g, "q")[-1]))
            tt(dup[:, t % 2, 0:n], view(tmp, 0, P, 0, [[HD, n], [0, 2], [1, HD]]),
               view(tmp, 0, P, 256, [[HD, n], [0, 2], [1, HD]]), ALU.add).then_inc(roped, 1)

        def heads(l, g, x, key_of, nat, dup, n, tmp, *parts):
            for t in [*units(l, g, x), None]:
                if t is not None:
                    rope(l, g, x, t, nat, dup, n, tmp)
                if t != 0:
                    u = units(l, g, x)[-1] if t is None else t - 1
                    qk_lo_of(l, g, x, u, (key_of, l, g, u), *parts)

        def qk_lo_of(l, g, x, t, key, qkT, klT, nq, k0, nk):
            dve.wait_ge(qk_hi, QK_HI[l, g, x, t])
            m = rows(t)
            src = psum[:, bank(key), :].rearrange("p (s c) -> p s c", s=4)
            if nq:
                dst = qkT[HD:P, 0:nq, cols(t)]
                ins = tt(dst, src[HD:P, 0:nq, 0:m], dst.bitcast(F32), ALU.subtract)
            if nk:
                ins = tt(klT[:, 0:nk, cols(t)], src[:, nq:nq + nk, 0:m], qkT[:, k0:k0 + nk, cols(t)].bitcast(F32),
                         ALU.subtract)
            ins.then_inc(released[bank(key)], 1)

        def gate(l, g, t, gn, ge, w):
            then(ts(ge, ge, 1.0, None, ALU.add))
            then(nc.vector.reciprocal(ge, ge))
            ins = tt(gn, gn, ge, ALU.mult)
            if w is not None:
                then(ins)
                ins = tt(gn, gn, w, ALU.mult)
            ins.then_inc(gate_ready, 1)

        def group_a(l):
            g = "A"
            heads(l, g, "q", "qT", n_a, twice_a, 4, ra, qkT_a, None, 4, 0, 0)
            heads(l, g, "kv", "kT", n_a, twice_a, 2, ra, qkT_a, klT_a, 0, 4, 2)
            for t in units(l, g, "g"):
                wait_read(dve, ("unit", l, g, "g", t))
                gate(l, g, t, g_a[:, t, :], ge_a[:], None)

            def mask(t, h):
                if t >= q_tiles(l):
                    return
                m, i = rows(t), t % 2
                w = window(t)[1] * P + META
                key = ("s", l, g, t, h)
                wait_filled(dve, key)
                if t >= 2:
                    wait_filled(dve, ("pT", l, g, t - 2, h))
                then(nc.vector.tensor_tensor_reduce(s_a[0:m, i, h, 0:w], psum[0:m, bank(key), 0:w],
                                                    band_sb[0:m, band_columns(t)], 1.0, NEG, ALU.add, ALU.max,
                                                    row_max[0:m, i, h:h + 1]))
                release(key)
                then(ts(neg_max[0:m, i, h:h + 1], row_max[0:m, i, h:h + 1], SCALE, sink_sb[0:m, l, h:h + 1],
                        ALU.mult, ALU.max))
                ts(neg_max[0:m, i, h:h + 1], neg_max[0:m, i, h:h + 1], -1.0, None, ALU.mult).then_inc(a_masked, 1)

            for h in range(4):
                mask(0, h)
            for t in range(q_tiles(l)):
                m, i = rows(t), t % 2
                for h in range(4):
                    mask(t + 1, h)
                dve.wait_ge(a_sinks, A_HEAD[l, t, 3])
                then(tt(inv_sum[0:m, i, :], row_sum[0:m, i, :], sink_exp[0:m, i, :], ALU.add))
                then(nc.vector.reciprocal(inv_sum[0:m, i, :], inv_sum[0:m, i, :]))
                key = ("o", l, g, t)
                wait_filled(dve, key)
                s = y_slot(l, g, t)
                for h in range(4):
                    v0 = h * P + (h // 2) * HD
                    ins = stt(y_stage[0:m, s, h * HD:(h + 1) * HD], psum[0:m, bank(key), v0:v0 + HD],
                              inv_sum[0:m, i, h:h + 1], g_a[0:m, t, h * HD:(h + 1) * HD], ALU.mult, ALU.mult)
                ins.then_inc(released[bank(key)], 1)

        def group_b(l, g):
            hb = int(g[1])
            for c in range(2):
                for j in range(2):
                    nc.vector.memset(p_b[:, j, c, TOK:], 0.0)
            heads(l, g, "qk", "qkT", n_b, twice_b, 4, rb, qkT_b, klT_b, 2, 2, 2)
            for t in units(l, g, "vg"):
                wait_read(dve, ("unit", l, g, "vg", t))
                gate(l, g, t, g_b[:, t, :], ge_b[:], norm_w[:, hb * P:(hb + 1) * P])
            for c in range(2):
                then(nc.vector.memset(psum[:, 4 + 3 * c, TOK - 2 * S_W:S_W], NEG))
            dve.sem_inc(b_pad, 1)

            def finish(t):
                m, i = rows(t), t % 2
                dve.wait_ge(rstd_ready, RSTD[l, g, t])
                then(stt(coef[0:m, i, 1:2], rstd[0:m, t, 0:1], 1.0 - LAM_INIT[l], inv_sum[0:m, i, 0:1],
                         ALU.mult, ALU.mult))
                s = y_slot(l, g, t)
                stt(y_stage[0:m, s, 0:P], o_b[0:m, i, :], coef[0:m, i, 1:2], g_b[0:m, t, :],
                    ALU.mult, ALU.mult).then_inc(b_y, 1)

            def maximum(t, c):
                if t >= q_tiles(l):
                    return
                m, i = rows(t), t % 2
                key = ("s", l, g, t, c)
                b = bank(key)
                wait_filled(dve, key)
                if t >= 2 and c == 0:
                    wait_filled(dve, ("aT", l, g, t - 2, 2))
                then(nc.vector.tensor_reduce(row_max[0:m, i, c:c + 1], psum[0:m, b:b + 3, 0:S_W], AX.XY, ALU.max))
                ts(neg_max[0:m, i, c:c + 1], row_max[0:m, i, c:c + 1], -SCALE, None, ALU.mult).then_inc(b_max, 1)

            def combine(t):
                m, i = rows(t), t % 2
                for c in range(2):
                    wait_read(dve, ("s", l, g, t, c))
                then(tt(row_sum[0:m, i, 0:4:2], row_sum[0:m, i, 0:4:2], row_sum[0:m, i, 1:4:2], ALU.add))
                then(nc.vector.reciprocal(inv_sum[0:m, i, 0:2], row_sum[0:m, i, 0:4:2]))
                then(stt(coef[0:m, i, 0:1], inv_sum[0:m, i, 1:2], neg_lam[0:m, l:l + 1], row_sum[0:m, i, 0:1],
                         ALU.mult, ALU.mult))
                then(stt(fscale[0:m, i, :], inv_sum[0:m, i, 0:1], 1.0 / P, inv_sum[0:m, i, 0:1],
                         ALU.mult, ALU.mult))
                stt(p_b[0:m, i, 0, 0:TOK], p_b[0:m, i, 1, 0:TOK], coef[0:m, i, 0:1], p_b[0:m, i, 0, 0:TOK],
                    ALU.mult, ALU.add).then_inc(b_comb, 1)

            maximum(0, 0)
            maximum(0, 1)
            for t in range(q_tiles(l)):
                maximum(t + 1, 0)
                if g == GROUPS[-1] and t > Y_LAG:
                    lo_of_rows("y", l, t - 1 - Y_LAG)
                combine(t)
                maximum(t + 1, 1)
                if t:
                    finish(t - 1)
            finish(q_tiles(l) - 1)

        for l in range(DEPTH):
            for g in GROUPS:
                phase_start(dve, (l, g))
                if g[0] == "C":
                    group_c(l, g)
                elif g == "A":
                    group_a(l)
                else:
                    group_b(l, g)
            phase_start(dve, (l, "O"))
            for t in range(q_tiles(l) - 1 - Y_LAG, q_tiles(l)):
                lo_of_rows("y", l, t)

            for c in range(DM // CW):
                for t in units(l, "O", c):
                    key = ("unit", l, "O", c, t)
                    wait_filled(dve, key)
                    if c == 0:
                        dve.wait_ge(rows_in[t], 16 * (l + 2))
                    elif c == DM // CW - 1 and t == 0:
                        dve.wait_ge(ln_in, 32 * (l + 2))
                    part = hbuf[0:rows(t), t, c * CW:(c + 1) * CW]
                    then(stt(part, part, ALPHA, psum[0:rows(t), bank(key), 0:CW], ALU.mult, ALU.add))
                    release(key)
                    if c == DM // CW - 1:
                        ln_stats(l, t)
                        if t:
                            ln_apply(l, t - 1)
                        if t >= H_LAG and l < DEPTH - 1:
                            lo_of_rows("h", l + 1, t - H_LAG)
            ln_apply(l, q_tiles(l) - 1)
            if l < DEPTH - 1:
                for t in range(TILES - H_LAG, TILES):
                    lo_of_rows("h", l + 1, t)


N_CONSTS = 4 + 2 + DEPTH * 2
_INS = ["x", "meta", "emb_ln_g", "emb_ln_b", "w_in", "w_out", "a_sink", "b_lam", "b_subln_w", "c_lb_logits",
        "c_norm_w", "ln_g", "ln_b"]


def kernel(**inputs):
    import concourse.bacc as bacc
    from concourse.bass_utils import run_bass_kernel_spmd

    nc = bacc.Bacc("TRN2", target_bir_lowering=False, num_devices=1, dynamic_dma_scratch_size=1024)
    arrays, args = {}, []
    for name, a in [(n, inputs[n]) for n in _INS] + list(CONSTS.items()):
        a = np.ascontiguousarray(a)
        arrays[f"in_{name}"] = a
        args.append(nc.dram_tensor(f"in_{name}", a.shape, mybir.dt.from_np(a.dtype), kind="ExternalInput").ap())
    args.append(nc.dram_tensor("out", (1, REAL * P, DM), F32, kind="ExternalOutput").ap())
    build(nc, *args)
    r = run_bass_kernel_spmd(nc, [arrays], core_ids=[0])
    return r.results[0]["out"]
```

```python
from contextlib import ExitStack

import numpy as np

import concourse.bass as bass
from concourse import mybir

ALU = mybir.AluOpType
ACT = mybir.ActivationFunctionType
F32 = mybir.dt.float32
F32R = mybir.dt.float32r
I32 = mybir.dt.int32
AX = mybir.AxisListType

P = 128
DM = 1024
DEPTH = 2
META = 16
HD = 64
REAL = 8
TILES = REAL + 1
MT = REAL
TOK = REAL * P + META
KT = DM // P
CW = 256
SCALE = HD ** -0.5
ALPHA = (2 * DEPTH) ** 0.25
LN_EPS, RMS_EPS, F_MIN, E_MAX, NEG = 1e-5, 1e-6, 1e-30, 1e37, -1e30
LAM_INIT = [0.8 - 0.6 * float(np.exp(-0.3 * l)) for l in range(DEPTH)]

QA, KA, VA, GA, QB, KB, VB, GB, QC, IC, ZF, ZB, GC = (
    0, 256, 384, 512, 768, 1280, 1792, 2304, 2816, 3072, 3328, 3584, 3840)

LEVELS = 8
HALF = [0] + [2 ** (i - 1) for i in range(1, LEVELS)]
SPAN = [(0, 4 * P), (4 * P, TOK)]


def span(half, h):
    a, b = SPAN[half]
    return (a, b) if h <= META // 2 else (a, min(b, REAL * P))


SEG_N = [TOK if h <= META else REAL * P for h in (1, 2, 4, 8, 16, 32, 64, 128)]
SEG_LEN = [n // h for n, h in zip(SEG_N, (1, 2, 4, 8, 16, 32, 64, 128))]
SEG_AT = [sum(SEG_LEN[:i]) for i in range(8)]
SEG_ALL = sum(SEG_LEN)

GROUPS = ["C0", "C1", "A", "B0", "B1", "B2", "B3"]
Y_COL = {"A": 0, "B0": 256, "B1": 384, "B2": 512, "B3": 640, "C0": 768, "C1": 896}
Y_WIDTH = {g: 256 if g == "A" else 128 for g in GROUPS}
Y_SLOTS = 4
Y_LAG = 3
I_LAG = 2
H_LAG = 4


def rows(t):
    return META if t == MT else P


def q_tiles(l):
    return TILES if l < DEPTH - 1 else REAL


def cols(t):
    return slice(t * P, t * P + rows(t))


def numbered(keys):
    return {k: i + 1 for i, k in enumerate(keys)}


def chunks_of(group):
    if group[0] == "C":
        o = P * int(group[1])
        return [("qf", "T", [(QC + o, P), (ZF + o, P)]), ("b", "T", [(ZB + o, P)]),
                ("vg", "N", [(IC + o, P), (GC + o, P)])]
    if group == "A":
        return [("q", "N", [(QA, CW)]), ("kv", "N", [(KA, CW)]), ("g", "N", [(GA, CW)])]
    if group[0] == "B":
        o = P * int(group[1])
        return [("qk", "N", [(QB + o, P), (KB + o, P)]), ("vg", "N", [(VB + o, P), (GB + o, P)])]
    return [(c, "N", [(c * CW, CW)]) for c in range(DM // CW)]


CHUNKS = [(l, g, *c) for l in range(DEPTH) for g in [*GROUPS, "O"] for c in chunks_of(g)]
CHUNK = {(l, g, name): i for i, (l, g, name, _, _) in enumerate(CHUNKS)}
CHUNK_DMAS = np.cumsum([len(c[4]) for c in CHUNKS]).tolist()
T_PIECES = [(0, 348), (348, 346), (694, 346)]
S_PIECES = [(0, 348), (348, 348), (696, 344)]
S_W = 348
PHASES = ["I"] + [(l, g) for l in range(DEPTH) for g in [*GROUPS, "O"]]
PHASE = {k: i for i, k in enumerate(PHASES)}


def window(t):
    if t == MT:
        return 0, 1
    return max(t - 1, 0), min(t + 1, REAL - 1) - max(t - 1, 0) + 1


def units(l, g, name):
    if g[0] == "C" and name != "vg":
        return [(f, j) for f in range(2 if name == "qf" else 1) for j in range(3)]
    if g == "O" or (g == "A" and name in ("q", "g")):
        return list(range(q_tiles(l)))
    return list(range(TILES))


def level_fills(half, lev):
    a = 4 * half
    out = [(a, 2), (a + 2, 2)]
    if half and HALF[lev] <= META // 2:
        out.append((MT, 1))
    return out


def level_steps():
    steps = [(lev, half) for lev in range(LEVELS) for half in range(2)]
    return [(lev, half, i if i < TILES else None) for i, (lev, half) in enumerate(steps)]


def b_passes(l):
    heads = [None] + [g for g in GROUPS if g[0] == "B"] + [None]
    return list(zip(heads, heads[1:]))


def b_steps(l, g, nx):
    made = [(c, x) for c in ("qk", "vg") for x in units(l, nx, c)] if nx else []
    made = [made[i:i + 2] for i in range(0, len(made), 2)]
    n = q_tiles(l) if g else 0
    steps = max(n, len(made) + 1 if made else 0)
    made = made + [[]] * (steps - len(made))
    return [(t if t < n else None, made[t], made[t - 1] if t else []) for t in range(steps)]


def b_step(l, g, t, k):
    steps = [(h, u) for h in GROUPS if h[0] == "B" for u in range(q_tiles(l))]
    i = steps.index((g, t)) + k
    return steps[i] if 0 <= i < len(steps) else None


def heads_of(made, j):
    return made[j][1] if j < len(made) and made[j][0] == "qk" else None


def bank_plan():
    used, plan = [0] * 8, {}

    def add(key, bank):
        plan[key] = (bank, used[bank])
        used[bank] += 1

    def transposed(what, l, tiles, beside_scores=False):
        for t in tiles:
            for j in range(2):
                add((what, l, t, j), j if beside_scores else 2 + 2 * (t % 2) + j)

    transposed("h", 0, range(TILES))
    for l in range(DEPTH):
        u = 0
        for g in GROUPS:
            for name, kind, _ in chunks_of(g) if g[0] != "B" else []:
                for x in units(l, g, name) if (g, name) != ("A", "g") else []:
                    add(("unit", l, g, name, x), u % 2)
                    u += 1
            if g[0] == "C":
                n = 0
                for lev in range(LEVELS):
                    for half in range(2):
                        for first, _ in level_fills(half, lev):
                            add(("level", l, g, lev, first), 2 + n % 6)
                            n += 1
                for i, t in enumerate([MT, *range(REAL)]):
                    add(("knat", l, g, t), 2 + i % 2)
                    add(("u", l, g, t), 4 + i % 2)
                for t in range(q_tiles(l)):
                    add(("o", l, g, t), (6, 7, 2, 3)[t % 4])
            if g == "A":
                for t in units(l, g, "q"):
                    add(("qT", l, g, t), 2 + 2 * (t % 2))
                for t in units(l, g, "kv"):
                    add(("kT", l, g, t), 3 + 2 * (t % 2))
                for t in range(q_tiles(l)):
                    for h in range(4):
                        add(("s", l, g, t, h), 2 + h)
                        add(("pT", l, g, t, h), 6 + h % 2)
                    add(("unit", l, g, "g", t), t % 2)
                    add(("o", l, g, t), t % 2)
        for g, nx in b_passes(l):
            if g == "B0":
                for t, c in ((0, 0), (0, 1), (1, 0)):
                    add(("s", l, g, t, c), 2 + 3 * c)
            for t, made, before in b_steps(l, g, nx):
                if t is not None and b_step(l, g, t, 1):
                    add(("s", l, *b_step(l, g, t, 1), 1), 5)
                for j in range(2):
                    if t is not None:
                        add(("aT", l, g, t, j), 1 if j == 0 and not nx else 0)
                    if j < len(made):
                        add(("unit", l, nx, *made[j]), 1 if g else (1, 3)[j])
                    if heads_of(before, j) is not None:
                        add(("qkT", l, nx, heads_of(before, j)), 0)
                if t is not None:
                    add(("aT", l, g, t, 2), 0 if nx else 1)
                    if not nx and t >= Y_LAG:
                        transposed("y", l, [t - Y_LAG], True)
                    if b_step(l, g, t, 2):
                        add(("s", l, *b_step(l, g, t, 2), 0), 2)
                    add(("o", l, g, t), 0)
        transposed("y", l, range(q_tiles(l) - Y_LAG, q_tiles(l)))
        for c in range(DM // CW):
            for t in units(l, "O", c):
                add(("unit", l, "O", c, t), t % 2)
        if l < DEPTH - 1:
            transposed("h", l + 1, range(TILES))
    return plan


BANK = bank_plan()

HT = [("h", 0, TILES)] + [x for l in range(DEPTH) for x in
                          [("y", l, q_tiles(l))] + ([("h", l + 1, TILES)] if l < DEPTH - 1 else [])]
T_SPLIT = numbered([(w, l, t, j) for w, l, n in HT for t in range(n) for j in range(2)])
NORM = numbered([("I", t) for t in range(TILES)] + [(l, t) for l in range(DEPTH) for t in range(q_tiles(l))])
HEADS_IN = [(l, g, x, t) for l in range(DEPTH) for g in GROUPS if g[0] != "C"
            for x in (("q", "kv") if g == "A" else ("qk",)) for t in units(l, g, x)]
ROPE = numbered(HEADS_IN)
QK_HI = numbered(HEADS_IN)
Y_OUT = numbered([(l, g, t) for l in range(DEPTH) for g in GROUPS for t in range(q_tiles(l))])
LEVEL = numbered([(l, g, lev, half) for l in range(DEPTH) for g in GROUPS if g[0] == "C"
                  for lev in range(LEVELS) for half in range(2)])
SEG = numbered([(l, g, lev, half) for l in range(DEPTH) for g in GROUPS if g[0] == "C"
                for lev in range(LEVELS + 1) for half in range(2)])
C_PAIR = numbered([(l, g) for l in range(DEPTH) for g in GROUPS if g[0] == "C"])
RSTD = numbered([("I", t) for t in range(TILES)] + [x for l in range(DEPTH) for x in
                [(l, g, t) for g in GROUPS if g != "A" for t in range(q_tiles(l))]
                + [(l, t) for t in range(q_tiles(l))]])
A_HEAD = numbered([(l, t, h) for l in range(DEPTH) for t in range(q_tiles(l)) for h in range(4)])
B_COMP = numbered([(l, g, t, c) for l in range(DEPTH) for g in GROUPS if g[0] == "B"
                   for t in range(q_tiles(l)) for c in range(2)])
B_STEP = numbered([(l, g, t) for l in range(DEPTH) for g in GROUPS if g[0] == "B" for t in range(q_tiles(l))])
A_PV = numbered([(l, t, h) for l in range(DEPTH) for t in range(q_tiles(l)) for h in range(3)])
GATE = numbered([(l, g, t) for l in range(DEPTH) for g in GROUPS
                 for t in (units(l, g, "vg") if g[0] == "B" else range(q_tiles(l)))])


def shape_constants():
    pos = np.zeros((P, TILES), np.float32)
    for t in range(REAL):
        pos[:, t] = META + t * P + np.arange(P)
    pos[:META, MT] = np.arange(META)
    inv = np.float32(10000.0) ** (-np.arange(0, HD, 2, dtype=np.float32) / np.float32(HD))
    ang = pos[:, :, None] * inv[None, None, :].astype(np.float32)
    cos, sin = np.cos(ang).astype(np.float32), np.sin(ang).astype(np.float32)
    s, t = np.arange(P)[:, None], np.arange(P)[None, :]
    pair = np.zeros((P, LEVELS, P), np.float32)
    pair[:, 0] = s == t
    for i in range(1, LEVELS):
        h = HALF[i]
        pair[:, i] = (s // (2 * h) == t // (2 * h)) & (s // h != t // h)
    i, j = np.arange(P)[:, None], np.arange(P)[None, :]
    prev = np.where(j >= i, 0, NEG).astype(np.float32)
    nxt = np.where(j <= i, 0, NEG).astype(np.float32)
    zero = np.zeros((P, P), np.float32)
    zm = np.zeros((P, META), np.float32)
    meta_q = np.where(j <= P - META + i, 0, NEG).astype(np.float32)
    band = np.concatenate([prev, zero, nxt, zm, prev, zero, zm, meta_q, zm], axis=1)
    return {"eye": np.eye(P, dtype=np.float32), "rope_cos": np.concatenate([cos, cos], axis=2),
            "rope_sin": np.concatenate([-sin, sin], axis=2), "pair_mask": pair, "band_mask": band}


BAND_W = 400 + 272 + 144
CONSTS = shape_constants()


def band_columns(t):
    if t == MT:
        return slice(672, 816)
    if t == REAL - 1:
        return slice(400, 672)
    return slice(P, 400) if t == 0 else slice(0, 400)


def build(nc, x, meta, emb_ln_g, emb_ln_b, w_in, w_out, a_sink, b_lam, b_subln_w, c_lb_logits,
          c_norm_w, ln_g, ln_b, eye, rope_cos, rope_sin, pair_mask, band_mask, out):
    top = ExitStack()

    def sb(stack, name, shape, dt=F32):
        return stack.enter_context(nc.sbuf_tensor(name, shape, dt))

    def sem(name):
        return top.enter_context(nc.semaphore(name))

    h_dram = nc.dram_tensor("h_dram", (TILES, P, DM), F32, kind="Internal").ap()
    y_dram = nc.dram_tensor("y_dram", (TILES, P, DM), F32, kind="Internal").ap()

    hT_hi = sb(top, "hT_hi", [P, KT * TOK + P - META], F32R)
    hT_lo = sb(top, "hT_lo", [P, KT * TOK + P - META], F32R)
    w_raw = sb(top, "w_raw", [P, KT, CW])
    w_hi = sb(top, "w_hi", [P, 2, KT, CW], F32R)
    w_lo = sb(top, "w_lo", [P, 2, KT, CW], F32R)
    ident = sb(top, "ident", [P, P])
    cos_sb = sb(top, "cos_sb", [P, TILES, HD])
    sin_sb = sb(top, "sin_sb", [P, TILES, HD])
    pair_sb = sb(top, "pair_sb", [P, LEVELS, P])
    band_sb = sb(top, "band_sb", [P, BAND_W])
    norm_w = sb(top, "norm_w", [P, 768])
    y_stage = sb(top, "y_stage", [P, Y_SLOTS, 256])
    sink_sb = sb(top, "sink_sb", [P, DEPTH, 4])
    lam_dot = sb(top, "lam_dot", [P, DEPTH, 2])
    lam_exp = sb(top, "lam_exp", [P, DEPTH, 2])
    neg_lam = sb(top, "neg_lam", [P, DEPTH])
    lbl = sb(top, "lbl", [P, DEPTH, 2])
    lb = sb(top, "lb", [P, DEPTH, 2])
    one_lb = sb(top, "one_lb", [P, DEPTH, 2])
    lb_max = sb(top, "lb_max", [P, 2])
    lb_sum = sb(top, "lb_sum", [P, 2])
    stats = sb(top, "stats", [P, TILES, 2, 6])
    mean_var = sb(top, "mean_var", [P, TILES, 2])
    rstd = sb(top, "rstd", [P, TILES, 2])
    sumsq = sb(top, "sumsq", [P, TILES, 2])
    fscale = sb(top, "fscale", [P, 2, 1])
    row_max = sb(top, "row_max", [P, 2, 4])
    neg_max = sb(top, "neg_max", [P, 2, 4])
    row_sum = sb(top, "row_sum", [P, 2, 4])
    sink_exp = sb(top, "sink_exp", [P, 2, 4])
    inv_sum = sb(top, "inv_sum", [P, 2, 4])
    coef = sb(top, "coef", [P, 2, 2])
    eps_ln = sb(top, "eps_ln", [P, 1])
    eps_rms = sb(top, "eps_rms", [P, 1])

    so = ExitStack()
    hbuf = sb(so, "hbuf", [P, TILES, DM])
    ln_w = sb(so, "ln_w", [P, 2, DM])
    lam_sb = sb(so, "lam_sb", [P, DEPTH, 4, HD])
    lam_tmp = sb(so, "lam_tmp", [P, HD])
    so.close()
    sc = ExitStack()
    KF_, QB_, QF_, KB_ = range(4)
    qk = sb(sc, "qk", [P, 4, TOK])
    q_c = sb(sc, "q_c", [P, TOK])
    seg = sb(sc, "seg", [P, 2, SEG_ALL])
    k_pair = sb(sc, "k_pair", [P, 2, TOK])
    pc = sb(sc, "pc", [P, REAL, 2, P])
    pc_meta = sb(sc, "pc_meta", [META, 2, META])
    v_c = sb(sc, "v_c", [P, TILES, P])
    g_c = sb(sc, "g_c", [P, TILES, P])
    state = sb(sc, "state", [P, 2, TILES, P])
    k_nat = sb(sc, "k_nat", [P, 2, 2, P])
    ge_c = sb(sc, "ge_c", [P, TILES, P])
    sc.close()
    sa = ExitStack()
    n_a = sb(sa, "n_a", [P, 2, 256])
    twice_a = sb(sa, "twice_a", [P, 2, 4, 2, HD])
    v_a = sb(sa, "v_a", [P, TILES, P])
    g_a = sb(sa, "g_a", [P, 2, 256])
    ge_a = sb(sa, "ge_a", [P, 2, 256])
    qkT_a = sb(sa, "qkT_a", [P, 6, TOK], F32R)
    klT_a = sb(sa, "klT_a", [P, 2, TOK], F32R)
    s_a = sb(sa, "s_a", [P, 2, 4, 400])
    pT_a = sb(sa, "pT_a", [P, 2, 4, P])
    ra = sb(sa, "ra", [P, 2, 256])
    sa.close()
    sB = ExitStack()
    n_b = sb(sB, "n_b", [P, 2, 256])
    twice_b = sb(sB, "twice_b", [P, 2, 4, 2, HD])
    p0_b = sb(sB, "p0_b", [P, 2, TILES * P])
    p1_b = sb(sB, "p1_b", [P, TOK])
    aT_b = sb(sB, "aT_b", [P, TILES, P])
    rb = sb(sB, "rb", [P, 2, 256])
    ge_b = sb(sB, "ge_b", [P, 2, P])
    o_b = sb(sB, "o_b", [P, 2, P])
    b_junk = sb(sB, "b_junk", [P, P])
    v_b = sb(sB, "v_b", [P, 2, TILES, P])
    g_b = sb(sB, "g_b", [P, 2, TILES, P])
    klT_b = sb(sB, "klT_b", [P, 2, 2, TOK], F32R)
    qkT_b = sb(sB, "qkT_b", [P, 2, 4, TOK], F32R)
    sB.close()

    y_load = qkT_b[:, 1].bitcast(F32).rearrange("p s t -> p (s t)")[:, 0:2 * DM].rearrange("p (s c) -> p s c", s=2)

    psum = top.enter_context(nc.psum_tensor("psum", [P, 8, 512], F32))

    filled = [sem(f"bank{b}_filled") for b in range(8)]
    released = [sem(f"bank{b}_released") for b in range(8)]
    consts_in = sem("consts_in")
    norm_w_in = sem("norm_w_in")
    w_loaded = sem("w_loaded")
    w_hi_done = sem("w_hi_done")
    w_split = sem("w_split")
    ident_in = sem("ident_in")
    rows_in = [sem(f"rows_in{t}") for t in range(TILES)]
    ln_in = sem("ln_in")
    y_in = [sem(f"y_in{i}") for i in range(2)]
    y_saved = [sem(f"y_saved{i}") for i in range(Y_SLOTS)]
    h_saved = sem("h_saved")
    out_saved = sem("out_saved")
    var_ready = sem("var_ready")
    rstd_ready = sem("rstd_ready")
    scaled = sem("scaled")
    h_ready = sem("h_ready")
    hi_split = sem("hi_split")
    gate_ready = sem("gate_ready")
    seg_ready = sem("seg_ready")
    level_selected = sem("level_selected")
    scores_c_ready = sem("scores_c_ready")
    state_ready = sem("state_ready")
    roped = sem("roped")
    qk_hi = sem("qk_hi")
    a_masked = sem("a_masked")
    a_exp = sem("a_exp")
    a_sinks = sem("a_sinks")
    a_pv = sem("a_pv")
    b_max = sem("b_max")
    b_comb = sem("b_comb")
    b_pad = sem("b_pad")
    b_y = sem("b_y")
    setup_v = sem("setup_v")
    setup_s = sem("setup_s")
    vec = sem("vec")
    sca = sem("sca")

    block = top.enter_context(nc.Block())

    def view(t, p0, np_, off, dims):
        full = t[:]
        width = full.ap[0][0]
        return bass.AP(tensor=full.tensor, offset=p0 * width + off, ap=[[width, np_], *dims])

    def h_rows(h, j, t):
        return h[:, 0:KT * TOK].rearrange("p (k c) -> p k c", k=KT)[:, 4 * j:4 * j + 4, cols(t)]

    def slot_of(g):
        return (int(g[1]) + 1) % 2

    def bank(key):
        return BANK[key][0]

    def wait_free(eng, key):
        b, n = BANK[key]
        if n:
            eng.wait_ge(released[b], n)

    def wait_filled(eng, key):
        b, n = BANK[key]
        eng.wait_ge(filled[b], n + 1)

    def wait_read(eng, key):
        b, n = BANK[key]
        eng.wait_ge(released[b], n + 1)

    def phase_start(eng, key):
        before = PHASES[PHASE[key] - 1]
        if before == "I":
            wait_read(eng, ("h", 0, TILES - 1, 1))
        elif before[1] == "O":
            wait_read(eng, ("h", before[0] + 1, TILES - 1, 1))
        else:
            wait_y(eng, *before, q_tiles(before[0]) - 1)

    def wait_y(eng, l, g, t):
        if g[0] == "B":
            eng.wait_ge(b_y, B_STEP[l, g, t])
        else:
            wait_read(eng, ("o", l, g, t))

    def level_ap(lev, side, p0, np_, a, n):
        h = HALF[lev]
        left, right = (KF_, KB_) if side == "k" else (QB_, QF_)
        return view(qk, p0, np_, left * TOK + a, [[2 * h, n // (2 * h)], [(right - left) * TOK + h, 2], [1, h]])

    def k_sum():
        return state[:, 0].rearrange("p t c -> p (t c)")[:, 0:TOK]

    @block.sync
    def _(sp):
        def load_ln(g_ap, b_ap):
            sp.dma_start(ln_w[:, 0], g_ap.partition_broadcast(P)).then_inc(ln_in, 16)
            sp.dma_start(ln_w[:, 1], b_ap.partition_broadcast(P)).then_inc(ln_in, 16)

        for t in range(REAL):
            sp.dma_start(hbuf[:, t], x[0, t * P:(t + 1) * P, :]).then_inc(rows_in[t], 16)
            if t == 0:
                sp.dma_start(ident[:], eye).then_inc(ident_in, 16)
                load_ln(emb_ln_g, emb_ln_b)
        sp.dma_start(hbuf[0:META, MT], meta).then_inc(rows_in[MT], 16)

        def load_chunk(i):
            l, g, name, kind, parts = CHUNKS[i]
            if i:
                sp.wait_ge(w_split, i)
            w = (w_out if g == "O" else w_in)[l].rearrange("(k p) n -> p k n", p=P)
            at = 0
            for c0, n in parts:
                sp.dma_start(w_raw[:, :, at:at + n], w[:, :, c0:c0 + n]).then_inc(w_loaded, 16)
                at += n

        def save_h(l, n):
            for t in range(n):
                sp.wait_ge(h_ready, NORM["I" if l < 0 else l, t])
                if l == DEPTH - 1:
                    sp.dma_start(out[0, t * P:(t + 1) * P, :], hbuf[:, t]).then_inc(out_saved, 16)
                else:
                    sp.dma_start(h_dram[t, 0:rows(t)], hbuf[0:rows(t), t]).then_inc(h_saved, 16)

        load_chunk(0)
        for dst, src in ((cos_sb[:], rope_cos), (sin_sb[:], rope_sin),
                         (pair_sb[:], pair_mask), (band_sb[:], band_mask)):
            sp.dma_start(dst, src).then_inc(consts_in, 16)
        sp.dma_start(sink_sb[:], a_sink.partition_broadcast(P)).then_inc(consts_in, 16)
        sp.dma_start(lam_sb[:], b_lam.partition_broadcast(P)).then_inc(consts_in, 16)
        for l in range(DEPTH):
            for p in range(2):
                sp.dma_start(lbl[:, l, p:p + 1],
                             c_lb_logits[l, p * P:(p + 1) * P].rearrange("(p o) -> p o", o=1)).then_inc(consts_in, 16)

        load_chunk(1)
        save_h(-1, TILES)
        n_chunk = 2
        for l in range(DEPTH):
            if l:
                phase_start(sp, (l - 1, "O"))
            sp.dma_start(norm_w[:, 0:512], b_subln_w[l].partition_broadcast(P)).then_inc(norm_w_in, 16)
            sp.dma_start(norm_w[:, 512:768], c_norm_w[l].partition_broadcast(P)).then_inc(norm_w_in, 16)
            for g in GROUPS:
                while n_chunk < len(CHUNKS) and n_chunk <= CHUNK[l, g, chunks_of(g)[-1][0]] + (2 if g == "A" else 3):
                    load_chunk(n_chunk)
                    n_chunk += 1
                for t in range(q_tiles(l)):
                    n = Y_OUT[l, g, t]
                    wait_y(sp, l, g, t)
                    c = Y_COL[g]
                    sp.dma_start(y_dram[t, 0:rows(t), c:c + Y_WIDTH[g]],
                                 y_stage[0:rows(t), n % Y_SLOTS, 0:Y_WIDTH[g]]).then_inc(y_saved[n % Y_SLOTS], 16)
                    if g == GROUPS[-1]:
                        for s in range(Y_SLOTS):
                            sp.wait_ge(y_saved[s], 16 * sum(1 for k in range(1, n + 1) if k % Y_SLOTS == s))
                        if t >= 2:
                            wait_filled(sp, ("y", l, t - 2, 1))
                        sp.dma_start(y_load[0:rows(t), t % 2], y_dram[t, 0:rows(t)]).then_inc(y_in[t % 2], 16)
            phase_start(sp, (l, "O"))
            for t in range(q_tiles(l)):
                sp.dma_start(hbuf[0:rows(t), t], h_dram[t, 0:rows(t)]).then_inc(rows_in[t], 16)
            load_ln(ln_g[l], ln_b[l])
            while n_chunk < len(CHUNKS) and n_chunk <= CHUNK[l, "O", 3] + 2:
                load_chunk(n_chunk)
                n_chunk += 1
            save_h(l, q_tiles(l))
        sp.wait_ge(out_saved, 16 * REAL)

    @block.gpsimd
    def _(pool):
        def split_chunk(i):
            l, g, name, kind, parts = CHUNKS[i]
            n = sum(p[1] for p in parts)
            pool.wait_ge(w_loaded, 16 * CHUNK_DMAS[i])
            if i >= 2:
                before = CHUNKS[i - 2][:3]
                wait_filled(pool, ("unit", *before, units(*before)[-1]))
            pool.tensor_copy(w_hi[:, i % 2, :, 0:n], w_raw[:, :, 0:n]).then_inc(w_hi_done, 1)
            pool.wait_ge(w_hi_done, i + 1)
            pool.tensor_tensor(w_lo[:, i % 2, :, 0:n], w_raw[:, :, 0:n],
                               w_hi[:, i % 2, :, 0:n].bitcast(F32), ALU.subtract).then_inc(w_split, 1)

        def add_ln_bias(l, tiles):
            for t in tiles:
                pool.wait_ge(scaled, NORM[l, t])
                row = hbuf[0:rows(t), t, :]
                pool.tensor_tensor(row, row, ln_w[0:rows(t), 1, :], ALU.add).then_inc(h_ready, 1)

        add_ln_bias("I", range(4))
        split_chunk(0)
        add_ln_bias("I", range(4, TILES))
        for i, (l, g, name, _, _) in enumerate(CHUNKS):
            if i + 1 < len(CHUNKS):
                split_chunk(i + 1)
            if g == "O" and name == DM // CW - 1:
                add_ln_bias(l, range(q_tiles(l)))

    @block.tensor
    def _(pe):
        def split_product(out_ap, lhs, rhs, ks=range(KT)):
            for k in ks:
                for a, b in ((0, 0), (1, 0), (0, 1)):
                    last = nc.tensor.matmul(out_ap, lhs[a](k), rhs[b](k), start=k == 0 and a + b == 0,
                                            stop=k == KT - 1 and b == 1)
            return last

        def half_unit(l, g, name, x, h):
            key = ("unit", l, g, name, x)
            i, b = CHUNK[l, g, name], bank(key)
            if h == 0:
                pe.wait_ge(w_split, i + 1)
                wait_free(pe, key)
            last = split_product(psum[:, b, 0:CW],
                                 [lambda k, h=h: h[:, k * TOK + x * P:k * TOK + (x + 1) * P] for h in (hT_hi, hT_lo)],
                                 [lambda k, w=w: w[:, i % 2, k, 0:CW] for w in (w_hi, w_lo)],
                                 range(h * KT // 2, (h + 1) * KT // 2))
            if h == 1:
                last.then_inc(filled[b], 1)

        def project(l, g, name, kind, only=None):
            heads = g != "O" and name in HEAD_T
            last_chunk = g == "O" and name == DM // CW - 1 and l < DEPTH - 1
            if heads and g == "A":
                phase_start(pe, (l, g))
            i = CHUNK[l, g, name]
            pe.wait_ge(w_split, i + 1)
            for x in units(l, g, name) if only is None else [only]:
                key = ("unit", l, g, name, x)
                b = bank(key)
                if g == "O" and name == 0:
                    for j in range(2):
                        wait_read(pe, ("y", l, x, j))
                wait_free(pe, key)
                if kind == "T":
                    f, (a, n) = x[0], T_PIECES[x[1]]
                    last = split_product(
                        psum[:, b, 0:n],
                        [lambda k, w=w: w[:, i % 2, k, f * P:(f + 1) * P] for w in (w_hi, w_lo)],
                        [lambda k, h=h: h[:, k * TOK + a:k * TOK + a + n] for h in (hT_hi, hT_lo)])
                else:
                    last = split_product(
                        psum[:, b, 0:CW],
                        [lambda k, h=h: h[:, k * TOK + x * P:k * TOK + (x + 1) * P] for h in (hT_hi, hT_lo)],
                        [lambda k, w=w: w[:, i % 2, k, 0:CW] for w in (w_hi, w_lo)])
                last.then_inc(filled[b], 1)
                if heads and x:
                    transposes_of(l, g, name, x - 1)
                if last_chunk and x >= H_LAG - 1:
                    transpose_h(l, x - H_LAG + 1)
            if heads:
                transposes_of(l, g, name, units(l, g, name)[-1])
            if last_chunk:
                for t in range(TILES - H_LAG + 1, TILES):
                    transpose_h(l, t)

        def transpose_h(l, t):
            pe.wait_ge(h_ready, NORM[l, t])
            transpose_rows("h", l + 1, t, hbuf[:, t])

        def transpose_y(l, t):
            pe.wait_ge(y_in[t % 2], 16 * (sum((q_tiles(m) + 1 - t % 2) // 2 for m in range(l)) + t // 2 + 1))
            transpose_rows("y", l, t, y_load[:, t % 2])

        def transpose_rows(what, l, t, src):
            for j in range(2):
                key = (what, l, t, j)
                b = bank(key)
                wait_free(pe, key)
                for k in range(4):
                    c = (4 * j + k) * P
                    last = nc.tensor.transpose(psum[:, b, k * P:k * P + rows(t)], src[0:rows(t), c:c + P],
                                               ident[0:rows(t), 0:rows(t)])
                last.then_inc(filled[b], 1)

        def mix_c(l, g):
            phase_start(pe, (l, g))
            for lev, half, vg_tile in level_steps():
                h = HALF[lev]
                pe.wait_ge(level_selected, LEVEL[l, g, lev, half])
                pe.wait_ge(seg_ready, SEG[l, g, lev, half])
                for first, n in level_fills(half, lev):
                    key = ("level", l, g, lev, first)
                    b = bank(key)
                    wait_free(pe, key)
                    for j in range(n):
                        a, m = (first + j) * P, rows(first)
                        q_ap = q_c[:, a:a + m] if lev == 0 else level_ap(lev, "q", 0, P, a, m)
                        for hh in range(2):
                            at = (2 * j + hh) * m
                            o_ap = psum[0:m, b, at:at + m]
                            if lev:
                                o_ap = o_ap.rearrange("p (n s h) -> p n s h", s=2, h=h)
                            last = nc.tensor.matmul(o_ap, k_pair[:, hh, a:a + m], q_ap, start=True, stop=True)
                    last.then_inc(filled[b], 1)
                if vg_tile is not None:
                    project(l, g, "vg", "N", vg_tile)
            for half in range(2):
                pe.wait_ge(seg_ready, SEG[l, g, LEVELS, half])

            def k_transposes(t):
                key = ("knat", l, g, t)
                wait_free(pe, key)
                for d, slot in enumerate((KF_, KB_)):
                    last = nc.tensor.transpose(psum[0:rows(t), bank(key), d * P:(d + 1) * P],
                                               qk[:, slot, cols(t)], ident[:])
                last.then_inc(filled[bank(key)], 1)

            order = [MT, *range(REAL)]
            k_transposes(order[0])
            for i, t in enumerate(order):
                if i + 1 < TILES:
                    k_transposes(order[i + 1])
                key = ("u", l, g, t)
                wait_free(pe, key)
                wait_read(pe, ("knat", l, g, t))
                wait_read(pe, ("unit", l, g, "vg", t))
                for d in range(2):
                    last = nc.tensor.matmul(psum[:, bank(key), d * P:(d + 1) * P], k_nat[0:rows(t), i % 2, d, :],
                                            v_c[0:rows(t), t, :], start=True, stop=True)
                last.then_inc(filled[bank(key)], 1)
            pe.wait_ge(state_ready, C_PAIR[l, g])
            pe.wait_ge(scores_c_ready, C_PAIR[l, g])
            for t in range(q_tiles(l)):
                key = ("o", l, g, t)
                b, m = bank(key), rows(t)
                wait_free(pe, key)
                first = True
                for d, slot in enumerate((QF_, QB_)):
                    if t == (MT, REAL - 1)[d]:
                        continue
                    nc.tensor.matmul(psum[0:m, b, 0:P], qk[:, slot, cols(t)], state[:, d, t, :],
                                     start=first, stop=False)
                    first = False
                for hh in range(2):
                    s_ap = pc_meta[:, hh, :] if t == MT else pc[:, t, hh, :]
                    last = nc.tensor.matmul(psum[0:m, b, hh * HD:(hh + 1) * HD], s_ap,
                                            v_c[0:m, t, hh * HD:(hh + 1) * HD], start=False, stop=hh == 1)
                last.then_inc(filled[b], 1)

        def stacked(out_ap, q_ap, kh_ap, kl_ap):
            nc.tensor.matmul(out_ap, q_ap, kh_ap, start=True, stop=False)
            return nc.tensor.matmul(out_ap, q_ap, kl_ap, start=False, stop=True)

        def transposes_of(l, g, x, t):
            key, n, src = HEAD_T[x](l, g, t)
            pe.wait_ge(roped, ROPE[l, g, x, t])
            wait_free(pe, key)
            for j in range(n):
                last = nc.tensor.transpose(psum[:, bank(key), j * P:(j + 1) * P],
                                           src[:, t % 2, j].rearrange("p d c -> p (d c)"), ident[:])
            last.then_inc(filled[bank(key)], 1)

        HEAD_T = {"q": lambda l, g, t: (("qT", l, g, t), 4, twice_a),
                  "kv": lambda l, g, t: (("kT", l, g, t), 2, twice_a),
                  "qk": lambda l, g, t: (("qkT", l, g, t), 4, twice_b)}

        def mix_a(l):
            g = "A"
            for name, x in (("qT", "q"), ("kT", "kv")):
                for t in units(l, g, x)[-2:]:
                    wait_read(pe, (name, l, g, t))
            wait_read(pe, ("unit", l, g, "kv", TILES - 1))

            def scores(t, h):
                if t >= q_tiles(l):
                    return
                f, n = window(t)
                m = rows(t)
                key = ("s", l, g, t, h)
                b = bank(key)
                wait_free(pe, key)
                q_ap = qkT_a[:, h, cols(t)]
                stacked(psum[0:m, b, 0:n * P], q_ap, qkT_a[:, 4 + h // 2, f * P:(f + n) * P],
                        klT_a[:, h // 2, f * P:(f + n) * P])
                last = stacked(psum[0:m, b, n * P:n * P + META], q_ap, qkT_a[:, 4 + h // 2, cols(MT)],
                               klT_a[:, h // 2, cols(MT)])
                last.then_inc(filled[b], 1)

            def attend(t):
                f, n = window(t)
                m = rows(t)
                o_key = ("o", l, g, t)

                def p_transposes(h):
                    key = ("pT", l, g, t, h)
                    b = bank(key)
                    pe.wait_ge(a_exp, A_HEAD[l, t, h])
                    wait_free(pe, key)
                    for j in range(n):
                        nc.tensor.transpose(psum[:, b, j * P:j * P + m], s_a[0:m, t % 2, h, j * P:(j + 1) * P],
                                            ident[0:m, 0:m])
                    last = nc.tensor.transpose(psum[0:META, b, n * P:n * P + m],
                                               s_a[0:m, t % 2, h, n * P:n * P + META], ident[0:m, 0:m])
                    last.then_inc(filled[b], 1)

                p_transposes(0)
                project(l, g, "g", "N", t)
                for h in range(4):
                    if h < 3:
                        p_transposes(h + 1)
                    scores(t + 1, h)
                    wait_read(pe, ("pT", l, g, t, h))
                    if h == 0:
                        wait_free(pe, o_key)
                    for j in range(n + 1):
                        kr = P if j < n else META
                        last = nc.tensor.matmul(psum[0:m, bank(o_key), h * P:(h + 1) * P],
                                                pT_a[0:kr, h % 2, j, 0:m], v_a[0:kr, f + j if j < n else MT, :],
                                                start=j == 0, stop=j == n)
                    last.then_inc(a_pv if h < 3 else filled[bank(o_key)], 1)

            for h in range(4):
                scores(0, h)
            for t in range(q_tiles(l)):
                attend(t)

        def pass_b(l, g, nx):
            def scores(step, c):
                if step is None:
                    return
                g, t = step
                sl = slot_of(g)
                if t == 0:
                    wait_read(pe, ("qkT", l, g, TILES - 1))
                m = rows(t)
                key = ("s", l, g, t, c)
                b = bank(key)
                wait_free(pe, key)
                for i, (a, n) in enumerate(S_PIECES):
                    last = stacked(psum[0:m, b + i, 0:n], qkT_b[:, sl, c, cols(t)], qkT_b[:, sl, 2 + c, a:a + n],
                                   klT_b[:, sl, c, a:a + n])
                last.then_inc(filled[b], 1)

            def transposes(t, j):
                m = rows(t)
                key = ("aT", l, g, t, j)
                b = bank(key)
                wait_free(pe, key)
                for i in range(3):
                    k = 3 * j + i
                    last = nc.tensor.transpose(psum[:, b, i * P:i * P + m], p0_b[0:m, B_STEP[l, g, t] % 2, k * P:(k + 1) * P],
                                               ident[0:m, 0:m])
                last.then_inc(filled[b], 1)

            def values(t):
                m = rows(t)
                key = ("o", l, g, t)
                if t == 0:
                    wait_read(pe, ("unit", l, g, "vg", TILES - 1))
                wait_free(pe, key)
                for k in range(TILES):
                    if k % 3 == 0:
                        wait_read(pe, ("aT", l, g, t, k // 3))
                    last = nc.tensor.matmul(psum[0:m, 0, 0:P], aT_b[:, k, 0:m], v_b[:, slot_of(g), k, :],
                                            start=k == 0, stop=k == TILES - 1)
                last.then_inc(filled[0], 1)

            if g == "B0":
                for x in (TILES - 2, TILES - 1):
                    wait_read(pe, ("unit", l, g, "vg", x))
                pe.wait_ge(b_pad, l + 1)
                scores((g, 0), 0)
                scores((g, 0), 1)
                scores((g, 1), 0)
            for t, made, before in b_steps(l, g, nx):
                if t is not None:
                    scores(b_step(l, g, t, 1), 1)
                for j in range(2):
                    if t is not None:
                        if j == 0:
                            pe.wait_ge(b_comb, B_STEP[l, g, t])
                        transposes(t, j)
                    if j < len(made):
                        half_unit(l, nx, *made[j], 0)
                    if heads_of(before, j) is not None:
                        transposes_of(l, nx, "qk", heads_of(before, j))
                    if j < len(made):
                        half_unit(l, nx, *made[j], 1)
                if t is not None:
                    transposes(t, 2)
                    if not nx and t >= Y_LAG:
                        transpose_y(l, t - Y_LAG)
                    scores(b_step(l, g, t, 2), 0)
                    values(t)

        pe.wait_ge(ident_in, 16)
        for t in range(TILES):
            pe.wait_ge(h_ready, NORM["I", t])
            transpose_rows("h", 0, t, hbuf[:, t])
        for l in range(DEPTH):
            for j in range(2):
                wait_read(pe, ("h", l, TILES - 1, j))
            for g in ("C0", "C1", "A"):
                for name, kind, _ in chunks_of(g):
                    if (g[0], name) not in (("C", "vg"), ("A", "g")):
                        project(l, g, name, kind)
                if g[0] == "C":
                    mix_c(l, g)
                else:
                    mix_a(l)
            for g, nx in b_passes(l):
                pass_b(l, g, nx)
            for t in range(q_tiles(l) - Y_LAG, q_tiles(l)):
                transpose_y(l, t)
            for name, kind, _ in chunks_of("O"):
                project(l, "O", name, kind)

    @block.scalar
    def _(act):
        n_sca = [0]

        def then(ins):
            n_sca[0] += 1
            ins.then_inc(sca, 1)
            act.wait_ge(sca, n_sca[0])

        def hi_of_rows(what, l, t):
            for j in range(2):
                key = (what, l, t, j)
                wait_filled(act, key)
                nc.scalar.copy(h_rows(hT_hi, j, t),
                               psum[:, bank(key), :].rearrange("p (k c) -> p k c", k=4)[:, :, 0:rows(t)]).then_inc(hi_split, 1)

        def rstd_of(l, t):
            m = rows(t)
            act.wait_ge(var_ready, NORM[l, t])
            then(nc.scalar.activation(rstd[0:m, t, 0:1], mean_var[0:m, t, 1:2], ACT.Ln, bias=eps_ln[0:m]))
            then(nc.scalar.activation(rstd[0:m, t, 0:1], rstd[0:m, t, 0:1], ACT.Exp, scale=-0.5))
            then(nc.scalar.activation(rstd[0:m, t, 1:2], mean_var[0:m, t, 0:1], ACT.Copy, scale=rstd[0:m, t, 0:1]))
            then(nc.scalar.activation(rstd[0:m, t, 1:2], rstd[0:m, t, 1:2], ACT.Copy, scale=-1.0))
            nc.scalar.activation(hbuf[0:m, t, :], hbuf[0:m, t, :], ACT.Identity, scale=rstd[0:m, t, 0:1],
                                 bias=rstd[0:m, t, 1:2]).then_inc(rstd_ready, 1)

        nc.scalar.preload_act_table_set("natural_log_exp_and_others")
        for t in range(TILES + I_LAG):
            if t < TILES:
                rstd_of("I", t)
            if t >= I_LAG:
                hi_of_rows("h", 0, t - I_LAG)
        act.wait_ge(setup_v, 1)
        then(nc.scalar.activation(lam_exp[:], lam_dot[:], ACT.Exp))
        nc.scalar.activation(lbl[:], lbl[:], ACT.Exp).then_inc(setup_s, 1)

        def evac_c(l, g):
            for name in ("qf", "b"):
                for f, j in units(l, g, name):
                    key = ("unit", l, g, name, (f, j))
                    wait_filled(act, key)
                    b = bank(key)
                    a, n = T_PIECES[j]
                    src = psum[:, b, 0:n]
                    if name == "qf" and f == 0:
                        nc.scalar.copy(q_c[:, a:a + n], src)
                        slot = QB_
                    else:
                        slot = KF_ if name == "qf" else KB_
                    nc.scalar.activation(qk[:, slot, a:a + n], src, ACT.Exp, scale=-1.0).then_inc(released[b], 1)

        def mix_c(l, g):
            for i, (lev, half, vg_tile) in enumerate(level_steps()):
                act.wait_ge(seg_ready, SEG[l, g, lev, half])
                if lev:
                    wait_filled(act, ("level", l, g, lev - 1, level_fills(half, lev - 1)[-1][0]))
                a, e = span(half, HALF[lev])
                for hh in range(2):
                    p0 = hh * HD
                    src = k_sum()[p0:p0 + HD, a:e] if lev == 0 else level_ap(lev, "k", p0, HD, a, e - a)
                    dst = k_pair[p0:p0 + HD, hh, a:e]
                    if lev:
                        dst = dst.rearrange("p (n s h) -> p n s h", s=2, h=HALF[lev])
                    ins = nc.scalar.copy(dst, src)
                ins.then_inc(level_selected, 1)
                x = level_steps()[i - 1][2] if i else None
                if x is not None:
                    key = ("unit", l, g, "vg", x)
                    wait_filled(act, key)
                    nc.scalar.copy(v_c[:, x, :], psum[:, bank(key), 0:P])
                    nc.scalar.copy(g_c[:, x, :], psum[:, bank(key), P:2 * P])
                    nc.scalar.activation(ge_c[:, x, :], psum[:, bank(key), P:2 * P], ACT.Exp, scale=-1.0)\
                        .then_inc(released[bank(key)], 1)
            for i, t in enumerate([MT, *range(REAL)]):
                key = ("knat", l, g, t)
                wait_filled(act, key)
                if i >= 2:
                    wait_filled(act, ("u", l, g, [MT, *range(REAL)][i - 2]))
                m = rows(t)
                nc.scalar.copy(k_nat[0:m, i % 2], psum[0:m, bank(key), 0:2 * P].rearrange("p (d c) -> p d c", d=2))\
                    .then_inc(released[bank(key)], 1)
            for t in range(q_tiles(l)):
                key = ("o", l, g, t)
                wait_filled(act, key)
                m = rows(t)
                for hh in range(2):
                    then(nc.scalar.activation(k_nat[0:m, 0, 0, hh * HD:(hh + 1) * HD],
                                              psum[0:m, bank(key), hh * HD:(hh + 1) * HD], ACT.Square,
                                              accum_out=sumsq[0:m, t, hh:hh + 1]))
                then(nc.scalar.activation(rstd[0:m, t, :], sumsq[0:m, t, :], ACT.Ln, bias=eps_rms[0:m], scale=1.0 / HD))
                nc.scalar.activation(rstd[0:m, t, :], rstd[0:m, t, :], ACT.Exp, scale=-0.5).then_inc(rstd_ready, 1)

        def evac_n(l, g, name, x, copies, exps):
            key = ("unit", l, g, name, x)
            wait_filled(act, key)
            b = bank(key)
            for dst, a, n in copies:
                ins = nc.scalar.copy(dst, psum[:, b, a:a + n])
            if exps:
                dst, a, n = exps
                ins = nc.scalar.activation(dst, psum[:, b, a:a + n], ACT.Exp, scale=-1.0)
            ins.then_inc(released[b], 1)

        def qk_hi_of(key, dst, n, m):
            wait_filled(act, key)
            nc.scalar.copy(dst, psum[:, bank(key), 0:n * P].rearrange("p (s c) -> p s c", s=n)[:, :, 0:m])\
                .then_inc(qk_hi, 1)

        def evac_heads(l, g, x, key_of, nat, dst, n, more):
            us = units(l, g, x)
            for t in [*us, None]:
                if t is not None:
                    if ROPE[l, g, x, t] > 2:
                        act.wait_ge(roped, ROPE[l, g, x, t] - 2)
                    evac_n(l, g, x, t, [(nat[:, t % 2, 0:n * HD], 0, n * HD)] + more(t), None)
                if t != 0:
                    u = us[-1] if t is None else t - 1
                    qk_hi_of((key_of, l, g, u), dst[:, :, cols(u)], n, rows(u))

        def group_a(l):
            g = "A"
            evac_heads(l, g, "q", "qT", n_a, qkT_a[:, 0:4], 4, lambda t: [])
            evac_heads(l, g, "kv", "kT", n_a, qkT_a[:, 4:6], 2, lambda t: [(v_a[:, t, :], P, P)])

            def exps(t, h):
                if t >= q_tiles(l):
                    return
                m, i = rows(t), t % 2
                w = window(t)[1] * P + META
                act.wait_ge(a_masked, A_HEAD[l, t, h])
                nc.scalar.activation(s_a[0:m, i, h, 0:w], s_a[0:m, i, h, 0:w], ACT.Exp, scale=SCALE,
                                     bias=neg_max[0:m, i, h:h + 1], accum_out=row_sum[0:m, i, h:h + 1])\
                    .then_inc(a_exp, 1)
                nc.scalar.activation(sink_exp[0:m, i, h:h + 1], sink_sb[0:m, l, h:h + 1], ACT.Exp,
                                     bias=neg_max[0:m, i, h:h + 1]).then_inc(a_sinks, 1)

            def evac_probs(t, h):
                key = ("pT", l, g, t, h)
                m, n = rows(t), window(t)[1]
                wait_filled(act, key)
                if h >= 2:
                    act.wait_ge(a_pv, A_PV[l, t, h - 2])
                elif t and h == 0:
                    act.wait_ge(a_pv, A_PV[l, t - 1, 2])
                elif t:
                    wait_filled(act, ("o", l, g, t - 1))
                src = psum[:, bank(key), :].rearrange("p (k c) -> p k c", k=4)
                nc.scalar.copy(pT_a[:, h % 2, 0:n, 0:m], src[:, 0:n, 0:m])
                nc.scalar.copy(pT_a[0:META, h % 2, n, 0:m], src[0:META, n, 0:m]).then_inc(released[bank(key)], 1)

            for h in range(3):
                exps(0, h)
            for t in range(q_tiles(l)):
                for h in range(4):
                    evac_probs(t, h)
                    if h == 0:
                        act.wait_ge(gate_ready, GATE[l, g, t] - (2 if t >= 2 else 1))
                        evac_n(l, g, "g", t, [(g_a[:, t % 2, :], 0, 256)], (ge_a[:, t % 2, :], 0, 256))
                    exps(*((t, 3) if h == 0 else (t + 1, h - 1)))

        def pass_b(l, g, nx):
            def evac_unit(made, j):
                if j >= len(made):
                    return
                name, x = made[j]
                if name == "qk":
                    act.wait_ge(roped, ROPE[l, nx, "qk", x] - (2 if x else 1))
                    evac_n(l, nx, name, x, [(n_b[:, x % 2, :], 0, 256)], None)
                else:
                    act.wait_ge(gate_ready, GATE[l, nx, x] - (2 if x else 1))
                    evac_n(l, nx, name, x, [(v_b[:, slot_of(nx), x, :], 0, P), (g_b[:, slot_of(nx), x, :], P, P)],
                           (ge_b[:, x % 2, :], P, P))

            def evac_transposed(before, j):
                x = heads_of(before, j)
                if x is not None:
                    qk_hi_of(("qkT", l, nx, x), qkT_b[:, slot_of(nx), :, cols(x)], 4, rows(x))

            def exps(step, c):
                if step is None:
                    return
                g, t = step
                m, i = rows(t), B_STEP[l, g, t] % 2
                act.wait_ge(b_max, B_COMP[l, g, t, c])
                b = bank(("s", l, g, t, c))
                probs = p0_b[0:m, i] if c == 0 else p1_b[0:m]
                nc.scalar.activation(probs[:, 0:2 * S_W].rearrange("p (i n) -> p i n", i=2),
                                     psum[0:m, b:b + 2, 0:S_W], ACT.Exp, scale=SCALE,
                                     bias=neg_max[0:m, i, c:c + 1],
                                     accum_out=row_sum[0:m, i, 2 * c:2 * c + 1])
                nc.scalar.activation(probs[:, 2 * S_W:TOK], psum[0:m, b + 2, 0:TOK - 2 * S_W],
                                     ACT.Exp, scale=SCALE, bias=neg_max[0:m, i, c:c + 1],
                                     accum_out=row_sum[0:m, i, 2 * c + 1:2 * c + 2])\
                    .then_inc(released[b], 1)

            def evac_probs(t, j):
                key = ("aT", l, g, t, j)
                b, m = bank(key), rows(t)
                wait_filled(act, key)
                if b_step(l, g, t, -1) and j == 0:
                    wait_filled(act, ("o", l, *b_step(l, g, t, -1)))
                nc.scalar.copy(aT_b[:, 3 * j:3 * j + 3, 0:m],
                               psum[:, b, 0:3 * P].rearrange("p (k c) -> p k c", k=3)[:, :, 0:m])\
                    .then_inc(released[b], 1)

            def norm(t):
                key = ("o", l, g, t)
                m, i = rows(t), B_STEP[l, g, t] % 2
                wait_filled(act, key)
                if B_STEP[l, g, t] > 2:
                    act.wait_ge(b_y, B_STEP[l, g, t] - 2)
                nc.scalar.copy(o_b[0:m, i, :], psum[0:m, 0, 0:P]).then_inc(released[0], 1)
                wait_read(act, key)
                then(nc.scalar.activation(b_junk[0:m, :], o_b[0:m, i, :], ACT.Square,
                                          accum_out=sumsq[0:m, t, 0:1]))
                then(nc.scalar.activation(rstd[0:m, t, 0:1], sumsq[0:m, t, 0:1], ACT.Ln, bias=eps_rms[0:m],
                                          scale=fscale[0:m, i, :]))
                nc.scalar.activation(rstd[0:m, t, 0:1], rstd[0:m, t, 0:1], ACT.Exp, scale=-0.5).then_inc(rstd_ready, 1)

            if g == "B0":
                exps((g, 0), 0)
                exps((g, 0), 1)
                exps((g, 1), 0)
            for t, made, before in b_steps(l, g, nx):
                if t is not None:
                    evac_probs(t, 0)
                    exps(b_step(l, g, t, 1), 1)
                evac_transposed(before, 0)
                evac_unit(made, 0)
                if t is not None:
                    evac_probs(t, 1)
                evac_transposed(before, 1)
                evac_unit(made, 1)
                if t is not None:
                    evac_probs(t, 2)
                    if not nx and t >= Y_LAG:
                        hi_of_rows("y", l, t - Y_LAG)
                    exps(b_step(l, g, t, 2), 0)
                    norm(t)

        for l in range(DEPTH):
            for g in ("C0", "C1", "A"):
                phase_start(act, (l, g))
                if g == "C0":
                    act.wait_ge(h_saved, 16 * TILES * (l + 1))
                if g[0] == "C":
                    evac_c(l, g)
                    mix_c(l, g)
                else:
                    group_a(l)
            phase_start(act, (l, "B0"))
            for g, nx in b_passes(l):
                pass_b(l, g, nx)
            for t in range(q_tiles(l) - Y_LAG, q_tiles(l)):
                hi_of_rows("y", l, t)
            for t in range(q_tiles(l)):
                rstd_of(l, t)
                if t >= H_LAG and l < DEPTH - 1:
                    hi_of_rows("h", l + 1, t - H_LAG)
            if l < DEPTH - 1:
                for t in range(TILES - H_LAG, TILES):
                    hi_of_rows("h", l + 1, t)

    @block.vector
    def _(dve):
        n_vec = [0]

        def then(ins):
            n_vec[0] += 1
            ins.then_inc(vec, 1)
            dve.wait_ge(vec, n_vec[0])

        tt, ts, stt = nc.vector.tensor_tensor, nc.vector.tensor_scalar, nc.vector.scalar_tensor_tensor

        def release(key):
            dve.sem_inc(released[bank(key)], 1)

        def lo_of_rows(what, l, t):
            for j in range(2):
                key = (what, l, t, j)
                dve.wait_ge(hi_split, T_SPLIT[key])
                tt(h_rows(hT_lo, j, t),
                   psum[:, bank(key), :].rearrange("p (k c) -> p k c", k=4)[:, :, 0:rows(t)],
                   h_rows(hT_hi, j, t).bitcast(F32), ALU.subtract).then_inc(released[bank(key)], 1)

        def ln_stats(l, t):
            m = rows(t)
            for i in range(2):
                then(nc.vector.bn_stats(stats[0:m, t, i, :], hbuf[0:m, t, i * 512:(i + 1) * 512]))
            nc.vector.bn_aggr(mean_var[0:m, t, :], stats[0:m, t, :, :].rearrange("p a b -> p (a b)")).then_inc(var_ready, 1)

        def ln_apply(l, t):
            m = rows(t)
            dve.wait_ge(rstd_ready, RSTD[l, t])
            row = hbuf[0:m, t, :]
            tt(row, row, ln_w[0:m, 0, :], ALU.mult).then_inc(scaled, 1)

        for h in (hT_hi, hT_lo):
            nc.vector.memset(h[:, KT * TOK:].bitcast(F32), 0.0)
        nc.vector.memset(eps_ln[:], LN_EPS)
        nc.vector.memset(eps_rms[:], RMS_EPS)
        dve.wait_ge(rows_in[0], 16)
        ln_stats("I", 0)
        dve.wait_ge(ln_in, 32)
        for t in range(TILES + I_LAG):
            if t + 1 < TILES:
                dve.wait_ge(rows_in[t + 1], 16)
                ln_stats("I", t + 1)
            if t < TILES:
                ln_apply("I", t)
            if t >= I_LAG:
                lo_of_rows("h", 0, t - I_LAG)
        dve.wait_ge(consts_in, 16 * N_CONSTS)
        for l in range(DEPTH):
            for i in range(2):
                then(nc.vector.tensor_tensor_reduce(lam_tmp[:], lam_sb[:, l, 2 * i, :], lam_sb[:, l, 2 * i + 1, :],
                                                    1.0, 0.0, ALU.mult, ALU.add, lam_dot[:, l, i:i + 1]))
        then(tt(lb_max[:], lbl[:, 0], lbl[:, 1], ALU.max))
        for l in range(DEPTH):
            then(tt(lbl[:, l], lbl[:, l], lb_max[:], ALU.subtract))
        dve.sem_inc(setup_v, 1)
        dve.wait_ge(setup_s, 1)
        for l in range(DEPTH):
            then(stt(neg_lam[:, l:l + 1], lam_exp[:, l, 1:2], -LAM_INIT[l], lam_exp[:, l, 0:1], ALU.add, ALU.subtract))
        then(tt(lb_sum[:], lbl[:, 0], lbl[:, 1], ALU.add))
        then(nc.vector.reciprocal(lb_sum[:], lb_sum[:]))
        for l in range(DEPTH):
            then(tt(lbl[:, l], lbl[:, l], lb_sum[:], ALU.mult))
        then(tt(lb[:, 1], lbl[:, 0], lbl[:, 1], ALU.add))
        then(tt(lb[:, 1], lb[:, 1], lbl[:, 0], ALU.subtract))
        then(tt(lb[:, 0], lbl[:, 0], lbl[:, 0], ALU.subtract))
        then(ts(one_lb[:], lb[:], -1.0, 1.0, ALU.mult, ALU.add))

        def y_slot(l, g, t):
            n = Y_OUT[l, g, t]
            s = n % Y_SLOTS
            before = (n - 1) // Y_SLOTS if s else n // Y_SLOTS - 1
            if before > 0:
                dve.wait_ge(y_saved[s], 16 * before)
            return s

        def group_c(l, g):
            p = int(g[1])
            oml, lbp = one_lb[:, l, p:p + 1], lb[:, l, p:p + 1]
            then(nc.vector.memset(k_pair[HD:P, 0, :], 0.0))
            then(nc.vector.memset(k_pair[0:HD, 1, :], 0.0))
            for name in ("qf", "b"):
                for fb, j in units(l, g, name):
                    wait_read(dve, ("unit", l, g, name, (fb, j)))
                    a, n = T_PIECES[j]
                    if name == "qf" and fb == 0:
                        qe = qk[:, QB_, a:a + n]
                        then(ts(qe, qe, 1.0, None, ALU.add))
                        then(nc.vector.reciprocal(qe, qe))
                        then(tt(q_c[:, a:a + n], q_c[:, a:a + n], qe, ALU.mult))
                        continue
                    d, slot = (0, KF_) if name == "qf" else (1, KB_)
                    k, f = qk[:, slot, a:a + n], seg[:, d, a:a + n]
                    then(ts(k, k, E_MAX, None, ALU.min))
                    then(ts(f, k, 1.0, None, ALU.add))
                    then(nc.vector.reciprocal(f, f))
                    then(stt(k, k, oml, f, ALU.mult, ALU.mult))
                    then(ts(f, f, oml, lbp, ALU.mult, ALU.add))
                    then(ts(f, f, F_MIN, None, ALU.max))
            if g == "C0":
                dve.wait_ge(norm_w_in, 32 * (l + 1))
            w = norm_w[:, 512 + p * P:512 + (p + 1) * P]
            then(tt(k_sum(), qk[:, KF_, :], qk[:, KB_, :], ALU.add))
            dve.sem_inc(seg_ready, 2)
            then(tt(qk[:, QF_, :], q_c[:], seg[:, 0, 0:TOK], ALU.mult))
            then(tt(qk[:, QB_, :], q_c[:], seg[:, 1, 0:TOK], ALU.mult))
            dve.sem_inc(seg_ready, 2)
            for i, (lev, half, _) in enumerate(level_steps()):
                fills = level_fills(half, lev)
                if lev:
                    wait_filled(dve, ("level", l, g, lev, fills[-1][0]))
                    extend_segments(lev, half)
                    dve.sem_inc(seg_ready, 1)
                for first, n in fills:
                    key = ("level", l, g, lev, first)
                    wait_filled(dve, key)
                    m = rows(first)
                    if first == MT:
                        then(nc.vector.copy_predicated(
                            pc_meta[:], view(pair_sb, 0, META, lev * P, [[0, 2], [1, META]]).bitcast(I32),
                            psum[0:m, bank(key), 0:2 * m].rearrange("p (h t) -> p h t", h=2)))
                    else:
                        then(nc.vector.copy_predicated(
                            pc[:, first:first + n].rearrange("p n h t -> p (n h) t"),
                            view(pair_sb, 0, P, lev * P, [[0, 2 * n], [1, P]]).bitcast(I32),
                            psum[:, bank(key), 0:2 * n * P].rearrange("p (h t) -> p h t", t=P)))
                    release(key)
                if lev == 0 and half:
                    then(nc.vector.memset(state[:].rearrange("p d t c -> p (d t c)"), 0.0))
            dve.sem_inc(scores_c_ready, 1)
            uu = k_pair[:].rearrange("p h t -> p (h t)")[:, 0:TILES * P].rearrange("p (t d c) -> p t d c", d=2, c=HD)
            for t in [MT, *range(REAL)]:
                key = ("u", l, g, t)
                wait_filled(dve, key)
                src = psum[:, bank(key), 0:2 * P].rearrange("p (d c) -> p d c", d=2)
                for p0 in (0, HD):
                    then(nc.vector.tensor_copy(uu[p0:p0 + HD, t], src[p0:p0 + HD, :, p0:p0 + HD]))
                release(key)
            fwd = [MT, *range(REAL)]
            bwd = [*range(REAL - 1, -1, -1), MT]
            for i in range(TILES - 1):
                for d, order in ((0, fwd), (1, bwd)):
                    a, b_ = order[i], order[i + 1]
                    for p0 in (0, HD):
                        ps = slice(p0, p0 + HD)
                        if i == 0:
                            ins = nc.vector.tensor_copy(state[ps, d, b_, ps], uu[ps, a, d, :])
                        else:
                            tot = seg[ps, d, SEG_AT[7] + a:SEG_AT[7] + a + 1]
                            ins = stt(state[ps, d, b_, ps], state[ps, d, a, ps], tot, uu[ps, a, d, :],
                                      ALU.mult, ALU.add)
                        if d and p0:
                            then(ins)
            dve.sem_inc(state_ready, 1)

            def gate_c(t):
                wait_read(dve, ("unit", l, g, "vg", t))
                gate(l, g, t, g_c[:, t, :], ge_c[:, t, :], w)

            gate_c(0)
            for t in range(q_tiles(l)):
                if t + 1 < q_tiles(l):
                    gate_c(t + 1)
                dve.wait_ge(gate_ready, GATE[l, g, t])
                key = ("o", l, g, t)
                m = rows(t)
                dve.wait_ge(rstd_ready, RSTD[l, g, t])
                s = y_slot(l, g, t)
                for hh in range(2):
                    hs = slice(hh * HD, (hh + 1) * HD)
                    ins = stt(y_stage[0:m, s, hs], psum[0:m, bank(key), hs], rstd[0:m, t, hh:hh + 1],
                              g_c[0:m, t, hs], ALU.mult, ALU.mult)
                ins.then_inc(released[bank(key)], 1)

        def extend_segments(lev, half):
            h = HALF[lev]
            a, e = span(half, h)
            n = (e - a) // (2 * h)
            at = SEG_AT[lev - 1] + a // h
            tot = [view(seg, 0, P, at + side, [[SEG_ALL, 2], [2, n], [0, h]]) for side in (0, 1)]
            left = view(qk, 0, P, KF_ * TOK + a, [[(QB_ - KF_) * TOK, 2], [2 * h, n], [1, h]])
            right = view(qk, 0, P, QF_ * TOK + a + h, [[(KB_ - QF_) * TOK, 2], [2 * h, n], [1, h]])
            tt(left, left, tot[1], ALU.mult)
            tt(right, right, tot[0], ALU.mult)
            then(tt(view(seg, 0, P, SEG_AT[lev] + a // (2 * h), [[SEG_ALL, 2], [1, n]]),
                    view(seg, 0, P, at, [[SEG_ALL, 2], [2, n]]),
                    view(seg, 0, P, at + 1, [[SEG_ALL, 2], [2, n]]), ALU.mult))

        def rope(l, g, x, t, nat, dup, n, tmp):
            wait_read(dve, ("unit", l, g, x, t))
            if ROPE[l, g, x, t] > 1:
                dve.wait_ge(roped, ROPE[l, g, x, t] - 1)
            base = (t % 2) * 256
            cs = view(cos_sb, 0, P, t * HD, [[0, n], [1, HD]])
            tt(view(tmp, 0, P, 0, [[HD, n], [1, HD]]), view(nat, 0, P, base, [[HD, n], [1, HD]]), cs, ALU.mult)
            for dst, src in ((0, HD // 2), (HD // 2, 0)):
                ins = tt(view(tmp, 0, P, 256 + dst, [[HD, n], [1, HD // 2]]),
                         view(nat, 0, P, base + src, [[HD, n], [1, HD // 2]]),
                         view(sin_sb, 0, P, t * HD + dst, [[0, n], [1, HD // 2]]), ALU.mult)
            then(ins)
            if t >= 2:
                wait_filled(dve, ({"q": "qT", "kv": "kT", "qk": "qkT"}[x], l, g, t - 2))
            elif x == "kv":
                wait_filled(dve, ("qT", l, g, units(l, g, "q")[-1]))
            tt(dup[:, t % 2, 0:n], view(tmp, 0, P, 0, [[HD, n], [0, 2], [1, HD]]),
               view(tmp, 0, P, 256, [[HD, n], [0, 2], [1, HD]]), ALU.add).then_inc(roped, 1)

        def heads(l, g, x, key_of, nat, dup, n, tmp, *parts):
            for t in [*units(l, g, x), None]:
                if t is not None:
                    rope(l, g, x, t, nat, dup, n, tmp)
                if t != 0:
                    u = units(l, g, x)[-1] if t is None else t - 1
                    qk_lo_of(l, g, x, u, (key_of, l, g, u), *parts)

        def qk_lo_of(l, g, x, t, key, qkT, klT, nq, k0, nk):
            dve.wait_ge(qk_hi, QK_HI[l, g, x, t])
            m = rows(t)
            src = psum[:, bank(key), :].rearrange("p (s c) -> p s c", s=4)
            if nq:
                dst = qkT[HD:P, 0:nq, cols(t)]
                ins = tt(dst, src[HD:P, 0:nq, 0:m], dst.bitcast(F32), ALU.subtract)
            if nk:
                ins = tt(klT[:, 0:nk, cols(t)], src[:, nq:nq + nk, 0:m], qkT[:, k0:k0 + nk, cols(t)].bitcast(F32),
                         ALU.subtract)
            ins.then_inc(released[bank(key)], 1)

        def gate(l, g, t, gn, ge, w):
            then(ts(ge, ge, 1.0, None, ALU.add))
            then(nc.vector.reciprocal(ge, ge))
            ins = tt(gn, gn, ge, ALU.mult)
            if w is not None:
                then(ins)
                ins = tt(gn, gn, w, ALU.mult)
            ins.then_inc(gate_ready, 1)

        def group_a(l):
            g = "A"
            heads(l, g, "q", "qT", n_a, twice_a, 4, ra, qkT_a, None, 4, 0, 0)
            heads(l, g, "kv", "kT", n_a, twice_a, 2, ra, qkT_a, klT_a, 0, 4, 2)

            def mask(t, h):
                if t >= q_tiles(l):
                    return
                m, i = rows(t), t % 2
                w = window(t)[1] * P + META
                key = ("s", l, g, t, h)
                wait_filled(dve, key)
                if t >= 2:
                    wait_filled(dve, ("pT", l, g, t - 2, h))
                then(nc.vector.tensor_tensor_reduce(s_a[0:m, i, h, 0:w], psum[0:m, bank(key), 0:w],
                                                    band_sb[0:m, band_columns(t)], 1.0, NEG, ALU.add, ALU.max,
                                                    row_max[0:m, i, h:h + 1]))
                release(key)
                then(ts(neg_max[0:m, i, h:h + 1], row_max[0:m, i, h:h + 1], SCALE, sink_sb[0:m, l, h:h + 1],
                        ALU.mult, ALU.max))
                ts(neg_max[0:m, i, h:h + 1], neg_max[0:m, i, h:h + 1], -1.0, None, ALU.mult).then_inc(a_masked, 1)

            for h in range(4):
                mask(0, h)
            for t in range(q_tiles(l)):
                m, i = rows(t), t % 2
                for h in range(4):
                    mask(t + 1, h)
                    if h == 1:
                        wait_read(dve, ("unit", l, g, "g", t))
                        gate(l, g, t, g_a[:, i, :], ge_a[:, i, :], None)
                dve.wait_ge(gate_ready, GATE[l, g, t])
                dve.wait_ge(a_sinks, A_HEAD[l, t, 3])
                then(tt(inv_sum[0:m, i, :], row_sum[0:m, i, :], sink_exp[0:m, i, :], ALU.add))
                then(nc.vector.reciprocal(inv_sum[0:m, i, :], inv_sum[0:m, i, :]))
                key = ("o", l, g, t)
                wait_filled(dve, key)
                s = y_slot(l, g, t)
                for h in range(4):
                    v0 = h * P + (h // 2) * HD
                    ins = stt(y_stage[0:m, s, h * HD:(h + 1) * HD], psum[0:m, bank(key), v0:v0 + HD],
                              inv_sum[0:m, i, h:h + 1], g_a[0:m, i, h * HD:(h + 1) * HD], ALU.mult, ALU.mult)
                ins.then_inc(released[bank(key)], 1)

        def pads_b():
            for j in range(2):
                nc.vector.memset(p0_b[:, j, TOK:], 0.0)
            for c in range(2):
                then(nc.vector.memset(psum[:, 4 + 3 * c, TOK - 2 * S_W:S_W], NEG))
            dve.sem_inc(b_pad, 1)

        def pass_b(l, g, nx):
            def lo_of(before, j):
                x = heads_of(before, j)
                if x is not None:
                    qk_lo_of(l, nx, "qk", x, ("qkT", l, nx, x), qkT_b[:, slot_of(nx)], klT_b[:, slot_of(nx)], 2, 2, 2)

            def finish_unit(made, j):
                if j >= len(made):
                    return
                name, x = made[j]
                if name == "qk":
                    rope(l, nx, "qk", x, n_b, twice_b, 4, rb)
                else:
                    hb = int(nx[1])
                    wait_read(dve, ("unit", l, nx, "vg", x))
                    gate(l, nx, x, g_b[:, slot_of(nx), x, :], ge_b[:, x % 2, :], norm_w[:, hb * P:(hb + 1) * P])

            def finish(step):
                g, t = step
                m, i = rows(t), B_STEP[l, g, t] % 2
                dve.wait_ge(rstd_ready, RSTD[l, g, t])
                then(stt(coef[0:m, i, 1:2], rstd[0:m, t, 0:1], 1.0 - LAM_INIT[l], inv_sum[0:m, i, 0:1],
                         ALU.mult, ALU.mult))
                s = y_slot(l, g, t)
                stt(y_stage[0:m, s, 0:P], o_b[0:m, i, :], coef[0:m, i, 1:2], g_b[0:m, slot_of(g), t, :],
                    ALU.mult, ALU.mult).then_inc(b_y, 1)

            def maximum(step, c):
                if step is None:
                    return
                g, t = step
                m, i = rows(t), B_STEP[l, g, t] % 2
                key = ("s", l, g, t, c)
                b = bank(key)
                wait_filled(dve, key)
                if b_step(l, g, t, -2) and c == 0:
                    wait_filled(dve, ("aT", l, *b_step(l, g, t, -2), 2))
                then(nc.vector.tensor_reduce(row_max[0:m, i, c:c + 1], psum[0:m, b:b + 3, 0:S_W], AX.XY, ALU.max))
                ts(neg_max[0:m, i, c:c + 1], row_max[0:m, i, c:c + 1], -SCALE, None, ALU.mult).then_inc(b_max, 1)

            def combine(step):
                if step is None:
                    return
                g, t = step
                m, i = rows(t), B_STEP[l, g, t] % 2
                for c in range(2):
                    wait_read(dve, ("s", l, g, t, c))
                then(tt(row_sum[0:m, i, 0:4:2], row_sum[0:m, i, 0:4:2], row_sum[0:m, i, 1:4:2], ALU.add))
                then(nc.vector.reciprocal(inv_sum[0:m, i, 0:2], row_sum[0:m, i, 0:4:2]))
                then(stt(coef[0:m, i, 0:1], inv_sum[0:m, i, 1:2], neg_lam[0:m, l:l + 1], row_sum[0:m, i, 0:1],
                         ALU.mult, ALU.mult))
                then(stt(fscale[0:m, i, :], inv_sum[0:m, i, 0:1], 1.0 / P, inv_sum[0:m, i, 0:1],
                         ALU.mult, ALU.mult))
                stt(p0_b[0:m, i, 0:TOK], p1_b[0:m, :], coef[0:m, i, 0:1], p0_b[0:m, i, 0:TOK],
                    ALU.mult, ALU.add).then_inc(b_comb, 1)

            if g == "B0":
                maximum((g, 0), 0)
                maximum((g, 0), 1)
                combine((g, 0))
                maximum((g, 1), 0)
            for t, made, before in b_steps(l, g, nx):
                if t is not None:
                    maximum(b_step(l, g, t, 1), 1)
                finish_unit(before, 1)
                if t is not None and b_step(l, g, t, -1):
                    finish(b_step(l, g, t, -1))
                lo_of(before, 0)
                if t is not None:
                    combine(b_step(l, g, t, 1))
                lo_of(before, 1)
                finish_unit(made, 0)
                if t is not None:
                    if not nx and t >= Y_LAG:
                        lo_of_rows("y", l, t - Y_LAG)
                    maximum(b_step(l, g, t, 2), 0)
            if g and not nx:
                finish((g, q_tiles(l) - 1))

        for l in range(DEPTH):
            for g in ("C0", "C1", "A"):
                phase_start(dve, (l, g))
                if g[0] == "C":
                    group_c(l, g)
                else:
                    group_a(l)
            phase_start(dve, (l, "B0"))
            pads_b()
            for g, nx in b_passes(l):
                pass_b(l, g, nx)
            phase_start(dve, (l, "O"))
            for t in range(q_tiles(l) - Y_LAG, q_tiles(l)):
                lo_of_rows("y", l, t)

            for c in range(DM // CW):
                for t in units(l, "O", c):
                    key = ("unit", l, "O", c, t)
                    wait_filled(dve, key)
                    if c == 0:
                        dve.wait_ge(rows_in[t], 16 * (l + 2))
                    elif c == DM // CW - 1 and t == 0:
                        dve.wait_ge(ln_in, 32 * (l + 2))
                    part = hbuf[0:rows(t), t, c * CW:(c + 1) * CW]
                    then(stt(part, part, ALPHA, psum[0:rows(t), bank(key), 0:CW], ALU.mult, ALU.add))
                    release(key)
                    if c == DM // CW - 1:
                        ln_stats(l, t)
                        if t:
                            ln_apply(l, t - 1)
                        if t >= H_LAG and l < DEPTH - 1:
                            lo_of_rows("h", l + 1, t - H_LAG)
            ln_apply(l, q_tiles(l) - 1)
            if l < DEPTH - 1:
                for t in range(TILES - H_LAG, TILES):
                    lo_of_rows("h", l + 1, t)


N_CONSTS = 4 + 2 + DEPTH * 2
_INS = ["x", "meta", "emb_ln_g", "emb_ln_b", "w_in", "w_out", "a_sink", "b_lam", "b_subln_w", "c_lb_logits",
        "c_norm_w", "ln_g", "ln_b"]


def kernel(**inputs):
    import concourse.bacc as bacc
    from concourse.bass_utils import run_bass_kernel_spmd

    nc = bacc.Bacc("TRN2", target_bir_lowering=False, num_devices=1, dynamic_dma_scratch_size=1024)
    arrays, args = {}, []
    for name, a in [(n, inputs[n]) for n in _INS] + list(CONSTS.items()):
        a = np.ascontiguousarray(a)
        arrays[f"in_{name}"] = a
        args.append(nc.dram_tensor(f"in_{name}", a.shape, mybir.dt.from_np(a.dtype), kind="ExternalInput").ap())
    args.append(nc.dram_tensor("out", (1, REAL * P, DM), F32, kind="ExternalOutput").ap())
    build(nc, *args)
    r = run_bass_kernel_spmd(nc, [arrays], core_ids=[0])
    return r.results[0]["out"]
```
